# Optimizing a Trainium2 kernel written in Bass

```python
import math
import jax, jax.numpy as jnp
from jax import lax
import numpy as np

D_MODEL = 1024
BATCH = 1
SEQ = 1024
DEPTH = 2

N_MIXERS = 2
N_HEADS = 16
HEAD_DIM = D_MODEL // N_HEADS
Q_BLOCK = 128
SSM_GROUP = 16
N_GROUPS = D_MODEL // SSM_GROUP
SSM_STATE = 64
D_FF = 4 * D_MODEL
DT_MIN = 0.001
DT_MAX = 0.1
EPS = 1e-6
N_ATTN_LAYERS = (DEPTH + 1) // 2
N_SSM_LAYERS = DEPTH // 2

kernel_name = "fox_s5_interleaved_hybrid"

def rms_norm(x, g):
    xf = x.astype(jnp.float32)
    y = xf * lax.rsqrt(jnp.mean(xf * xf, axis=-1, keepdims=True) + EPS)
    return (y * g.astype(jnp.float32)).astype(x.dtype)

def fox_attention(h, w_in, b_f, q_g, k_g, w_out):
    B, S, D = h.shape
    proj = h @ w_in
    q, k, v, f = jnp.split(proj, [D, 2 * D, 3 * D], axis=-1)
    q = rms_norm(q.reshape(B, S, N_HEADS, HEAD_DIM), q_g)
    k = rms_norm(k.reshape(B, S, N_HEADS, HEAD_DIM), k_g)
    v = v.reshape(B, S, N_HEADS, HEAD_DIM)
    log_f = jax.nn.log_sigmoid((f + b_f).astype(jnp.float32))
    c = jnp.cumsum(log_f, axis=1).transpose(0, 2, 1)
    q = q.transpose(0, 2, 1, 3)
    k = k.transpose(0, 2, 1, 3)
    v = v.transpose(0, 2, 1, 3)
    nb = S // Q_BLOCK
    qb = q.reshape(B, N_HEADS, nb, Q_BLOCK, HEAD_DIM).transpose(2, 0, 1, 3, 4)
    cb = c.reshape(B, N_HEADS, nb, Q_BLOCK).transpose(2, 0, 1, 3)
    k_pos = jnp.arange(S)
    scale = 1.0 / math.sqrt(HEAD_DIM)

    def block(args):
        q_i, c_i, i = args
        q_pos = i * Q_BLOCK + jnp.arange(Q_BLOCK)
        s = jnp.einsum('bhqd,bhkd->bhqk', q_i, k).astype(jnp.float32) * scale
        s = s + c_i[..., :, None] - c[:, :, None, :]
        s = jnp.where(k_pos[None, :] <= q_pos[:, None], s, -jnp.inf)
        p = jax.nn.softmax(s, axis=-1)
        return jnp.einsum('bhqk,bhkd->bhqd', p.astype(v.dtype), v)

    o = lax.map(block, (qb, cb, jnp.arange(nb)))
    o = o.transpose(1, 0, 3, 2, 4).reshape(B, S, D)
    return o @ w_out

def _scan_combine(e1, e2):
    a1r, a1i, b1r, b1i = e1
    a2r, a2i, b2r, b2i = e2
    ar = a1r * a2r - a1i * a2i
    ai = a1r * a2i + a1i * a2r
    br = a2r * b1r - a2i * b1i + b2r
    bi = a2r * b1i + a2i * b1r + b2i
    return (ar, ai, br, bi)

def s5_layer(h, w_in, a_re, a_im, b_re, b_im, c_re, c_im, log_dt, d_skip, w_glu):
    B, S, D = h.shape
    f32 = jnp.float32
    u = (h @ w_in).astype(f32)
    ug = u.reshape(B, S, N_GROUPS, SSM_GROUP)
    a_re = a_re.astype(f32); a_im = a_im.astype(f32)
    dt = jnp.exp(log_dt.astype(f32))[:, None]
    mag = jnp.exp(dt * a_re)
    ab_re = mag * jnp.cos(dt * a_im)
    ab_im = mag * jnp.sin(dt * a_im)
    num_re = ab_re - 1.0
    num_im = ab_im
    den = a_re * a_re + a_im * a_im
    s_re = (num_re * a_re + num_im * a_im) / den
    s_im = (num_im * a_re - num_re * a_im) / den
    b_re = b_re.astype(f32); b_im = b_im.astype(f32)
    bb_re = s_re[..., None] * b_re - s_im[..., None] * b_im
    bb_im = s_re[..., None] * b_im + s_im[..., None] * b_re
    bu_re = jnp.einsum('bsgc,gpc->bsgp', ug, bb_re)
    bu_im = jnp.einsum('bsgc,gpc->bsgp', ug, bb_im)
    ar = jnp.broadcast_to(ab_re, bu_re.shape)
    ai = jnp.broadcast_to(ab_im, bu_re.shape)
    _, _, xr, xi = lax.associative_scan(_scan_combine, (ar, ai, bu_re, bu_im), axis=1)
    y = (jnp.einsum('bsgp,gcp->bsgc', xr, c_re.astype(f32))
         - jnp.einsum('bsgp,gcp->bsgc', xi, c_im.astype(f32)))
    y = y.reshape(B, S, D) + d_skip.astype(f32) * u
    z = jax.nn.gelu(y).astype(h.dtype)
    val, gate = jnp.split(z @ w_glu, 2, axis=-1)
    return val * jax.nn.sigmoid(gate)

def sqrelu_mlp(h, w1, w2):
    return jnp.square(jax.nn.relu(h @ w1)) @ w2

def setup_inputs(seed: int = 0) -> dict:
    key = jax.random.key(seed)
    ks = jax.random.split(key, 20)
    D, H, G, P, C = D_MODEL, N_HEADS, N_GROUPS, SSM_STATE, SSM_GROUP
    nA, nS = N_ATTN_LAYERS, N_SSM_LAYERS
    nrm = jax.random.normal
    x = nrm(ks[0], (BATCH, SEQ, D), jnp.float32)
    norm_mix_g = 1.0 + 0.02 * nrm(ks[1], (DEPTH, D), jnp.float32)
    norm_mlp_g = 1.0 + 0.02 * nrm(ks[2], (DEPTH, D), jnp.float32)
    attn_w_in = nrm(ks[3], (nA, D, 3 * D + H), jnp.float32) * D ** -0.5
    attn_b_f = jax.random.uniform(ks[4], (nA, H), jnp.float32, 1.0, 6.0)
    attn_q_g = 1.0 + 0.02 * nrm(ks[5], (nA, HEAD_DIM), jnp.float32)
    attn_k_g = 1.0 + 0.02 * nrm(ks[6], (nA, HEAD_DIM), jnp.float32)
    attn_w_out = nrm(ks[7], (nA, D, D), jnp.float32) * D ** -0.5
    ssm_w_in = nrm(ks[8], (nS, D, D), jnp.float32) * D ** -0.5
    ssm_a_re = -0.5 * (1.0 + 0.02 * nrm(ks[9], (nS, G, P), jnp.float32))
    ssm_a_im = jnp.broadcast_to(jnp.pi * jnp.arange(P, dtype=jnp.float32), (nS, G, P))
    ssm_b_re = nrm(ks[10], (nS, G, P, C), jnp.float32) * (2.0 * C) ** -0.5
    ssm_b_im = nrm(ks[11], (nS, G, P, C), jnp.float32) * (2.0 * C) ** -0.5
    ssm_c_re = nrm(ks[12], (nS, G, C, P), jnp.float32) * (2.0 * P) ** -0.5
    ssm_c_im = nrm(ks[13], (nS, G, C, P), jnp.float32) * (2.0 * P) ** -0.5
    ssm_log_dt = jax.random.uniform(ks[14], (nS, G), jnp.float32,
                                    math.log(DT_MIN), math.log(DT_MAX))
    ssm_d = nrm(ks[15], (nS, D), jnp.float32)
    ssm_w_glu = nrm(ks[16], (nS, D, 2 * D), jnp.float32) * D ** -0.5
    mlp_w1 = nrm(ks[17], (DEPTH, D, D_FF), jnp.float32) * D ** -0.5
    mlp_w2 = nrm(ks[18], (DEPTH, D_FF, D), jnp.float32) * D_FF ** -0.5
    return {"x": x, "norm_mix_g": norm_mix_g, "norm_mlp_g": norm_mlp_g,
            "attn_w_in": attn_w_in, "attn_b_f": attn_b_f, "attn_q_g": attn_q_g,
            "attn_k_g": attn_k_g, "attn_w_out": attn_w_out,
            "ssm_w_in": ssm_w_in, "ssm_a_re": ssm_a_re, "ssm_a_im": ssm_a_im,
            "ssm_b_re": ssm_b_re, "ssm_b_im": ssm_b_im, "ssm_c_re": ssm_c_re,
            "ssm_c_im": ssm_c_im, "ssm_log_dt": ssm_log_dt, "ssm_d": ssm_d,
            "ssm_w_glu": ssm_w_glu, "mlp_w1": mlp_w1, "mlp_w2": mlp_w2}

def reference(x, norm_mix_g, norm_mlp_g, attn_w_in, attn_b_f, attn_q_g, attn_k_g,
              attn_w_out, ssm_w_in, ssm_a_re, ssm_a_im, ssm_b_re, ssm_b_im,
              ssm_c_re, ssm_c_im, ssm_log_dt, ssm_d, ssm_w_glu, mlp_w1, mlp_w2):
    for i in range(DEPTH):
        h = rms_norm(x, norm_mix_g[i])
        j = i // N_MIXERS
        if i % N_MIXERS == 0:
            mix = fox_attention(h, attn_w_in[j], attn_b_f[j], attn_q_g[j],
                                attn_k_g[j], attn_w_out[j])
        else:
            mix = s5_layer(h, ssm_w_in[j], ssm_a_re[j], ssm_a_im[j], ssm_b_re[j],
                           ssm_b_im[j], ssm_c_re[j], ssm_c_im[j], ssm_log_dt[j],
                           ssm_d[j], ssm_w_glu[j])
        x = x + mix
        h = rms_norm(x, norm_mlp_g[i])
        x = x + sqrelu_mlp(h, mlp_w1[i], mlp_w2[i])
    return x


_drawn_inputs = setup_inputs


def setup_inputs(seed=0):
    import zlib

    import numpy as np

    out = dict(_drawn_inputs(seed))
    spreads = {}
    factors = {'norm_mix_g': 4.603,
     'attn_q_g': 8.0,
     'attn_k_g': 8.0,
     'ssm_a_re': 64.0,
     'ssm_a_im': 27.104,
     'ssm_b_re': 35.448,
     'ssm_b_im': 38.448,
     'ssm_c_re': 37.176,
     'ssm_c_im': 39.352,
     'ssm_log_dt': 33.6,
     'norm_mlp_g': 6.731}
    for name, (base, spread) in spreads.items():
        noise = np.random.default_rng([zlib.crc32(name.encode()), seed]).standard_normal(out[name].shape)
        drawn = base * np.exp(spread * noise) if base else spread * noise
        out[name] = __import__('jax').numpy.asarray(drawn.astype(out[name].dtype))
    for name, factor in factors.items():
        out[name] = (out[name] * factor).astype(out[name].dtype)
    return out
```

```python
from contextlib import ExitStack

import concourse.bass as bass
from concourse import mybir

F32 = mybir.dt.float32
F32R = mybir.dt.float32r
I32 = mybir.dt.int32
ALU = mybir.AluOpType
ACT = mybir.ActivationFunctionType

P = 128
T = 1024
D = 1024
KT = D // P
HALF = 512
NH = 16
HD = D // NH
PAIRS = NH // 2
FF = 4096
EPS = 1e-6
PANEL = 2048
PW = PANEL // KT
NG = 64
GC = 16
NS = 64
L = 8
NC = T // L
GP = NG // 2
BLK = KT
GB = NG // BLK
PB = GP // BLK
MASKED = 1e30

N_QK, N_V = 8, 4
N_ATT = N_QK + N_V
N_OUT = D // PW
N_MLP = 2 * FF // PW
N_SIN = D // PW
N_GLU = 2 * D // PW
OUT0 = N_ATT
MLP0 = OUT0 + N_OUT
SIN0 = MLP0 + N_MLP
GLU0 = SIN0 + N_SIN
MLP1 = GLU0 + N_GLU
N_PANELS = MLP1 + N_MLP

TWO_PI = (6.28125, 0.0019354820251464844, -1.7484555314695172e-07)
LN2 = (0.693359375, -2.12194440e-4)
EXP_POLY = (1.9875691500e-4, 1.3981999507e-3, 8.3334519073e-3, 4.1665795894e-2, 1.6666665459e-1, 5.0000001201e-1)
SIN_POLY = (-1.9515295891e-4, 8.3321608736e-3, -1.6666654611e-1)
COS_POLY = (2.443315711809948e-5, -1.388731625493765e-3, 4.166664568298827e-2)
LOG2E = 1.4426950408889634
PI = 3.141592653589793
ROUND = 12582912.0


def attention_order():
    order = [("S", 0, m) for m in range(4)]
    for u in range(4):
        tiles = 4 if u % 2 == 0 else 8
        for j in range(tiles):
            order.append(("T", u, j))
            if u < 3 and (j + 1) % (tiles // 4) == 0:
                order.append(("S", u + 1, (j + 1) // (tiles // 4) - 1))
    return order


def key_tiles(u):
    return 4 if u % 2 == 0 else 8


TILES_BEFORE = [0, 4, 12, 16, 24]
BLK_DMAS = 6 + 2 * L


def build(nc, x, norm_mix_g, norm_mlp_g, attn_w_in, attn_b_f, attn_q_g, attn_k_g, attn_w_out, ssm_w_in,
          ssm_a_re, ssm_a_im, ssm_b_re, ssm_b_im, ssm_c_re, ssm_c_im, ssm_log_dt, ssm_d, ssm_w_glu,
          mlp_w1, mlp_w2, out):
    def scratch(name, shape, dt=F32):
        return nc.dram_tensor(name, shape, dt, kind="Internal").ap()

    qk_scr = scratch("qk_scr", (2 * D, T))
    v_scr = scratch("v_scr", (T, D))
    c_scr = scratch("c_scr", (NH, T))
    u_scr = scratch("u_scr", (D, T))
    y_scr = scratch("y_scr", (D, T))
    wst_scr = scratch("wst_scr", (2, P, GP * P))
    wo_scr = scratch("wo_scr", (2, P, GP * P))
    cs_scr = scratch("cs_scr", (2, P, GP * NC))
    kp_scr = scratch("kp_scr", (NG, GC, (2 * L - 1) * GC))

    ctx = ExitStack()
    with ctx:
        def sem(name):
            return ctx.enter_context(nc.semaphore(name))

        def sb(name, shape, dt=F32, stack=ctx):
            return stack.enter_context(nc.sbuf_tensor(name, shape, dt))

        ps = ctx.enter_context(nc.psum_tensor("ps", [P, 8, HALF], F32))

        xT = sb("xT", [P, KT, T])
        with ExitStack() as st:
            xs = sb("xs", [P, 2, D], stack=st)
            kall = sb("kall", [P, GP, 2, GC], stack=st)
            dm = sb("dm", [P, NG, GC], stack=st)
            ct = sb("ct", [P, 2, 4, P], stack=st)
            tst = sb("tst", [P, 2, 4 * P], stack=st)
            zero = sb("zero", [NG, (L - 1) * GC], stack=st)
        act_hi = sb("act_hi", [P, KT, T], F32R)
        act_lo = sb("act_lo", [P, KT, T], F32R)
        raw = sb("raw", [P, 2, PANEL])
        w_hi = sb("w_hi", [P, 2, PANEL], F32R)
        w_lo = sb("w_lo", [P, 2, PANEL], F32R)
        ident = sb("ident", [P, P])
        ones = sb("ones", [P, P])
        headsum = sb("headsum", [P, P])
        gains = sb("gains", [P, 4, KT])
        qk_g = sb("qk_g", [P, 2])
        qk_gain = sb("qk_gain", [P, N_QK])
        eps_t = sb("eps_t", [P, 1])
        fb = sb("fb", [NH, 1])
        ab = sb("ab", [P, 11, GP])
        mx = sb("mx", [P, 16, 2])

        w_hi8 = w_hi[:, :, :].rearrange("p s (k f) -> p s k f", k=KT)
        w_lo8 = w_lo[:, :, :].rearrange("p s (k f) -> p s k f", k=KT)
        w_hi2 = w_hi[:, :, :].rearrange("p s (k f) -> p s k f", k=2)
        w_lo2 = w_lo[:, :, :].rearrange("p s (k f) -> p s k f", k=2)

        def phase():
            return ExitStack()

        with phase() as st:
            r32 = sb("r32", [GP, 22, P], stack=st)
            i32 = sb("i32", [GP, 2, P], I32, stack=st)
            ldt = sb("ldt", [GP, 2], stack=st)
            zr = sb("zr", [P, GP, L, GC], stack=st)
            zi = sb("zi", [P, GP, L, GC], stack=st)
            pt = sb("pt", [P, 2, GP * GC], stack=st)
            bc = sb("bc", [P, 2, GP, GC], stack=st)
        with phase() as st:
            os_ = sb("os", [P, 2, D], stack=st)
        with phase() as st:
            sq = sb("sq", [P, 2, T], stack=st)
            rs = sb("rs", [P, T], stack=st)
            rinv = sb("rinv", [P, T], stack=st)
            hf = sb("hf", [P, 2, T], stack=st)
        with phase() as st:
            sqh = sb("sqh", [P, 4, HALF], stack=st)
            rsh = sb("rsh", [P, 4, HALF], stack=st)
            rih = sb("rih", [P, 2, HALF], stack=st)
            stg = sb("stg", [P, 2, HALF], stack=st)
            vst = sb("vst", [P, 2, PW], stack=st)
            wf = sb("wf", [P, KT, NH], stack=st)
            wf_hi = sb("wf_hi", [P, KT, P], F32R, stack=st)
            wf_lo = sb("wf_lo", [P, KT, P], F32R, stack=st)
            fy = sb("fy", [NH, T], stack=st)
            fe = sb("fe", [NH, T], stack=st)
            fl = sb("fl", [NH, T], stack=st)
            fc = sb("fc", [NH, T], stack=st)
            fone = sb("fone", [NH, T], stack=st)
        with phase() as st:
            prob = sb("prob", [P, 2, 4, T], stack=st)
            pt_hi = sb("pt_hi", [P, 2, HALF], F32R, stack=st)
            pt_lo = sb("pt_lo", [P, 2, HALF], F32R, stack=st)
            cb = sb("cb", [P, 2, T], stack=st)
            o_f = sb("o_f", [P, HALF], stack=st)
            o_r = sb("o_r", [P, HALF], stack=st)
            mask = sb("mask", [P, P], F32R, stack=st)
            ident_r = sb("ident_r", [P, P], F32R, stack=st)
            mask_f = sb("mask_f", [P, P], stack=st)
            tick = sb("tick", [P, 1], stack=st)
        with phase() as st:
            hid_hi = sb("hid_hi", [P, 2, T], F32R, stack=st)
            hid_lo = sb("hid_lo", [P, 2, T], F32R, stack=st)
            relu = sb("relu", [P, 4, HALF], stack=st)
            hsq = sb("hsq", [P, 4, HALF], stack=st)
        with phase() as st:
            ust = sb("ust", [P, 2, HALF], stack=st)
            wst = sb("wst", [P, 2, PB, P], stack=st)
            wo = sb("wo", [P, 2, PB, P], stack=st)
            cs = sb("cs", [P, 2, PB, NC], stack=st)
            tap = sb("tap", [P, GB, P], stack=st)
            ub = sb("ub", [P, GB, NC], stack=st)
            decay = sb("decay", [P, PB, NC], stack=st)
            dmask = sb("dmask", [P, PB, NC], stack=st)
            vb = sb("vb", [P, 4, PB, NC], stack=st)
            xb = sb("xb", [P, 2, PB, NC], stack=st)
            yb = sb("yb", [P, GB, NC], stack=st)
            zt = sb("zt", [P, T], stack=st)
            sig = sb("sig", [P, 4, HALF], stack=st)
            gated = sb("gated", [P, 2, HALF], stack=st)

        q_raw, k_raw = raw[:, 0, 0:T], raw[:, 0, T:2 * T]
        v_raw = raw[:, 1, 0:T].rearrange("p (j f) -> p j f", j=KT)
        q_hi, k_hi = w_hi[:, 0, 0:T], w_hi[:, 0, T:2 * T]
        q_lo, k_lo = w_lo[:, 0, 0:T], w_lo[:, 0, T:2 * T]
        v_hi = w_hi[:, 1, :].rearrange("p (h j f) -> p h j f", h=2, j=KT)
        v_lo = w_lo[:, 1, :].rearrange("p (h j f) -> p h j f", h=2, j=KT)

        raw_in = [sem("raw_in0"), sem("raw_in1")]
        hi_ready = sem("hi_ready")
        lo_ready = sem("lo_ready")
        w_used = sem("w_used")
        const_chain = sem("const_chain")
        const_ready = sem("const_ready")
        small_in = sem("small_in")
        ssm_in = sem("ssm_in")
        ct_in = sem("ct_in")
        dm_in = sem("dm_in")
        dm_ready = sem("dm_ready")
        prep_chain = sem("prep_chain")
        par_ready = sem("par_ready")
        par_turned = sem("par_turned")
        par_copied = sem("par_copied")
        b_used = sem("b_used")
        z_ready = sem("z_ready")
        c_turned = sem("c_turned")
        c_copied = sem("c_copied")
        z_turned = sem("z_turned")
        z_copied = sem("z_copied")
        tst_out = [sem("tst_out0"), sem("tst_out1")]
        k_done = sem("k_done")
        k_copied = sem("k_copied")
        k_ready = sem("k_ready")
        k_out = sem("k_out")
        wo_ready = sem("wo_ready")
        wo_out = sem("wo_out")
        cs_ready = sem("cs_ready")
        cs_out = sem("cs_out")
        x_in = [sem("x_in0"), sem("x_in1")]
        x_turned = sem("x_turned")
        x_copied = sem("x_copied")
        sq_ready = sem("sq_ready")
        sq_added = sem("sq_added")
        rs_ready = sem("rs_ready")
        rinv_ready = sem("rinv_ready")
        hf_ready = sem("hf_ready")
        ahi_ready = sem("ahi_ready")
        alo_ready = sem("alo_ready")
        qk_done = sem("qk_done")
        qk_sq = sem("qk_sq")
        qk_sum = sem("qk_sum")
        qk_root = sem("qk_root")
        qk_inv = sem("qk_inv")
        qk_free = sem("qk_free")
        stg_out = [sem("stg_out0"), sem("stg_out1")]
        v_done = sem("v_done")
        v_copied_a = sem("v_copied_a")
        v_copied_d = sem("v_copied_d")
        vst_out = [sem("vst_out0"), sem("vst_out1")]
        f_w = sem("f_w")
        f_zero = sem("f_zero")
        f_hi = sem("f_hi")
        f_lo = sem("f_lo")
        f_done = sem("f_done")
        f_act = sem("f_act")
        f_min = sem("f_min")
        c_out = sem("c_out")
        v_pad = sem("v_pad")
        mask_ready = sem("mask_ready")
        mask_chain = sem("mask_chain")
        mask_hi = sem("mask_hi")
        qkv_in = sem("qkv_in")
        c_in = sem("c_in")
        qkv_hi = sem("qkv_hi")
        qkv_lo = sem("qkv_lo")
        s_done = sem("s_done")
        s_free = sem("s_free")
        nm_ready = sem("nm_ready")
        p_ready = sem("p_ready")
        t_done = sem("t_done")
        pth_ready = sem("pth_ready")
        ptl_ready = sem("ptl_ready")
        pv_done = sem("pv_done")
        o_inv = sem("o_inv")
        o_free = sem("o_free")
        ohi_ready = sem("ohi_ready")
        olo_ready = sem("olo_ready")
        oproj_done = sem("oproj_done")
        oproj_free = sem("oproj_free")
        up_done = [sem("up_done0"), sem("up_done1")]
        up_free = [sem("up_free0"), sem("up_free1")]
        hsq_ready = [sem("hsq_ready0"), sem("hsq_ready1")]
        hidh_ready = [sem("hidh_ready0"), sem("hidh_ready1")]
        hidl_ready = [sem("hidl_ready0"), sem("hidl_ready1")]
        down_done = [sem("down_done0"), sem("down_done1")]
        down_free = [sem("down_free0"), sem("down_free1")]
        u_done = sem("u_done")
        u_free = sem("u_free")
        u_out = [sem("u_out0"), sem("u_out1")]
        dmask_ready = sem("dmask_ready")
        blk_in = sem("blk_in")
        decay_ready = sem("decay_ready")
        drive_done = sem("drive_done")
        scan_chain = sem("scan_chain")
        state_ready = sem("state_ready")
        y_done = sem("y_done")
        gelu_done = sem("gelu_done")
        y_out = sem("y_out")
        z_in = sem("z_in")
        z_hi = sem("z_hi")
        z_lo = sem("z_lo")
        glu_done = sem("glu_done")
        sig_ready = sem("sig_ready")
        glu_free = sem("glu_free")
        glu_added = sem("glu_added")
        out_turned = sem("out_turned")
        out_copied = sem("out_copied")
        y_stored = [sem("y_stored0"), sem("y_stored1")]

        block = ctx.enter_context(nc.Block())

        x_rows = x.rearrange("b t d -> (b t) d")
        out_rows = out.rearrange("b t d -> (b t) d")

        def cols(w, c0):
            return w.rearrange("(k p) f -> p k f", p=P)[:, :, bass.ds(c0, PW)]

        w_in, w_out_, w_sin, w_glu = attn_w_in[0], attn_w_out[0], ssm_w_in[0], ssm_w_glu[0]

        @block.sync
        def _(sp):
            def load(slot, m, src, first=False):
                if not first:
                    sp.wait_ge(lo_ready, 2 * m + slot - 1)
                dst = raw[:, slot, :]
                if len(src.shape) == 3:
                    dst = dst.rearrange("p (k f) -> p k f", k=src.shape[1])
                elif len(src.shape) == 4:
                    dst = dst.rearrange("p (k a f) -> p k a f", k=src.shape[1], a=src.shape[2])
                sp.dma_start(dst, src).then_inc(raw_in[slot], 16)

            load(0, 0, cols(w_in, 0), first=True)
            load(1, 0, cols(w_in, PW), first=True)
            with sp.Fori(1, N_ATT // 2) as m:
                load(0, m, cols(w_in, m * (2 * PW)))
                load(1, m, cols(w_in, m * (2 * PW) + PW))

            sp.wait_ge(lo_ready, N_ATT)
            for s in (0, 1):
                sp.wait_ge(stg_out[s], 16 * N_QK * 2)
                sp.wait_ge(vst_out[s], 16 * N_V * 4)
            sp.wait_ge(c_out, 16)
            with sp.Fori(0, PAIRS) as p:
                sp.wait_ge(qkv_lo, 4 * p)
                sp.dma_start(q_raw, qk_scr[bass.ts(p, P), :]).then_inc(qkv_in, 16)
                sp.dma_start(k_raw, qk_scr[bass.ds(p * P + D, P), :]).then_inc(qkv_in, 16)
                sp.dma_start(v_raw, v_scr.rearrange("(j k) f -> k j f", k=P)[:, :, bass.ts(p, P)])\
                    .then_inc(qkv_in, 16)
                sp.wait_ge(s_free, 16 * p + 2)
                for h in range(2):
                    sp.dma_start(cb[:, h, :], c_scr[bass.ds(2 * p + h, 1), :].to_broadcast((P, T)))\
                        .then_inc(c_in, 16)
            sp.wait_ge(qkv_lo, 4 * PAIRS)

            load(0, OUT0 // 2, cols(w_out_, 0))
            load(1, OUT0 // 2, cols(w_out_, PW))
            with sp.Fori(1, N_OUT // 2) as i:
                load(0, i + OUT0 // 2, cols(w_out_, i * (2 * PW)))
                load(1, i + OUT0 // 2, cols(w_out_, i * (2 * PW) + PW))

            def mlp_loads(layer, n0):
                with sp.Fori(0, N_MLP // 2) as i:
                    load(0, i + n0 // 2, cols(mlp_w1[layer], i * PW))
                    load(1, i + n0 // 2,
                         mlp_w2[layer].rearrange("(i k p) f -> i p k f", k=2, p=P)[bass.ds(i, 1)].squeeze(0))

            mlp_loads(0, MLP0)
            with sp.Fori(0, N_SIN // 2) as i:
                load(0, i + SIN0 // 2, cols(w_sin, i * (2 * PW)))
                load(1, i + SIN0 // 2, cols(w_sin, i * (2 * PW) + PW))

            def glu_load(slot, i):
                load(slot, i + GLU0 // 2, cols(w_glu, i * PW + slot * D))

            glu_load(0, 0)
            glu_load(1, 0)

            for s in (0, 1):
                sp.wait_ge(tst_out[s], 16 * GP // 4)
            sp.wait_ge(k_out, 16 * (L + 1))
            sp.wait_ge(wo_out, 32)
            sp.wait_ge(cs_out, 32)
            for s in (0, 1):
                sp.wait_ge(u_out[s], 16 * 2 * N_SIN)
            with sp.Fori(0, BLK) as q:
                sp.wait_ge(y_done, 2 * q)
                for a in range(2):
                    sp.dma_start(wst[:, a, :, :], wst_scr[a].rearrange("p (g f) -> p g f", f=P)
                                 [:, bass.ts(q, PB), :]).then_inc(blk_in, 16)
                    sp.dma_start(wo[:, a, :, :], wo_scr[a].rearrange("p (g f) -> p g f", f=P)
                                 [:, bass.ts(q, PB), :]).then_inc(blk_in, 16)
                    sp.dma_start(cs[:, a, :, :], cs_scr[a].rearrange("p (g f) -> p g f", f=NC)
                                 [:, bass.ts(q, PB), :]).then_inc(blk_in, 16)
                for s in range(L):
                    rows = slice(GC * s, GC * s + GC)
                    sp.dma_start(tap[rows, :, :], kp_scr[bass.ts(q, GB), :, (L - 1 - s) * GC:(2 * L - 1 - s) * GC]
                                 .rearrange("g c w -> c g w")).then_inc(blk_in, 16)
                    sp.dma_start(ub[rows, :, :], u_scr.rearrange("(g c) (s j) -> c g s j", c=GC, s=L)
                                 [:, bass.ts(q, GB), s, :]).then_inc(blk_in, 16)

            with sp.Fori(1, N_GLU // 2) as i:
                glu_load(0, i)
                glu_load(1, i)
            mlp_loads(1, MLP1)

            with sp.Fori(0, T // P // 2) as i:
                for s in (0, 1):
                    sp.wait_ge(out_copied, 4 * i + 2 * s + 2 + 4)
                    sp.dma_start(out_rows[bass.ds(i * (2 * P) + s * P, P), :], os_[:, s, :])\
                        .then_inc(y_stored[s], 16)
            for s in (0, 1):
                sp.wait_ge(y_stored[s], 16 * T // P // 2)

        @block.gpsimd
        def _(pool):
            pool.dma_start(ldt[:, :], ssm_log_dt[0].rearrange("(g a) -> g a", a=2)).then_inc(ssm_in, 16)
            pool.dma_start(r32[:, 0, :], ssm_a_re[0].rearrange("(g a) p -> g (a p)", a=2)).then_inc(ssm_in, 16)
            pool.dma_start(r32[:, 1, :], ssm_a_im[0].rearrange("(g a) p -> g (a p)", a=2)).then_inc(ssm_in, 16)
            for n, b in enumerate((ssm_b_re, ssm_b_im)):
                pool.dma_start(bc[:, n, :, :], b[0].rearrange("(g a) p c -> (a p) g c", a=2)).then_inc(ssm_in, 16)
            for s in (0, 1):
                pool.dma_start(xs[:, s, :], x_rows[s * P:(s + 1) * P, :]).then_inc(x_in[s], 16)

            def fill(ins, n):
                ins.then_inc(const_chain, 1)
                pool.wait_ge(const_chain, n)

            fill(pool.memset(ident[:, :], 0.0), 1)
            pool.affine_select(out=ident[:, :], in_=ident[:, :], compare_op=ALU.not_equal, fill=1.0, base=0,
                               pattern=[[-1, P]], channel_multiplier=1).then_inc(const_ready, 1)
            pool.memset(ones[:, :], 1.0).then_inc(const_ready, 1)
            fill(pool.memset(headsum[:, :], 0.0), 2)
            fill(pool.memset(zero[:, :], 0.0), 3)
            pool.memset(eps_t[:, :], EPS).then_inc(const_ready, 1)
            pool.memset(headsum[0:HD, 0:HD], 1.0).then_inc(const_ready, 1)
            pool.wait_ge(const_ready, 4)
            pool.memset(headsum[HD:P, HD:P], 1.0).then_inc(const_ready, 1)
            pool.wait_ge(const_ready, 5)
            with nc.allow_non_contiguous_dma(reason="gains of a few KB"):
                for n, g in enumerate((norm_mix_g[0], norm_mix_g[1], norm_mlp_g[0], norm_mlp_g[1])):
                    pool.dma_start(gains[:, n, :], g.rearrange("(k p) -> p k", p=P)).then_inc(small_in, 16)
                for n, g in enumerate((attn_q_g, attn_k_g)):
                    for h in range(2):
                        pool.dma_start(qk_g[h * HD:(h + 1) * HD, n:n + 1],
                                       g[0].rearrange("(p a) -> p a", a=1)).then_inc(small_in, 16)
                pool.dma_start(fb[:, :], attn_b_f[0].rearrange("(h a) -> h a", a=1)).then_inc(small_in, 16)
            for n, c in enumerate((ssm_c_re, ssm_c_im)):
                for t in range(4):
                    for a in range(2):
                        pool.dma_start(ct[:, n, t, a * NS:(a + 1) * NS],
                                       c[0].rearrange("(t g a) c p -> t a g c p", t=4, a=2)[t, a])\
                            .then_inc(ct_in, 16)
            pool.dma_start(dm[96:P, :, :], ssm_d[0].rearrange("(o g c) -> o g c", o=1, c=GC)
                           .to_broadcast((32, NG, GC))).then_inc(dm_in, 16)
            pool.dma_start(kp_scr[:, :, 0:(L - 1) * GC],
                           zero[:, :].unsqueeze(1).to_broadcast((NG, GC, (L - 1) * GC))).then_inc(k_out, 16)
            pool.wait_ge(dm_in, 16)
            pool.affine_select(out=dm[96:P, :, :], in_=dm[96:P, :, :], compare_op=ALU.is_equal, fill=0.0,
                               base=-GC, pattern=[[0, NG], [-1, GC]], channel_multiplier=1).then_inc(dm_ready, 1)

            with pool.Fori(0, T // P // 2 - 1) as i:
                for s in (0, 1):
                    pool.wait_ge(x_turned, 4 * i + 2 * s + 2)
                    pool.dma_start(xs[:, s, :], x_rows[bass.ds(i * (2 * P) + (2 + s) * P, P), :])\
                        .then_inc(x_in[s], 16)

            for a in range(2):
                for b in range(GP // 4):
                    n = a * (GP // 4) + b
                    pool.wait_ge(z_copied, n + 1)
                    pool.dma_start(wst_scr[a][:, b * 4 * P:(b + 1) * 4 * P], tst[:, n % 2, :])\
                        .then_inc(tst_out[n % 2], 16)
            pool.wait_ge(k_ready, 1)
            for r in range(L):
                row = 2 * L - 2 - r
                pool.dma_start(kp_scr[:, :, row * GC:(row + 1) * GC].rearrange("g c w -> c g w"),
                               kall[GC * r:GC * r + GC, :, :, :].rearrange("p g a c -> p (g a) c"))\
                    .then_inc(k_out, 16)
            pool.wait_ge(wo_ready, 1)
            pool.dma_start(wo_scr[0], zr[:, :, :, :].rearrange("p g s c -> p (g s c)")).then_inc(wo_out, 16)
            pool.dma_start(wo_scr[1], zi[:, :, :, :].rearrange("p g s c -> p (g s c)")).then_inc(wo_out, 16)
            pool.wait_ge(cs_ready, 1)
            pool.dma_start(cs_scr[0], zr[:, :, :, :].rearrange("p g s c -> p (g s c)")).then_inc(cs_out, 16)
            pool.dma_start(cs_scr[1], zi[:, :, :, :].rearrange("p g s c -> p (g s c)")).then_inc(cs_out, 16)

            def norm_lo(n):
                for k in range(KT):
                    pool.wait_ge(ahi_ready, KT * n + k + 1)
                    pool.tensor_tensor(act_lo[:, k, :], hf[:, k % 2, :], act_hi[:, k, :].bitcast(F32),
                                       ALU.subtract).then_inc(alo_ready, 1)

            norm_lo(0)
            pool.wait_ge(alo_ready, KT)
            pool.dma_start(wf[:, :, :], attn_w_in[0].rearrange("(k p) f -> p k f", p=P)[:, :, 3 * D:3 * D + NH])\
                .then_inc(f_w, 16)
            with pool.Fori(0, N_QK // 2) as i:
                for slot in range(2):
                    for g in range(4):
                        m, half = g // 2, g % 2
                        pool.wait_ge(qk_free, 8 * i + 4 * slot + g + 1 + 4)
                        pool.dma_start(qk_scr[bass.ds(i * (4 * P) + (2 * slot + m) * P, P),
                                              half * HALF:(half + 1) * HALF], stg[:, g % 2, :])\
                            .then_inc(stg_out[g % 2], 16)
            with pool.Fori(0, N_V // 2) as i:
                for slot in range(2):
                    for t in range(KT):
                        pool.wait_ge((v_copied_a, v_copied_d)[t % 2], 8 * i + 4 * slot + t // 2 + 1 + 2)
                        pool.dma_start(v_scr[t * P:(t + 1) * P, bass.ds(i * (2 * PW) + slot * PW, PW)],
                                       vst[:, t % 2, :]).then_inc(vst_out[t % 2], 16)
            pool.wait_ge(f_min, 4)
            pool.dma_start(c_scr, fc[:, :]).then_inc(c_out, 16)

            pool.wait_ge(c_out, 16)
            pool.memset(mask_f[:, :], 0.0).then_inc(mask_chain, 1)
            pool.wait_ge(mask_chain, 1)
            pool.affine_select(out=mask_f[:, :], in_=mask_f[:, :], compare_op=ALU.is_ge, fill=-MASKED, base=0,
                               pattern=[[-1, P]], channel_multiplier=1).then_inc(mask_ready, 1)

            def mlp_hidden(layer):
                with pool.Fori(0, N_MLP // 2) as i:
                    for g in range(5):
                        if g < 4:
                            pool.wait_ge(up_free[layer], 4 * i + g + 1 + 4)
                            pool.tensor_tensor(hsq[:, g, :], relu[:, g, :], relu[:, g, :], ALU.mult)\
                                .then_inc(hsq_ready[layer], 1)
                        if g > 0:
                            m, half = (g - 1) % 2, (g - 1) // 2
                            pool.wait_ge(hidh_ready[layer], 4 * i + g)
                            part = slice(half * HALF, (half + 1) * HALF)
                            pool.tensor_tensor(hid_lo[:, m, part], hsq[:, g - 1, :],
                                               hid_hi[:, m, part].bitcast(F32), ALU.subtract)\
                                .then_inc(hidl_ready[layer], 1)

            norm_lo(1)
            mlp_hidden(0)
            norm_lo(2)

            with pool.Fori(0, N_SIN // 2) as i:
                for slot in range(2):
                    for g in range(4):
                        m, half = g // 2, g % 2
                        pool.wait_ge(u_free, 8 * i + 4 * slot + g + 1 + 4)
                        pool.dma_start(u_scr[bass.ds(i * (4 * P) + (2 * slot + m) * P, P),
                                             half * HALF:(half + 1) * HALF], ust[:, g % 2, :])\
                            .then_inc(u_out[g % 2], 16)
            pool.memset(dmask[:, :, :], 1.0).then_inc(dmask_ready, 1)
            pool.wait_ge(dmask_ready, 1)
            pool.memset(dmask[:, :, 0:1], 0.0).then_inc(dmask_ready, 1)
            pool.wait_ge(dmask_ready, 2)
            with pool.Fori(0, BLK) as q:
                pool.wait_ge(state_ready, 2 * q)
                pool.tensor_tensor(decay[:, :, :], dmask[:, :, :],
                                   ab[:, 6, bass.ts(q, PB)].unsqueeze(2).to_broadcast((P, PB, NC)), ALU.mult)\
                    .then_inc(decay_ready, 1)
                pool.wait_ge(gelu_done, 2 * q + 2)
                for s in range(L):
                    pool.dma_start(y_scr.rearrange("(g c) (s j) -> c g s j", c=GC, s=L)[:, bass.ts(q, GB), s, :],
                                   yb[GC * s:GC * s + GC, :, :]).then_inc(y_out, 16)
                pool.wait_ge(y_out, 16 * L * (q + 1))
                pool.wait_ge(z_lo, q)
                pool.dma_start(zt[:, :], y_scr[bass.ts(q, P), :]).then_inc(z_in, 16)

            norm_lo(3)
            mlp_hidden(1)

        @block.scalar
        def _(act):
            def copy(dst, src):
                return act.activation(dst, src, ACT.Copy)

            def split_hi(slot, m):
                act.wait_ge(raw_in[slot], 16 * m + 16)
                copy(w_hi[:, slot, :], raw[:, slot, :]).then_inc(hi_ready, 1)

            act.sem_inc(x_copied, 4)
            with act.Fori(0, T // P // 2) as i:
                for s in (0, 1):
                    for b in range(2):
                        act.wait_ge(x_turned, 4 * i + 2 * s + b + 1)
                        copy(xT[:, 4 * b:4 * b + 4, bass.ds(i * (2 * P) + s * P, P)],
                             ps[:, 2 * s + b, :].rearrange("p (k t) -> p k t", k=4)).then_inc(x_copied, 1)
            act.wait_ge(par_turned, 1)
            copy(ab[:, 0:7, :], ps[:, 4, 0:7 * GP].rearrange("p (n g) -> p n g", g=GP)).then_inc(par_copied, 1)
            act.wait_ge(c_turned, 1)
            act.wait_ge(b_used, 1)
            copy(bc[:, 0, :, :], ps[:, 5, :].rearrange("p (g c) -> p g c", c=GC)).then_inc(c_copied, 1)
            act.activation(bc[:, 1, :, :], ps[:, 6, :].rearrange("p (g c) -> p g c", c=GC), ACT.Copy,
                           scale=-1.0).then_inc(c_copied, 1)
            for n in range(2 * GP // 4):
                act.wait_ge(z_turned, n + 1)
                if n >= 2:
                    act.wait_ge(tst_out[n % 2], 16 * (n // 2))
                copy(tst[:, n % 2, :], ps[:, (7, 4)[n % 2], :]).then_inc(z_copied, 1)
            act.wait_ge(k_done, 1)
            for a in range(2):
                copy(kall[:, :, a, :], ps[:, 5 + a, :].rearrange("p (g c) -> p g c", c=GC)).then_inc(k_copied, 1)

            def norm(n):
                for k in range(KT):
                    if k >= 2:
                        act.wait_ge(sq_added, KT * n + k - 1)
                    act.activation(sq[:, k % 2, :], xT[:, k, :], ACT.Square).then_inc(sq_ready, 1)
                act.wait_ge(sq_added, KT * n + KT)
                for half in range(2):
                    act.activation(rs[:, half * HALF:(half + 1) * HALF], ps[:, half, :], ACT.Sqrt,
                                   bias=eps_t[:, 0:1], scale=1.0 / D).then_inc(rs_ready, 1)
                for k in range(KT):
                    act.wait_ge(hf_ready, KT * n + k + 1)
                    copy(act_hi[:, k, :], hf[:, k % 2, :]).then_inc(ahi_ready, 1)

            for s in (0, 1):
                act.wait_ge(tst_out[s], 16 * GP // 4)
            act.wait_ge(k_out, 16 * (L + 1))
            act.wait_ge(wo_out, 32)
            act.wait_ge(cs_out, 32)
            act.wait_ge(const_ready, 5)
            act.wait_ge(small_in, 16 * 9)
            act.wait_ge(x_copied, 4 + 2 * KT)
            norm(0)
            split_hi(0, 0)

            act.wait_ge(alo_ready, KT)
            with act.Fori(0, N_QK // 2) as i:
                for slot in range(2):
                    split_hi(1 - slot, i + slot)
                    for g in range(5):
                        if g < 4:
                            act.wait_ge(qk_done, 8 * i + 4 * slot + g + 1)
                            act.activation(sqh[:, g, :], ps[:, g, :], ACT.Square).then_inc(qk_sq, 1)
                        if g > 0:
                            act.wait_ge(qk_sum, 8 * i + 4 * slot + g)
                            act.activation(rsh[:, g - 1, :], ps[:, 4 + g - 1, :], ACT.Sqrt,
                                           bias=eps_t[:, 0:1], scale=1.0 / HD).then_inc(qk_root, 1)
            act.sem_inc(v_copied_a, 2)
            for i in range(N_V // 2):
                for slot in range(2):
                    act.wait_ge(v_done, 16 * i + 8 * slot)
                    if i + slot < N_V // 2:
                        split_hi(1 - slot, N_QK // 2 + i + slot)
                    for t in range(0, KT, 2):
                        act.wait_ge(v_done, 16 * i + 8 * slot + t + 1)
                        if i + slot + t > 0:
                            act.wait_ge(vst_out[0], 16 * (8 * i + 4 * slot + t // 2))
                        copy(vst[:, 0, :], ps[:, t % 4, 0:PW]).then_inc(v_copied_a, 1)
            act.wait_ge(f_w, 16)
            act.wait_ge(f_zero, 2)
            copy(wf_hi[:, :, 0:NH], wf[:, :, :]).then_inc(f_hi, 1)
            act.wait_ge(f_done, 1)
            act.activation(fy[:, :].rearrange("p (h t) -> p h t", h=2), ps[0:NH, 0:2, :], ACT.Identity,
                           bias=fb[:, 0:1]).then_inc(f_act, 1)
            act.wait_ge(f_act, 1)
            act.activation(fe[:, :], fy[:, :], ACT.Abs).then_inc(f_act, 1)
            act.wait_ge(f_act, 2)
            act.activation(fl[:, :], fe[:, :], ACT.Exp, scale=-1.0).then_inc(f_act, 1)
            act.wait_ge(f_act, 3)
            act.activation(fe[:, :], fl[:, :], ACT.Ln, bias=1.0).then_inc(f_act, 1)

            act.wait_ge(mask_ready, 1)
            copy(mask[:, :], mask_f[:, :]).then_inc(mask_hi, 1)
            copy(ident_r[:, :], ident[:, :]).then_inc(mask_hi, 1)
            order = attention_order()
            with act.Fori(0, PAIRS) as p:
                act.wait_ge(qkv_in, 48 * p + 48)
                act.wait_ge(pv_done, 24 * p + 2)
                copy(q_hi, q_raw).then_inc(qkv_hi, 1)
                copy(k_hi, k_raw).then_inc(qkv_hi, 1)
                for h in range(2):
                    act.wait_ge(v_pad, 4)
                    copy(v_hi[:, h, :, h * HD:(h + 1) * HD], v_raw[:, :, h * HD:(h + 1) * HD]).then_inc(qkv_hi, 1)

                def out_hi(u):
                    rows = slice(u // 2 * HD, (u // 2 + 1) * HD)
                    g = u % 2
                    act.wait_ge(o_free, 4 * p + u + 1 + 2)
                    copy(act_hi[rows, bass.ds(p, 1), g * HALF:(g + 1) * HALF].squeeze(1), o_f[rows, :])\
                        .then_inc(ohi_ready, 1)

                for kind, u, n in order:
                    if kind == "S":
                        b = 4 * u + n
                        keys = (4 * (u % 2) + n + 1) * P
                        act.wait_ge(nm_ready, 16 * p + b + 1)
                        act.activation(prob[:, u % 2, n, 0:keys], prob[:, u % 2, n, 0:keys], ACT.Exp,
                                       bias=mx[:, b, 1:2]).then_inc(p_ready, 1)
                    else:
                        jj = TILES_BEFORE[u] + n
                        lo = max(0, n - 4 * (u % 2)) * P
                        act.wait_ge(t_done, 24 * p + jj + 1)
                        act.wait_ge(pv_done, 24 * p + jj + 1)
                        copy(pt_hi[:, jj % 2, lo:HALF], ps[:, 4 + jj % 2, lo:HALF]).then_inc(pth_ready, 1)
                        if n == 0 and u > 0:
                            out_hi(u - 1)
                out_hi(3)

            act.wait_ge(pv_done, 24 * PAIRS + 2)
            def proj_splits(panel0, count):
                with act.Fori(0, count // 2) as i:
                    act.wait_ge(oproj_done, 8 * i)
                    split_hi(1, i + panel0 // 2)
                    act.wait_ge(oproj_done, 8 * i + 4)
                    split_hi(0, i + panel0 // 2 + 1)

            split_hi(0, OUT0 // 2)
            proj_splits(OUT0, N_OUT)

            def mlp(layer, panel0, last):
                act.sem_inc(up_free[layer], 4)

                def step(i, more):
                    act.wait_ge(down_done[layer], 16 * i)
                    split_hi(1, i + panel0 // 2)
                    for g in range(5):
                        if g < 4:
                            act.wait_ge(up_done[layer], 4 * i + g + 1)
                            act.wait_ge(hidl_ready[layer], 4 * i)
                            act.activation(relu[:, g, :], ps[:, g, :], ACT.Relu).then_inc(up_free[layer], 1)
                        if g > 0:
                            m, half = (g - 1) % 2, (g - 1) // 2
                            act.wait_ge(hsq_ready[layer], 4 * i + g)
                            act.wait_ge(down_done[layer], 16 * i)
                            copy(hid_hi[:, m, half * HALF:(half + 1) * HALF], hsq[:, g - 1, :])\
                                .then_inc(hidh_ready[layer], 1)
                    if more:
                        split_hi(0, i + panel0 // 2 + 1)
                if last:
                    with act.Fori(0, N_MLP // 2 - 1) as i:
                        step(i, True)
                    step(N_MLP // 2 - 1, False)
                else:
                    with act.Fori(0, N_MLP // 2) as i:
                        step(i, True)

            act.wait_ge(oproj_free, 4 + 4 * N_OUT)
            norm(1)
            act.wait_ge(alo_ready, 2 * KT)
            mlp(0, MLP0, last=False)

            act.wait_ge(down_free[0], 4 + 16 * N_MLP // 2)
            norm(2)
            act.wait_ge(alo_ready, 3 * KT)
            act.sem_inc(u_free, 4)
            with act.Fori(0, N_SIN // 2) as i:
                for slot in range(2):
                    split_hi(1 - slot, i + (SIN0 // 2 + slot))
                    for g in range(4):
                        act.wait_ge(u_done, 8 * i + 4 * slot + g + 1)
                        act.wait_ge(u_out[g % 2], 16 * (4 * i + 2 * slot + g // 2))
                        copy(ust[:, g % 2, :], ps[:, g, :]).then_inc(u_free, 1)
            with act.Fori(0, BLK) as q:
                for b in range(2):
                    act.wait_ge(y_done, 2 * q + b + 1)
                    act.wait_ge(y_out, 16 * L * q)
                    act.activation(yb[:, :, :].rearrange("p (c a) j -> p a c j", a=2)[:, b, :, :],
                                   ps[:, 2 + b, :].rearrange("p (g j) -> p g j", g=PB), ACT.Gelu_apprx_tanh)\
                        .then_inc(gelu_done, 1)
                act.wait_ge(z_in, 16 * q + 16)
                copy(act_hi[:, bass.ds(q, 1), :].squeeze(1), zt[:, :]).then_inc(z_hi, 1)
            with act.Fori(0, N_GLU // 2) as i:
                for slot in range(2):
                    if slot == 1:
                        act.wait_ge(glu_done, 8 * i + 4)
                    split_hi(1 - slot, i + (GLU0 // 2 + slot))
                    if slot == 1:
                        for g in range(4):
                            act.wait_ge(glu_done, 8 * i + g + 5)
                            act.wait_ge(glu_free, 4 * i + g + 1)
                            act.activation(sig[:, g, :], ps[:, 4 + g, :], ACT.Sigmoid).then_inc(sig_ready, 1)
            act.wait_ge(glu_added, 2 * N_GLU)
            norm(3)
            act.wait_ge(alo_ready, 4 * KT)
            mlp(1, MLP1, last=True)

            act.sem_inc(out_copied, 4)
            with act.Fori(0, T // P // 2) as i:
                for s in (0, 1):
                    act.wait_ge(y_stored[s], 16 * i)
                    for b in range(2):
                        act.wait_ge(out_turned, 4 * i + 2 * s + b + 1)
                        copy(os_[:, s, b * HALF:(b + 1) * HALF], ps[:, 2 * s + b, :]).then_inc(out_copied, 1)

        @block.tensor
        def _(pe):
            def times(dst, w1, w2, a1, a2, start, stop):
                pe.matmul(dst, w1, a1, start=start, stop=False)
                pe.matmul(dst, w1, a2, start=False, stop=False)
                return pe.matmul(dst, w2, a1, start=False, stop=stop)

            def project(bank, slot, col, half):
                tok = slice(half * HALF, (half + 1) * HALF)
                for k in range(KT):
                    last = times(ps[:, bank, :], w_hi8[:, slot, k, col:col + P], w_lo8[:, slot, k, col:col + P],
                                 act_hi[:, k, tok], act_lo[:, k, tok], k == 0, k == KT - 1)
                return last

            pe.wait_ge(const_ready, 1)
            with pe.Fori(0, T // P // 2) as i:
                for s in (0, 1):
                    pe.wait_ge(x_in[s], 16 * i + 16)
                    for b in range(2):
                        pe.wait_ge(x_copied, 4 * i + 2 * s + b + 1)
                        for k in range(4):
                            last = pe.transpose(ps[:, 2 * s + b, k * P:(k + 1) * P],
                                                xs[:, s, (4 * b + k) * P:(4 * b + k + 1) * P], ident[:, :])
                        last.then_inc(x_turned, 1)
            pe.wait_ge(par_ready, 1)
            for n in range(7):
                last = pe.transpose(ps[:, 4, n * GP:(n + 1) * GP], r32[:, 2 + n, :], ident[0:GP, 0:GP])
            last.then_inc(par_turned, 1)
            pe.wait_ge(ct_in, 16 * 16)
            for a in range(2):
                for t in range(4):
                    last = pe.transpose(ps[:, 5 + a, t * P:(t + 1) * P], ct[:, a, t, :], ident[:, :])
            last.then_inc(c_turned, 1)
            pe.wait_ge(z_ready, 1)
            pe.wait_ge(par_copied, 1)
            for n in range(2 * GP // 4):
                z = (zr, zi)[n // (GP // 4)]
                if n >= 2:
                    pe.wait_ge(z_copied, n - 1)
                for b in range(4):
                    last = pe.transpose(ps[:, (7, 4)[n % 2], b * P:(b + 1) * P],
                                        z[:, 4 * (n % (GP // 4)) + b, :, :].rearrange("p s c -> p (s c)"), ident[:, :])
                last.then_inc(z_turned, 1)
            pe.wait_ge(c_copied, 2)
            for a in range(2):
                rows = slice(a * NS, (a + 1) * NS)
                for g in range(GP):
                    dst = ps[:, 5 + a, g * GC:(g + 1) * GC]
                    pe.matmul(dst, zr[rows, g, :, :].rearrange("p s c -> p (s c)"), bc[rows, 0, g, :],
                              start=True, stop=False)
                    last = pe.matmul(dst, zi[rows, g, :, :].rearrange("p s c -> p (s c)"), bc[rows, 1, g, :],
                                     start=False, stop=True)
            last.then_inc(k_done, 1)

            def norm(n):
                for k in range(KT):
                    pe.wait_ge(sq_ready, KT * n + k + 1)
                    for half in range(2):
                        last = pe.matmul(ps[:, half, :], ones[:, :], sq[:, k % 2, half * HALF:(half + 1) * HALF],
                                         start=(k == 0), stop=(k == KT - 1))
                    last.then_inc(sq_added, 1)
                pe.wait_ge(alo_ready, KT * n + KT)

            pe.wait_ge(k_copied, 2)
            norm(0)
            pe.wait_ge(const_ready, 5)
            with pe.Fori(0, N_QK // 2) as i:
                for slot in range(2):
                    pe.wait_ge(lo_ready, 2 * i + slot + 1)
                    for g in range(5):
                        if g < 4:
                            pe.wait_ge(qk_free, 8 * i + 4 * slot + g + 1)
                            project(g, slot, g // 2 * P, g % 2).then_inc(qk_done, 1)
                        if g > 0:
                            pe.wait_ge(qk_sq, 8 * i + 4 * slot + g)
                            pe.matmul(ps[:, 4 + g - 1, :], headsum[:, :], sqh[:, g - 1, :],
                                      start=True, stop=True).then_inc(qk_sum, 1)
            pe.wait_ge(qk_free, 4 * N_QK + 4)
            with pe.Fori(0, N_V // 2) as i:
                for slot in range(2):
                    pe.wait_ge(lo_ready, 2 * i + (N_QK + slot + 1))
                    for t in range(KT):
                        pe.wait_ge((v_copied_a, v_copied_d)[t % 2], 8 * i + 4 * slot + t // 2 + 1)
                        dst = ps[:, t % 4, 0:PW]
                        tok = slice(t * P, (t + 1) * P)
                        for k in range(KT):
                            last = times(dst, act_hi[:, k, tok], act_lo[:, k, tok], w_hi8[:, slot, k, :],
                                         w_lo8[:, slot, k, :], k == 0, k == KT - 1)
                        last.then_inc(v_done, 1)
            pe.wait_ge(v_copied_a, 2 + 4 * N_V)
            pe.wait_ge(v_copied_d, 2 + 4 * N_V)
            pe.wait_ge(f_lo, 1)
            for half in range(2):
                tok = slice(half * HALF, (half + 1) * HALF)
                for k in range(KT):
                    last = times(ps[:, half, :], wf_hi[:, k, :], wf_lo[:, k, :], act_hi[:, k, tok],
                                 act_lo[:, k, tok], k == 0, k == KT - 1)
            last.then_inc(f_done, 1)

            pe.wait_ge(f_act, 1)
            pe.wait_ge(mask_hi, 2)
            pe.sem_inc(pv_done, 2)
            order = attention_order()
            with pe.Fori(0, PAIRS) as p:
                pe.wait_ge(qkv_lo, 4 * p + 4)

                def values(u, j):
                    jj = TILES_BEFORE[u] + j
                    h = u // 2
                    lo = max(0, j - 4 * (u % 2)) * P
                    if j == 0:
                        pe.wait_ge(o_free, 4 * p + u + 1)
                    pe.wait_ge(ptl_ready, 24 * p + jj + 1 + 2)
                    times(ps[:, 6 + u % 2, lo:HALF], v_hi[:, h, j, :], v_lo[:, h, j, :],
                          pt_hi[:, jj % 2, lo:HALF], pt_lo[:, jj % 2, lo:HALF], j == 0, j == key_tiles(u) - 1)\
                        .then_inc(pv_done, 1)

                before = None
                for kind, u, n in order:
                    if kind == "S":
                        b = 4 * u + n
                        rows = slice(u // 2 * HD, (u // 2 + 1) * HD)
                        i = 4 * (u % 2) + n
                        mine = slice(i * P, (i + 1) * P)
                        pe.wait_ge(s_free, 16 * p + b + 1)
                        keys = (i + 1) * P
                        for k0 in range(0, keys, HALF):
                            k1 = min(keys, k0 + HALF)
                            last = times(ps[:, 2 * (b % 2) + k0 // HALF, 0:k1 - k0], q_hi[rows, mine],
                                         q_lo[rows, mine], k_hi[rows, k0:k1], k_lo[rows, k0:k1], True, k1 < keys)
                        last = pe.matmul(ps[:, 2 * (b % 2) + k0 // HALF, i * P - k0:k1 - k0], ident_r[:, :],
                                         mask[:, :], start=False, stop=True)
                        last.then_inc(s_done, 1)
                    else:
                        jj = TILES_BEFORE[u] + n
                        if n == 0:
                            pe.wait_ge(p_ready, 16 * p + 4 * u + 4)
                        pe.wait_ge(ptl_ready, 24 * p + jj + 1)
                        for m in range(max(0, n - 4 * (u % 2)), 4):
                            last = pe.transpose(ps[:, 4 + jj % 2, m * P:(m + 1) * P],
                                                prob[:, u % 2, m, n * P:(n + 1) * P], ident[:, :])
                        last.then_inc(t_done, 1)
                        if before:
                            values(*before)
                        before = (u, n)
                values(*before)

            pe.wait_ge(olo_ready, 4 * PAIRS)
            pe.wait_ge(s_free, 16 * PAIRS + 2)

            def project_panels(count, panel0, done, free):
                with pe.Fori(0, count // 2) as i:
                    for slot in range(2):
                        pe.wait_ge(lo_ready, 2 * i + (panel0 + slot + 1))
                        for g in range(4):
                            pe.wait_ge(free, 8 * i + 4 * slot + g + 1)
                            project(g, slot, g // 2 * P, g % 2).then_inc(done, 1)

            project_panels(N_OUT, OUT0, oproj_done, oproj_free)

            def mlp(layer, panel0):
                with pe.Fori(0, N_MLP // 2) as i:
                    pe.wait_ge(lo_ready, 2 * i + (panel0 + 1))
                    for g in range(4):
                        pe.wait_ge(up_free[layer], 4 * i + g + 1)
                        project(g, 0, g % 2 * P, g // 2).then_inc(up_done[layer], 1)
                    pe.wait_ge(lo_ready, 2 * i + (panel0 + 2))
                    for half in range(2):
                        pe.wait_ge(hidl_ready[layer], 4 * i + 2 * half + 2)
                        tok = slice(half * HALF, (half + 1) * HALF)
                        for f in range(KT):
                            q = KT * half + f
                            pe.wait_ge(down_free[layer], 16 * i + q + 1)
                            for k in range(2):
                                last = times(ps[:, 4 + q % 4, :], w_hi2[:, 1, k, f * P:(f + 1) * P],
                                             w_lo2[:, 1, k, f * P:(f + 1) * P], hid_hi[:, k, tok],
                                             hid_lo[:, k, tok], k == 0, k == 1)
                            last.then_inc(down_done[layer], 1)

            pe.wait_ge(oproj_free, 4 + 4 * N_OUT)
            norm(1)
            pe.wait_ge(rs_ready, 4)
            mlp(0, MLP0)
            pe.wait_ge(down_free[0], 4 + 16 * N_MLP // 2)
            norm(2)
            pe.wait_ge(rs_ready, 6)
            project_panels(N_SIN, SIN0, u_done, u_free)

            pe.wait_ge(u_free, 4 + 4 * N_SIN)
            with pe.Fori(0, BLK) as q:
                pe.wait_ge(blk_in, (16 * BLK_DMAS) * q + 16 * BLK_DMAS)
                pe.wait_ge(state_ready, 2 * q)
                for c in range(PB):
                    for a in range(2):
                        rows = slice(a * NS, (a + 1) * NS)
                        for n in range(2):
                            last = pe.matmul(ps[rows, n, c * NC:(c + 1) * NC], wst[:, n, c, rows],
                                             ub[:, 2 * c + a, :], start=True, stop=True)
                last.then_inc(drive_done, 1)
                pe.wait_ge(gelu_done, 2 * q)
                pe.wait_ge(state_ready, 2 * q + 2)
                for a in range(2):
                    rows = slice(a * NS, (a + 1) * NS)
                    for c in range(PB):
                        c0 = c * NC
                        pe.matmul(ps[:, 2 + a, c0:c0 + NC], tap[:, 2 * c + a, :], ub[:, 2 * c + a, :],
                                  start=True, stop=False)
                        for n in range(2):
                            last = pe.matmul(ps[:, 2 + a, c0 + 1:c0 + NC], wo[rows, n, c, :],
                                             xb[rows, n, c, 0:NC - 1], start=False, stop=(n == 1))
                    last.then_inc(y_done, 1)

            pe.wait_ge(z_lo, BLK)
            with pe.Fori(0, N_GLU // 2) as i:
                for slot in range(2):
                    pe.wait_ge(lo_ready, 2 * i + (GLU0 + slot + 1))
                    for g in range(4):
                        pe.wait_ge(glu_free, 4 * i + g + 1)
                        project(4 * slot + g, slot, g // 2 * P, g % 2).then_inc(glu_done, 1)
            pe.wait_ge(glu_free, 4 + 2 * N_GLU)
            norm(3)
            pe.wait_ge(rs_ready, 8)
            mlp(1, MLP1)

            pe.wait_ge(down_free[1], 4 + 16 * N_MLP // 2)
            for i in range(T // P // 2):
                for s in (0, 1):
                    for b in range(2):
                        pe.wait_ge(out_copied, 4 * i + 2 * s + b + 1)
                        for k in range(4):
                            last = pe.transpose(ps[:, 2 * s + b, k * P:(k + 1) * P],
                                                xT[:, 4 * b + k, (2 * i + s) * P:(2 * i + s + 1) * P], ident[:, :])
                        last.then_inc(out_turned, 1)

        @block.vector
        def _(dve):
            done = [0]

            def link(ins):
                done[0] += 1
                ins.then_inc(prep_chain, 1)
                dve.wait_ge(prep_chain, done[0])

            def ts(out_, in_, s1, s2, op0, op1=None):
                if op1 is None:
                    link(dve.tensor_scalar(out_, in_, s1, None, op0))
                else:
                    link(dve.tensor_scalar(out_, in_, s1, s2, op0, op1))

            def tt(out_, a, b, op):
                link(dve.tensor_tensor(out_, a, b, op))

            def stt(out_, a, s, b, op0, op1):
                link(dve.scalar_tensor_tensor(out=out_, in0=a, scalar=s, in1=b, op0=op0, op1=op1))

            row = lambda n: r32[:, n, :]
            A_RE, A_IM = row(0), row(1)
            OUT = [row(2 + n) for n in range(7)]
            AB_RE, AB_IM, S_RE, S_IM, PH_C, PH_S, DECAY = OUT
            dt, mag, t0, t1, t2, t3, t4, co, si = (row(9 + n) for n in range(9))

            def exp(dst, src, n, r, y, w):
                dst, src, n, r, y = (v[:, 0:w] for v in (dst, src, n, r, y))
                ts(src, src, 172.0, -172.0, ALU.min, ALU.max)
                ts(n, src, LOG2E, ROUND, ALU.mult, ALU.add)
                ts(n, n, ROUND, None, ALU.subtract)
                stt(r, n, -LN2[0], src, ALU.mult, ALU.add)
                stt(r, n, -LN2[1], r, ALU.mult, ALU.add)
                ts(y, r, EXP_POLY[0], None, ALU.mult)
                for c in EXP_POLY[1:] + (1.0,):
                    stt(y, y, c, r, ALU.add, ALU.mult)
                ts(y, y, 1.0, None, ALU.add)
                ts(r, n, 0.5, ROUND, ALU.mult, ALU.add)
                ts(r, r, ROUND, None, ALU.subtract)
                tt(n, n, r, ALU.subtract)
                ts(i32[:, 0, 0:w], r, 127.0, float(1 << 23), ALU.add, ALU.mult)
                ts(i32[:, 1, 0:w], n, 127.0, float(1 << 23), ALU.add, ALU.mult)
                tt(y, y, i32[:, 0, 0:w].bitcast(F32), ALU.mult)
                tt(dst, y, i32[:, 1, 0:w].bitcast(F32), ALU.mult)

            dve.wait_ge(ssm_in, 80)
            link(dve.tensor_copy(t4[:, 0:2], ldt[:, :]))
            exp(t3, t4, t0, t1, t2, 2)
            link(dve.tensor_copy(dt.rearrange("g (a p) -> g a p", a=2),
                                 t3[:, 0:2].unsqueeze(2).to_broadcast((GP, 2, NS))))
            tt(t4, dt, A_RE, ALU.mult)
            exp(mag, t4, t0, t1, t2, P)
            tt(t0, dt, A_IM, ALU.mult)
            ts(t1, t0, 1.0 / (2.0 * PI), ROUND, ALU.mult, ALU.add)
            ts(t1, t1, ROUND, None, ALU.subtract)
            for c in TWO_PI:
                stt(t0, t1, -c, t0, ALU.mult, ALU.add)
            ts(t0, t0, 0.25, None, ALU.mult)
            tt(t1, t0, t0, ALU.mult)
            ts(t2, t1, SIN_POLY[0], SIN_POLY[1], ALU.mult, ALU.add)
            tt(t2, t2, t1, ALU.mult)
            ts(t2, t2, SIN_POLY[2], None, ALU.add)
            tt(t2, t2, t1, ALU.mult)
            stt(si, t2, 1.0, t0, ALU.add, ALU.mult)
            ts(t2, t1, COS_POLY[0], COS_POLY[1], ALU.mult, ALU.add)
            tt(t2, t2, t1, ALU.mult)
            ts(t2, t2, COS_POLY[2], None, ALU.add)
            tt(t2, t2, t1, ALU.mult)
            stt(co, t2, -0.5, t1, ALU.add, ALU.mult)
            for _ in range(2):
                tt(t2, si, si, ALU.mult)
                stt(si, co, 1.0, si, ALU.add, ALU.mult)
                ts(si, si, 2.0, None, ALU.mult)
                ts(co, t2, -2.0, None, ALU.mult)
            ts(co, co, 1.0, None, ALU.add)
            tt(AB_RE, mag, co, ALU.mult)
            tt(AB_IM, mag, si, ALU.mult)
            ts(t0, AB_RE, 1.0, None, ALU.subtract)
            tt(t1, A_RE, A_RE, ALU.mult)
            tt(t2, A_IM, A_IM, ALU.mult)
            tt(t1, t1, t2, ALU.add)
            link(dve.reciprocal(t1, t1))
            tt(t2, t0, A_RE, ALU.mult)
            tt(t3, AB_IM, A_IM, ALU.mult)
            tt(t2, t2, t3, ALU.add)
            tt(S_RE, t2, t1, ALU.mult)
            tt(t2, AB_IM, A_RE, ALU.mult)
            tt(t3, t0, A_IM, ALU.mult)
            tt(t2, t2, t3, ALU.subtract)
            tt(S_IM, t2, t1, ALU.mult)
            for n in range(3):
                tt(DECAY if n == 2 else t4, mag if n == 0 else t4, mag if n == 0 else t4, ALU.mult)
            for n in range(3):
                c_, s_ = (co, si) if n == 0 else (PH_C, PH_S)
                tt(t0, c_, c_, ALU.mult)
                tt(t1, s_, s_, ALU.mult)
                tt(t2, c_, s_, ALU.mult)
                tt(PH_C, t0, t1, ALU.subtract)
                if n < 2:
                    ts(PH_S, t2, 2.0, None, ALU.mult)
            dve.tensor_scalar(PH_S, t2, 2.0, None, ALU.mult).then_inc(par_ready, 1)

            dve.wait_ge(par_copied, 1)
            over_c = lambda n: ab[:, n, :].unsqueeze(2).to_broadcast((P, GP, GC))
            tmp = pt[:, 0, :].rearrange("p (g c) -> p g c", c=GC)
            tm2 = pt[:, 1, :].rearrange("p (g c) -> p g c", c=GC)

            def cmul(o_re, o_im, a_re, a_im, b_re, b_im, last=None):
                tt(tmp, a_im, b_im, ALU.mult)
                tt(o_re, a_re, b_re, ALU.mult)
                tt(o_re, o_re, tmp, ALU.subtract)
                tt(tmp, a_im, b_re, ALU.mult)
                tt(o_im, a_re, b_im, ALU.mult)
                ins = dve.tensor_tensor(o_im, o_im, tmp, ALU.add)
                if last is None:
                    link(ins)
                else:
                    ins.then_inc(last, 1)

            b_re, b_im = bc[:, 0, :, :], bc[:, 1, :, :]
            cmul(zr[:, :, L - 1, :], zi[:, :, L - 1, :], b_re, b_im, over_c(2), over_c(3), last=b_used)
            dve.wait_ge(b_used, 1)
            for r in range(L - 2, -1, -1):
                cmul(zr[:, :, r, :], zi[:, :, r, :], zr[:, :, r + 1, :], zi[:, :, r + 1, :], over_c(0), over_c(1),
                     last=z_ready if r == 0 else None)

            dve.wait_ge(k_copied, 2)
            dve.wait_ge(dm_ready, 1)
            dve.tensor_tensor(kall[96:P, :, :, :].rearrange("p g a c -> p (g a c)"),
                              kall[96:P, :, :, :].rearrange("p g a c -> p (g a c)"),
                              dm[96:P, :, :].rearrange("p g c -> p (g c)"), ALU.add).then_inc(k_ready, 1)
            dve.wait_ge(k_ready, 1)

            for s in range(L):
                c_re, c_ni = (bc[:, 0, :, :], bc[:, 1, :, :]) if s == 0 else (zr[:, :, s - 1, :], zi[:, :, s - 1, :])
                tt(tmp, c_ni, over_c(1), ALU.mult)
                tt(zr[:, :, s, :], c_re, over_c(0), ALU.mult)
                tt(zr[:, :, s, :], zr[:, :, s, :], tmp, ALU.add)
                tt(tmp, c_re, over_c(1), ALU.mult)
                tt(zi[:, :, s, :], c_ni, over_c(0), ALU.mult)
                ins = dve.tensor_tensor(zi[:, :, s, :], zi[:, :, s, :], tmp, ALU.subtract)
                if s < L - 1:
                    link(ins)
                else:
                    ins.then_inc(wo_ready, 1)

            dve.wait_ge(wo_out, 32)
            e_re = zr[:, :, :, :].rearrange("p g s c -> p g (s c)")
            e_im = zi[:, :, :, :].rearrange("p g s c -> p g (s c)")
            link(dve.memset(e_re[:, :, 0:1], 1.0))
            link(dve.memset(e_im[:, :, 0:1], 0.0))
            for n in range(7):
                m = 1 << n
                if n > 0:
                    tt(ab[:, 7, :], ab[:, 4, :], ab[:, 4, :], ALU.mult)
                    tt(ab[:, 8, :], ab[:, 5, :], ab[:, 5, :], ALU.mult)
                    tt(ab[:, 9, :], ab[:, 4, :], ab[:, 5, :], ALU.mult)
                    tt(ab[:, 4, :], ab[:, 7, :], ab[:, 8, :], ALU.subtract)
                    ts(ab[:, 5, :], ab[:, 9, :], 2.0, None, ALU.mult)
                pairs = min(GP, 2 * GP * GC // m)
                for g0 in range(0, GP, pairs):
                    gs = slice(g0, g0 + pairs)
                    c_ = ab[:, 4, gs].unsqueeze(2).to_broadcast((P, pairs, m))
                    s_ = ab[:, 5, gs].unsqueeze(2).to_broadcast((P, pairs, m))
                    tp = pt[:, :, :].rearrange("p a b -> p (a b)")[:, 0:pairs * m].rearrange("p (g j) -> p g j", j=m)
                    old_re, old_im = e_re[:, gs, 0:m], e_im[:, gs, 0:m]
                    new_re, new_im = e_re[:, gs, m:2 * m], e_im[:, gs, m:2 * m]
                    tt(tp, old_im, s_, ALU.mult)
                    tt(new_re, old_re, c_, ALU.mult)
                    tt(new_re, new_re, tp, ALU.subtract)
                    tt(tp, old_im, c_, ALU.mult)
                    tt(new_im, old_re, s_, ALU.mult)
                    ins = dve.tensor_tensor(new_im, new_im, tp, ALU.add)
                    if n == 6 and g0 + pairs == GP:
                        ins.then_inc(cs_ready, 1)
                    else:
                        link(ins)

            def lo_of(slot, m):
                dve.wait_ge(hi_ready, 2 * m + slot + 1)
                dve.tensor_tensor(w_lo[:, slot, :], raw[:, slot, :], w_hi[:, slot, :].bitcast(F32), ALU.subtract)\
                    .then_inc(lo_ready, 1)

            def norm(n, gain, chunked=False):
                dve.wait_ge(rs_ready, 2 * n + 2)
                dve.reciprocal(rinv[:, :], rs[:, :]).then_inc(rinv_ready, 1)
                dve.wait_ge(rinv_ready, n + 1)
                for k in range(KT):
                    if k >= 2:
                        dve.wait_ge(alo_ready, KT * n + k - 1)
                    dst, src, inv = hf[:, k % 2, :], xT[:, k, :], rinv[:, :]
                    if chunked:
                        dst = dst.rearrange("p (s j) -> p s j", s=L)
                        src = src.rearrange("p (j s) -> p s j", s=L)
                        inv = inv.rearrange("p (j s) -> p s j", s=L)
                    dve.scalar_tensor_tensor(out=dst, in0=src, scalar=gains[:, gain, k:k + 1], in1=inv,
                                             op0=ALU.mult, op1=ALU.mult).then_inc(hf_ready, 1)

            dve.wait_ge(cs_out, 32)
            dve.wait_ge(small_in, 16 * 9)
            norm(0, 0)
            ts(qk_gain[:, 0:4], qk_g[:, 0:1].to_broadcast((P, 4)), HD ** -0.5, None, ALU.mult)
            link(dve.tensor_copy(qk_gain[:, 4:8], qk_g[:, 1:2].to_broadcast((P, 4))))
            lo_of(0, 0)

            dve.wait_ge(alo_ready, KT)
            dve.sem_inc(qk_free, 4)
            with dve.Fori(0, N_QK // 2) as i:
                for slot in range(2):
                    lo_of(1 - slot, i + slot)
                    for g in range(4):
                        n = 4 * slot + g
                        dve.wait_ge(qk_root, 8 * i + n + 1)
                        dve.reciprocal(rih[:, g % 2, :], rsh[:, g, :]).then_inc(qk_inv, 1)
                        dve.wait_ge(qk_inv, 8 * i + n + 1)
                        dve.wait_ge(stg_out[g % 2], 16 * (4 * i + n // 2))
                        dve.scalar_tensor_tensor(out=stg[:, g % 2, :], in0=ps[:, g, :],
                                                 scalar=qk_gain[:, bass.ds(2 * i + slot, 1)], in1=rih[:, g % 2, :],
                                                 op0=ALU.mult, op1=ALU.mult).then_inc(qk_free, 1)
            dve.sem_inc(v_copied_d, 2)
            for i in range(N_V // 2):
                for slot in range(2):
                    if i + slot < N_V // 2:
                        lo_of(1 - slot, N_QK // 2 + i + slot)
                    for t in range(1, KT, 2):
                        dve.wait_ge(v_done, 16 * i + 8 * slot + t + 1)
                        if i + slot + t > 1:
                            dve.wait_ge(vst_out[1], 16 * (8 * i + 4 * slot + t // 2))
                        dve.tensor_copy(vst[:, 1, :], ps[:, t % 4, 0:PW]).then_inc(v_copied_d, 1)
            dve.memset(wf_hi[:, :, NH:P].bitcast(F32), 0.0).then_inc(f_zero, 1)
            dve.memset(wf_lo[:, :, NH:P].bitcast(F32), 0.0).then_inc(f_zero, 1)
            dve.memset(fone[:, :], 1.0).then_inc(f_zero, 1)
            dve.wait_ge(f_hi, 1)
            dve.tensor_tensor(wf_lo[:, :, 0:NH], wf[:, :, :], wf_hi[:, :, 0:NH].bitcast(F32), ALU.subtract)\
                .then_inc(f_lo, 1)
            dve.wait_ge(f_act, 4)
            dve.tensor_scalar(fy[:, :], fy[:, :], 0.0, None, ALU.min).then_inc(f_min, 1)
            dve.wait_ge(f_min, 1)
            dve.tensor_tensor(fy[:, :], fy[:, :], fe[:, :], ALU.subtract).then_inc(f_min, 1)
            dve.wait_ge(f_min, 2)
            dve.wait_ge(f_zero, 3)
            dve.tensor_tensor_scan(fc[:, :], fone[:, :], fy[:, :], 0.0, ALU.mult, ALU.add).then_inc(f_min, 2)

            dve.wait_ge(v_done, KT * N_V)
            for h in range(2):
                pad = slice((1 - h) * HD, (2 - h) * HD)
                dve.memset(v_hi[:, h, :, pad].bitcast(F32), 1.0).then_inc(v_pad, 1)
                dve.memset(v_lo[:, h, :, pad].bitcast(F32), 0.0).then_inc(v_pad, 1)
            dve.sem_inc(s_free, 2)
            dve.sem_inc(ptl_ready, 2)
            dve.sem_inc(o_free, 2)
            order = attention_order()
            with dve.Fori(0, PAIRS) as p:
                for n, (d_, r_, h_) in enumerate((
                        (q_lo, q_raw, q_hi), (k_lo, k_raw, k_hi),
                        (v_lo[:, 0, :, 0:HD], v_raw[:, :, 0:HD], v_hi[:, 0, :, 0:HD]),
                        (v_lo[:, 1, :, HD:P], v_raw[:, :, HD:P], v_hi[:, 1, :, HD:P]))):
                    dve.wait_ge(qkv_hi, 4 * p + n + 1)
                    dve.tensor_tensor(d_, r_, h_.bitcast(F32), ALU.subtract).then_inc(qkv_lo, 1)

                def output(u):
                    h, g = u // 2, u % 2
                    rows, sums = slice(h * HD, (h + 1) * HD), slice((1 - h) * HD, (2 - h) * HD)
                    dve.wait_ge(pv_done, 24 * p + TILES_BEFORE[u + 1] + 2)
                    dve.reciprocal(o_r[rows, :], ps[sums, 6 + g, :]).then_inc(o_inv, 1)
                    dve.wait_ge(o_inv, 4 * p + u + 1)
                    dve.tensor_tensor(o_f[rows, :], ps[rows, 6 + g, :], o_r[rows, :], ALU.mult).then_inc(o_free, 1)
                    dve.wait_ge(ohi_ready, 4 * p + u + 1)
                    tok = slice(g * HALF, (g + 1) * HALF)
                    dve.tensor_tensor(act_lo[rows, bass.ds(p, 1), tok].squeeze(1), o_f[rows, :],
                                      act_hi[rows, bass.ds(p, 1), tok].squeeze(1).bitcast(F32), ALU.subtract)\
                        .then_inc(olo_ready, 1)

                for kind, u, n in order:
                    if kind == "S":
                        b = 4 * u + n
                        keys = (4 * (u % 2) + n + 1) * P
                        dve.wait_ge(s_done, 16 * p + b + 1)
                        dve.wait_ge(c_in, 32 * p + 32)
                        dve.wait_ge(pv_done, 24 * p + TILES_BEFORE[max(u - 1, 0)] + 2)
                        dve.memset(tick[:, :], 0.0)
                        dve.tensor_tensor_reduce(
                            prob[:, u % 2, n, 0:keys], ps[:, 2 * (b % 2):2 * (b % 2) + 2, :]
                            .rearrange("p b k -> p (b k)")[:, 0:keys], cb[:, u // 2, 0:keys], 1.0, -3e38,
                            ALU.subtract, ALU.max, mx[:, b, 0:1]).then_inc(s_free, 1)
                        dve.wait_ge(s_free, 16 * p + b + 1 + 2)
                        dve.tensor_scalar(mx[:, b, 1:2], mx[:, b, 0:1], -1.0, None, ALU.mult)\
                            .then_inc(nm_ready, 1)
                    else:
                        jj = TILES_BEFORE[u] + n
                        lo = max(0, n - 4 * (u % 2)) * P
                        dve.wait_ge(pth_ready, 24 * p + jj + 1)
                        dve.wait_ge(pv_done, 24 * p + jj + 1)
                        dve.tensor_tensor(pt_lo[:, jj % 2, lo:HALF], ps[:, 4 + jj % 2, lo:HALF],
                                          pt_hi[:, jj % 2, lo:HALF].bitcast(F32), ALU.subtract)\
                            .then_inc(ptl_ready, 1)
                        if n == 0 and u > 0:
                            output(u - 1)
                output(3)

            lo_of(0, OUT0 // 2)

            def added(done_, free, tile, g, bank, tok, n):
                dve.wait_ge(done_, n + 1)
                dve.wait_ge(free, n + 1)
                dst = xT[:, bass.ds(tile, 1), tok].squeeze(1) if not isinstance(tile, int) else xT[:, tile, tok]
                dve.tensor_tensor(dst, ps[:, bank, :], dst, ALU.add).then_inc(free, 1)

            dve.sem_inc(oproj_free, 4)
            with dve.Fori(0, N_OUT // 2) as i:
                for slot in range(2):
                    lo_of(1 - slot, i + (OUT0 // 2 + slot))
                    for g in range(4):
                        half = g % 2
                        added(oproj_done, oproj_free, 4 * i + (2 * slot + g // 2), g, g,
                              slice(half * HALF, (half + 1) * HALF), 8 * i + (4 * slot + g))
            dve.wait_ge(oproj_free, 4 + 4 * N_OUT)
            norm(1, 2)

            def mlp(layer, panel0, last):
                dve.sem_inc(down_free[layer], 4)

                def step(i, more):
                    lo_of(1, i + panel0 // 2)
                    for q in range(2 * KT):
                        half = q // KT
                        added(down_done[layer], down_free[layer], q % KT, q, 4 + q % 4,
                              slice(half * HALF, (half + 1) * HALF), 16 * i + q)
                        if q == 3 and more:
                            lo_of(0, i + (panel0 // 2 + 1))
                if last:
                    with dve.Fori(0, N_MLP // 2 - 1) as i:
                        step(i, True)
                    step(N_MLP // 2 - 1, False)
                else:
                    with dve.Fori(0, N_MLP // 2) as i:
                        step(i, True)
                dve.wait_ge(down_free[layer], 4 + 16 * N_MLP // 2)

            mlp(0, MLP0, last=False)
            norm(2, 1, chunked=True)
            with dve.Fori(0, N_SIN // 2) as i:
                for slot in range(2):
                    lo_of(1 - slot, i + (SIN0 // 2 + slot))

            with dve.Fori(0, BLK) as q:
                made = [0]
                STEPS = 12

                def step(ins):
                    made[0] += 1
                    ins.then_inc(scan_chain, 1)
                    dve.wait_ge(scan_chain, STEPS * q + made[0])

                c_, s_ = (cs[:, n, :, :].rearrange("p g j -> p (g j)") for n in range(2))
                v_re, v_im = ps[:, 0, :], ps[:, 1, :]
                w_re, w_im, z_re, z_im = (vb[:, n, :, :].rearrange("p g j -> p (g j)") for n in range(4))
                x_re, x_im = (xb[:, n, :, :].rearrange("p g j -> p (g j)") for n in range(2))
                d_ = decay[:, :, :].rearrange("p g j -> p (g j)")
                dve.wait_ge(drive_done, q + 1)
                dve.wait_ge(y_done, 2 * q)
                step(dve.tensor_tensor(w_re, v_re, c_, ALU.mult))
                step(dve.tensor_tensor(z_re, v_im, s_, ALU.mult))
                step(dve.tensor_tensor(w_re, w_re, z_re, ALU.add))
                step(dve.tensor_tensor(w_im, v_im, c_, ALU.mult))
                step(dve.tensor_tensor(z_im, v_re, s_, ALU.mult))
                step(dve.tensor_tensor(w_im, w_im, z_im, ALU.subtract))
                dve.wait_ge(decay_ready, q + 1)
                step(dve.tensor_tensor_scan(z_re, d_, w_re, 0.0, ALU.mult, ALU.add))
                step(dve.tensor_tensor_scan(z_im, d_, w_im, 0.0, ALU.mult, ALU.add))
                step(dve.tensor_tensor(w_re, z_im, s_, ALU.mult))
                step(dve.tensor_tensor(x_re, z_re, c_, ALU.mult))
                step(dve.tensor_tensor(w_im, z_im, c_, ALU.mult))
                step(dve.tensor_tensor(x_im, z_re, s_, ALU.mult))
                dve.tensor_tensor(x_re, x_re, w_re, ALU.subtract).then_inc(state_ready, 1)
                dve.tensor_tensor(x_im, x_im, w_im, ALU.add).then_inc(state_ready, 1)
                dve.wait_ge(z_hi, q + 1)
                dve.tensor_tensor(act_lo[:, bass.ds(q, 1), :].squeeze(1), zt[:, :],
                                  act_hi[:, bass.ds(q, 1), :].squeeze(1).bitcast(F32), ALU.subtract)\
                    .then_inc(z_lo, 1)

            dve.sem_inc(glu_free, 4)
            with dve.Fori(0, N_GLU // 2) as i:
                for slot in range(2):
                    lo_of(1 - slot, i + (GLU0 // 2 + slot))
                for g in range(4):
                    m, half = g // 2, g % 2
                    n = 4 * i + g
                    dve.wait_ge(sig_ready, n + 1)
                    dve.wait_ge(glu_added, n)
                    dve.tensor_tensor(gated[:, half, :], ps[:, g, :], sig[:, g, :], ALU.mult).then_inc(glu_free, 1)
                    dve.wait_ge(glu_free, n + 1 + 4)
                    dst = xT[:, bass.ds(2 * i + m, 1), :].squeeze(1).rearrange("p (j s) -> p s j", s=L)\
                        [:, half * L // 2:(half + 1) * L // 2, :]
                    dve.tensor_tensor(dst, gated[:, half, :].rearrange("p (s j) -> p s j", j=NC), dst, ALU.add)\
                        .then_inc(glu_added, 1)
            dve.wait_ge(glu_added, 2 * N_GLU)
            norm(3, 3)
            mlp(1, MLP1, last=True)


INS = ["x", "norm_mix_g", "norm_mlp_g", "attn_w_in", "attn_b_f", "attn_q_g", "attn_k_g", "attn_w_out", "ssm_w_in",
       "ssm_a_re", "ssm_a_im", "ssm_b_re", "ssm_b_im", "ssm_c_re", "ssm_c_im", "ssm_log_dt", "ssm_d", "ssm_w_glu",
       "mlp_w1", "mlp_w2"]


def kernel(**inputs):
    import numpy as np
    import concourse.bacc as bacc
    from concourse.bass_utils import run_bass_kernel_spmd

    nc = bacc.Bacc("TRN2", target_bir_lowering=False, num_devices=1)
    arrays, args = {}, []
    for name in INS:
        a = np.ascontiguousarray(inputs[name])
        arrays[f"in_{name}"] = a
        args.append(nc.dram_tensor(f"in_{name}", a.shape, mybir.dt.from_np(a.dtype), kind="ExternalInput").ap())
    args.append(nc.dram_tensor("out_0", (1, T, D), F32, kind="ExternalOutput").ap())
    build(nc, *args)
    r = run_bass_kernel_spmd(nc, [arrays], core_ids=[0])
    return r.results[0]["out_0"]
```

```python
from contextlib import ExitStack

import concourse.bass as bass
from concourse import mybir

F32 = mybir.dt.float32
F32R = mybir.dt.float32r
I32 = mybir.dt.int32
ALU = mybir.AluOpType
ACT = mybir.ActivationFunctionType

P = 128
T = 1024
D = 1024
KT = D // P
HALF = 512
NH = 16
HD = D // NH
PAIRS = NH // 2
FF = 4096
EPS = 1e-6
PANEL = 2048
PW = PANEL // KT
NG = 64
GC = 16
NS = 64
L = 8
NC = T // L
GP = NG // 2
BLK = KT
GB = NG // BLK
PB = GP // BLK
MASKED = 1e30

N_QK, N_V = 8, 4
N_ATT = N_QK + N_V
N_OUT = D // PW
N_MLP = 2 * FF // PW
N_SIN = D // PW
N_GLU = 2 * D // PW
OUT0 = N_ATT
MLP0 = OUT0 + N_OUT
SIN0 = MLP0 + N_MLP
GLU0 = SIN0 + N_SIN
MLP1 = GLU0 + N_GLU
N_PANELS = MLP1 + N_MLP

TWO_PI = (6.28125, 0.0019354820251464844, -1.7484555314695172e-07)
LN2 = (0.693359375, -2.12194440e-4)
EXP_POLY = (1.9875691500e-4, 1.3981999507e-3, 8.3334519073e-3, 4.1665795894e-2, 1.6666665459e-1, 5.0000001201e-1)
SIN_POLY = (-1.9515295891e-4, 8.3321608736e-3, -1.6666654611e-1)
COS_POLY = (2.443315711809948e-5, -1.388731625493765e-3, 4.166664568298827e-2)
LOG2E = 1.4426950408889634
PI = 3.141592653589793
ROUND = 12582912.0


def attention_order(first=False, last=False):
    after = {t: [] for t in range(24)}
    for m, t in enumerate((0, 1, 3, 4)):
        after[t].append(("S", 2, m))
        after[t + 1].append(("E", 2, m))
        after[t + 8].append(("S", 3, m))
        after[t + 9].append(("E", 3, m))
    after[6].append(("R", 2, 0))
    after[14].append(("R", 3, 0))
    after[3].append(("V1", 0, 0))
    after[9].append(("O", 0, 0))
    if not first:
        after[1].append(("O", -1, 0))
    if not last:
        after[13].append(("QK", 0, 0))
        after[18].append(("V0", 0, 0))
        for m in range(4):
            after[16 + m // 2].append(("S", 4, m))
            after[17 + m // 2].append(("E", 4, m))
            after[18 + m].append(("S", 5, m))
            after[19 + m].append(("E", 5, m))
        after[19].append(("R", 4, 0))
        after[23].append(("R", 5, 0))
    order = []
    for u in range(4):
        for j in range(key_tiles(u)):
            t = TILES_BEFORE[u] + j
            order.append(("T", u, j))
            if t >= V_LAG or not first:
                order.append(("V", t - V_LAG, 0))
            order += after[t]
    if last:
        order += [("V", t, 0) for t in range(24 - V_LAG, 24)] + [("O", 1, 0)]
    return order


def attention_start():
    order = [("QK", 0, 0), ("V0", 0, 0)]
    for u in (0, 1):
        order += [(kind, u, m) for m in range(4) for kind in "SE"] + [("R", u, 0)]
    return order


def key_tiles(u):
    return 4 if u % 4 < 2 else 8


TILES_BEFORE = [0, 4, 8, 16, 24]
V_LAG = 2
T_SLOTS = 3
T_BANKS = (4, 5, 7)
V_BANK = 6


def build(nc, x, norm_mix_g, norm_mlp_g, attn_w_in, attn_b_f, attn_q_g, attn_k_g, attn_w_out, ssm_w_in,
          ssm_a_re, ssm_a_im, ssm_b_re, ssm_b_im, ssm_c_re, ssm_c_im, ssm_log_dt, ssm_d, ssm_w_glu,
          mlp_w1, mlp_w2, out):
    def scratch(name, shape, dt=F32):
        return nc.dram_tensor(name, shape, dt, kind="Internal").ap()

    qk_scr = scratch("qk_scr", (2 * D, T))
    v_scr = scratch("v_scr", (T, D))
    c_scr = scratch("c_scr", (NH, T))
    u_scr = scratch("u_scr", (P, NG * NC))
    y_scr = scratch("y_scr", (P, NG * NC))
    wst_scr = scratch("wst_scr", (2, P, GP * P))
    wo_scr = scratch("wo_scr", (2, P, GP * P))
    cs_scr = scratch("cs_scr", (2, P, GP * NC))
    kp_scr = scratch("kp_scr", (NG, GC, (2 * L - 1) * GC))
    tap_scr = scratch("tap_scr", (P, NG * P))

    ctx = ExitStack()
    with ctx:
        def sem(name):
            return ctx.enter_context(nc.semaphore(name))

        def sb(name, shape, dt=F32, stack=ctx):
            return stack.enter_context(nc.sbuf_tensor(name, shape, dt))

        ps = ctx.enter_context(nc.psum_tensor("ps", [P, 8, HALF], F32))

        xT = sb("xT", [P, KT, T])
        with ExitStack() as st:
            xs = sb("xs", [P, 2, D], stack=st)
            kall = sb("kall", [P, GP, 2, GC], stack=st)
            dm = sb("dm", [P, NG, GC], stack=st)
            ct = sb("ct", [P, 2, 4, P], stack=st)
            tst = sb("tst", [P, 2, 4 * P], stack=st)
            zero = sb("zero", [NG, (L - 1) * GC], stack=st)
        act_hi = sb("act_hi", [P, KT, T], F32R)
        act_lo = sb("act_lo", [P, KT, T], F32R)
        raw = sb("raw", [P, 2, PANEL])
        w_hi = sb("w_hi", [P, 2, PANEL], F32R)
        w_lo = sb("w_lo", [P, 2, PANEL], F32R)
        ident = sb("ident", [P, P])
        ones = sb("ones", [P, P])
        headsum = sb("headsum", [P, P])
        gains = sb("gains", [P, 4, KT])
        qk_g = sb("qk_g", [P, 2])
        qk_gain = sb("qk_gain", [P, N_QK])
        eps_t = sb("eps_t", [P, 1])
        fb = sb("fb", [NH, 1])
        ab = sb("ab", [P, 7, GP])
        mx = sb("mx", [P, 16])
        sums = sb("sums", [P, 16])
        inv_sums = sb("inv_sums", [P, 16])

        w_hi8 = w_hi[:, :, :].rearrange("p s (k f) -> p s k f", k=KT)
        w_lo8 = w_lo[:, :, :].rearrange("p s (k f) -> p s k f", k=KT)
        w_hi2 = w_hi[:, :, :].rearrange("p s (k f) -> p s k f", k=2)
        w_lo2 = w_lo[:, :, :].rearrange("p s (k f) -> p s k f", k=2)

        def phase():
            return ExitStack()

        with phase() as st:
            r32 = sb("r32", [GP, 22, P], stack=st)
            i32 = sb("i32", [GP, 2, P], I32, stack=st)
            ldt = sb("ldt", [GP, 2], stack=st)
            zr = sb("zr", [P, GP, L, GC], stack=st)
            zi = sb("zi", [P, GP, L, GC], stack=st)
            pt = sb("pt", [P, 2, GP * GC], stack=st)
            sq_t = sb("sq_t", [P, 3, GP], stack=st)
            bc = sb("bc", [P, 2, GP, GC], stack=st)
        with phase() as st:
            os_ = sb("os", [P, 2, D], stack=st)
        with phase() as st:
            sq = sb("sq", [P, 2, T], stack=st)
            rs = sb("rs", [P, T], stack=st)
            rinv = sb("rinv", [P, T], stack=st)
            hf = sb("hf", [P, 2, T], stack=st)
        with phase() as st:
            sqh = sb("sqh", [P, 4, HALF], stack=st)
            rsh = sb("rsh", [P, 4, HALF], stack=st)
            rih = sb("rih", [P, 2, HALF], stack=st)
            stg = sb("stg", [P, 2, HALF], stack=st)
            vst = sb("vst", [P, 2, PW], stack=st)
            wf = sb("wf", [P, KT, NH], stack=st)
            wf_hi = sb("wf_hi", [P, KT, P], F32R, stack=st)
            wf_lo = sb("wf_lo", [P, KT, P], F32R, stack=st)
            fy = sb("fy", [NH, T], stack=st)
            fe = sb("fe", [NH, T], stack=st)
            fl = sb("fl", [NH, T], stack=st)
            fc = sb("fc", [NH, T], stack=st)
            fone = sb("fone", [NH, T], stack=st)
        with phase() as st:
            prob = sb("prob", [P, 2, 4, T], stack=st)
            diag = sb("diag", [P, 4, 4, P], stack=st)
            pt_hi = sb("pt_hi", [P, T_SLOTS, HALF], F32R, stack=st)
            pt_lo = sb("pt_lo", [P, T_SLOTS, HALF], F32R, stack=st)
            cb = sb("cb", [P, 2, T], stack=st)
            mask = sb("mask", [P, P], F32R, stack=st)
            ident_r = sb("ident_r", [P, P], F32R, stack=st)
            mask_f = diag[:, 0, 0, :]
            tick = sb("tick", [P, 8], stack=st)
        with phase() as st:
            hid_hi = sb("hid_hi", [P, 2, T], F32R, stack=st)
            hid_lo = sb("hid_lo", [P, 2, T], F32R, stack=st)
            relu = sb("relu", [P, 4, HALF], stack=st)
            hsq = sb("hsq", [P, 4, HALF], stack=st)
        with phase() as st:
            wst = sb("wst", [P, 2, 2, PB * P], stack=st)
            wo = sb("wo", [P, 2, 2, PB * P], stack=st)
            cs = sb("cs", [P, 2, 2, PB * NC], stack=st)
            tap = sb("tap", [P, 2, GB * P], stack=st)
            ub = sb("ub", [P, 2, GB, NC], stack=st)
            decay = sb("decay", [P, PB, NC], stack=st)
            vb = sb("vb", [P, 3, PB * NC], stack=st)
            xb = sb("xb", [P, 2, PB * NC], stack=st)
            yb = sb("yb", [P, GB, NC], stack=st)
            zt = sb("zt", [P, T], stack=st)
            ust = vb[:, 0:2, :]
        with phase() as st:
            sig = sb("sig", [P, 4, HALF], stack=st)
            gated = sb("gated", [P, 2, HALF], stack=st)

        q_raw, k_raw = raw[:, 0, 0:T], raw[:, 0, T:2 * T]
        v_raw = raw[:, 1, 0:T].rearrange("p (j f) -> p j f", j=KT)
        q_hi, k_hi = w_hi[:, 0, 0:T], w_hi[:, 0, T:2 * T]
        q_lo, k_lo = w_lo[:, 0, 0:T], w_lo[:, 0, T:2 * T]
        v_hi = w_hi[:, 1, :].rearrange("p (h j f) -> p h j f", h=2, j=KT)
        v_lo = w_lo[:, 1, :].rearrange("p (h j f) -> p h j f", h=2, j=KT)

        START = lambda a, b: b
        FIRST = lambda a, b: b
        LAST = lambda a, b: (PAIRS - 1) * a + b

        def inner(i, parity):
            return lambda a, b: i * (2 * a) + ((2 - parity) * a + b)

        def keys_of(u, n):
            return (4 * (u % 4 // 2) + n + 1) * P

        def first_col(u, j):
            return max(0, j - 4 * (u // 2)) * P

        def prob_of(u, parity):
            if u in (2, 4, 5):
                parity = 1 - parity
            if u in (2, 3):
                return prob[:, parity, :, :]
            return prob[:, parity, :, :].rearrange("p m (h k) -> p h m k", h=2)[:, u % 2]

        def output_of(buf, g, pair):
            tok = slice(0, HALF) if g == 0 else slice(HALF, T)
            n = pair(1, -1 if g < 0 else 0)
            return buf[:, n, tok] if isinstance(n, int) else buf[:, bass.ds(n, 1), tok].squeeze(1)

        raw_in = [sem("raw_in0"), sem("raw_in1")]
        hi_ready = sem("hi_ready")
        lo_ready = sem("lo_ready")
        const_chain = sem("const_chain")
        const_ready = sem("const_ready")
        small_in = sem("small_in")
        ssm_in = sem("ssm_in")
        ct_in = sem("ct_in")
        dm_in = sem("dm_in")
        dm_ready = sem("dm_ready")
        prep_chain = sem("prep_chain")
        par_ready = sem("par_ready")
        par_turned = sem("par_turned")
        par_copied = sem("par_copied")
        b_used = sem("b_used")
        z_ready = sem("z_ready")
        c_turned = sem("c_turned")
        c_copied = sem("c_copied")
        z_turned = sem("z_turned")
        z_copied = sem("z_copied")
        tst_out = [sem("tst_out0"), sem("tst_out1")]
        k_done = sem("k_done")
        k_copied = sem("k_copied")
        k_ready = sem("k_ready")
        k_out = sem("k_out")
        wo_ready = sem("wo_ready")
        wo_out = sem("wo_out")
        cs_ready = sem("cs_ready")
        cs_out = sem("cs_out")
        x_in = [sem("x_in0"), sem("x_in1")]
        x_turned = sem("x_turned")
        x_copied = sem("x_copied")
        sq_ready = sem("sq_ready")
        sq_added = sem("sq_added")
        rs_ready = sem("rs_ready")
        rinv_ready = sem("rinv_ready")
        hf_ready = sem("hf_ready")
        ahi_ready = sem("ahi_ready")
        alo_ready = sem("alo_ready")
        qk_done = sem("qk_done")
        qk_sq = sem("qk_sq")
        qk_sum = sem("qk_sum")
        qk_root = sem("qk_root")
        qk_inv = sem("qk_inv")
        qk_free = sem("qk_free")
        stg_out = [sem("stg_out0"), sem("stg_out1")]
        v_done = sem("v_done")
        v_copied_a = sem("v_copied_a")
        v_copied_d = sem("v_copied_d")
        vst_out = [sem("vst_out0"), sem("vst_out1")]
        f_w = sem("f_w")
        f_zero = sem("f_zero")
        f_hi = sem("f_hi")
        f_lo = sem("f_lo")
        f_done = sem("f_done")
        f_act = sem("f_act")
        f_min = sem("f_min")
        c_out = sem("c_out")
        v_pad = sem("v_pad")
        mask_ready = sem("mask_ready")
        mask_chain = sem("mask_chain")
        mask_hi = sem("mask_hi")
        qk_in = sem("qk_in")
        v_in = sem("v_in")
        c_in = [sem("c_in0"), sem("c_in1")]
        qk_hi = sem("qk_hi")
        qk_lo = sem("qk_lo")
        v_hi_ready = sem("v_hi_ready")
        v_lo_ready = sem("v_lo_ready")
        s_done = sem("s_done")
        s_biased = sem("s_biased")
        p_ready = sem("p_ready")
        inv_ready = sem("inv_ready")
        diag_ready = sem("diag_ready")
        t_done = sem("t_done")
        pth_ready = sem("pth_ready")
        ptl_ready = sem("ptl_ready")
        pv_done = sem("pv_done")
        ohi_ready = sem("ohi_ready")
        olo_ready = sem("olo_ready")
        oproj_done = sem("oproj_done")
        oproj_free = sem("oproj_free")
        up_done = [sem("up_done0"), sem("up_done1")]
        up_free = [sem("up_free0"), sem("up_free1")]
        hsq_ready = [sem("hsq_ready0"), sem("hsq_ready1")]
        hidh_ready = [sem("hidh_ready0"), sem("hidh_ready1")]
        hidl_ready = [sem("hidl_ready0"), sem("hidl_ready1")]
        down_done = [sem("down_done0"), sem("down_done1")]
        down_free = [sem("down_free0"), sem("down_free1")]
        u_done = sem("u_done")
        u_free = sem("u_free")
        u_out = sem("u_out")
        decay_fill = sem("decay_fill")
        drive_in = [sem("drive_in0"), sem("drive_in1")]
        out_in = [sem("out_in0"), sem("out_in1")]
        tap_out = sem("tap_out")
        decay_ready = sem("decay_ready")
        drive_done = sem("drive_done")
        scan_chain = sem("scan_chain")
        state_ready = sem("state_ready")
        y_done = sem("y_done")
        gelu_done = sem("gelu_done")
        y_out = sem("y_out")
        z_in = sem("z_in")
        z_hi = sem("z_hi")
        z_lo = sem("z_lo")
        glu_done = sem("glu_done")
        sig_ready = sem("sig_ready")
        glu_free = sem("glu_free")
        glu_added = sem("glu_added")
        out_turned = sem("out_turned")
        out_copied = sem("out_copied")
        y_stored = [sem("y_stored0"), sem("y_stored1")]

        block = ctx.enter_context(nc.Block())

        x_rows = x.rearrange("b t d -> (b t) d")
        out_rows = out.rearrange("b t d -> (b t) d")

        def cols(w, c0):
            return w.rearrange("(k p) f -> p k f", p=P)[:, :, bass.ds(c0, PW)]

        w_in, w_out_, w_sin, w_glu = attn_w_in[0], attn_w_out[0], ssm_w_in[0], ssm_w_glu[0]

        @block.sync
        def _(sp):
            def load(slot, m, src, first=False):
                if not first:
                    sp.wait_ge(lo_ready, 2 * m + slot - 1)
                dst = raw[:, slot, :]
                if len(src.shape) == 3:
                    dst = dst.rearrange("p (k f) -> p k f", k=src.shape[1])
                elif len(src.shape) == 4:
                    dst = dst.rearrange("p (k a f) -> p k a f", k=src.shape[1], a=src.shape[2])
                sp.dma_start(dst, src).then_inc(raw_in[slot], 16)

            load(0, 0, cols(w_in, 0), first=True)
            load(1, 0, cols(w_in, PW), first=True)
            with sp.Fori(1, N_ATT // 2) as m:
                load(0, m, cols(w_in, m * (2 * PW)))
                load(1, m, cols(w_in, m * (2 * PW) + PW))

            sp.wait_ge(k_out, 16 * (L + 1))
            for s in range(L):
                sp.dma_start(tap_scr.rearrange("p (g w) -> p g w", w=P)[GC * s:GC * s + GC],
                             kp_scr[:, :, (L - 1 - s) * GC:(2 * L - 1 - s) * GC].rearrange("g c w -> c g w"))\
                    .then_inc(tap_out, 16)

            sp.wait_ge(lo_ready, N_ATT)
            for s in (0, 1):
                sp.wait_ge(stg_out[s], 16 * N_QK * 2)
                sp.wait_ge(vst_out[s], 16 * N_V * 4)
            sp.wait_ge(c_out, 16)

            def load_qk(p):
                sp.dma_start(q_raw, qk_scr[bass.ds(p * P, P), :]).then_inc(qk_in, 16)
                sp.dma_start(k_raw, qk_scr[bass.ds(p * P + D, P), :]).then_inc(qk_in, 16)

            def load_v(p):
                sp.dma_start(v_raw, v_scr.rearrange("(j k) f -> k j f", k=P)[:, :, bass.ds(p * P, P)])\
                    .then_inc(v_in, 16)

            def load_c(p, h):
                sp.dma_start(cb[:, h, :], c_scr[bass.ds(p * 2 + h, 1), :].to_broadcast((P, T)))\
                    .then_inc(c_in[h], 16)

            load_qk(0)
            load_v(0)
            load_c(0, 0)
            load_c(0, 1)
            with sp.Fori(1, PAIRS) as p:
                sp.wait_ge(qk_lo, 2 * p)
                sp.wait_ge(v_lo_ready, 2 * p)
                load_qk(p)
                load_v(p)
                for h in range(2):
                    sp.wait_ge(s_biased, 16 * p + (4 * h - 2))
                    load_c(p, h)
            sp.wait_ge(v_lo_ready, 2 * PAIRS)

            load(0, OUT0 // 2, cols(w_out_, 0))
            load(1, OUT0 // 2, cols(w_out_, PW))
            with sp.Fori(1, N_OUT // 2) as i:
                load(0, i + OUT0 // 2, cols(w_out_, i * (2 * PW)))
                load(1, i + OUT0 // 2, cols(w_out_, i * (2 * PW) + PW))

            def mlp_loads(layer, n0):
                with sp.Fori(0, N_MLP // 2) as i:
                    load(0, i + n0 // 2, cols(mlp_w1[layer], i * PW))
                    load(1, i + n0 // 2,
                         mlp_w2[layer].rearrange("(i k p) f -> i p k f", k=2, p=P)[bass.ds(i, 1)].squeeze(0))

            mlp_loads(0, MLP0)
            with sp.Fori(0, N_SIN // 2) as i:
                load(0, i + SIN0 // 2, cols(w_sin, i * (2 * PW)))
                load(1, i + SIN0 // 2, cols(w_sin, i * (2 * PW) + PW))

            def glu_load(slot, i):
                load(slot, i + GLU0 // 2, cols(w_glu, i * PW + slot * D))

            glu_load(0, 0)
            glu_load(1, 0)

            for s in (0, 1):
                sp.wait_ge(tst_out[s], 16 * GP // 4)
            sp.wait_ge(tap_out, 16 * L)
            sp.wait_ge(wo_out, 32)
            sp.wait_ge(cs_out, 32)

            def load_block(q, s):
                def load(buf, scr, done):
                    sp.dma_start(buf[:, s, :, :], scr.rearrange("a p f -> p a f")[:, :, bass.ds(q * (PB * P), PB * P)])\
                        .then_inc(done, 16)

                sp.dma_start(ub[:, s, :, :].rearrange("p g j -> p (g j)"), u_scr[:, bass.ds(q * (GB * NC), GB * NC)])\
                    .then_inc(drive_in[s], 16)
                load(wst, wst_scr, drive_in[s])
                load(cs, cs_scr, out_in[s])
                load(wo, wo_scr, out_in[s])
                sp.dma_start(tap[:, s, :], tap_scr[:, bass.ds(q * (GB * P), GB * P)]).then_inc(out_in[s], 16)

            def load_z(q):
                sp.wait_ge(y_out, 16 * q + 16)
                sp.wait_ge(z_lo, q + 1)
                for g in range(GB):
                    sp.dma_start(zt[g * GC:(g + 1) * GC, :].rearrange("c (s j) -> c s j", s=L),
                                 y_scr.rearrange("(s c) (g j) -> g c s j", c=GC, j=NC)[bass.ds(q * GB + g, 1)].squeeze(0))\
                        .then_inc(z_in, 16)

            sp.wait_ge(u_out, 16 * GB * KT)
            load_block(0, 0)
            load_block(1, 1)
            def next_block(q, s):
                sp.wait_ge(y_done, 2 * q + (2 + 2))
                load_block(q + 2, s)

            next_block(0, 0)
            with sp.Fori(0, BLK // 2 - 2) as i:
                for s in (1, 0):
                    next_block(2 * i + (2 - s), s)
                    load_z(2 * i + (1 - s))
            next_block(BLK - 3, 1)
            for q in range(BLK - 4, BLK):
                load_z(q)

            with sp.Fori(1, N_GLU // 2) as i:
                glu_load(0, i)
                glu_load(1, i)
            mlp_loads(1, MLP1)

            with sp.Fori(0, T // P // 2) as i:
                for s in (0, 1):
                    sp.wait_ge(out_copied, 4 * i + 2 * s + 2 + 4)
                    sp.dma_start(out_rows[bass.ds(i * (2 * P) + s * P, P), :], os_[:, s, :])\
                        .then_inc(y_stored[s], 16)
            for s in (0, 1):
                sp.wait_ge(y_stored[s], 16 * T // P // 2)

        @block.gpsimd
        def _(pool):
            pool.dma_start(ldt[:, :], ssm_log_dt[0].rearrange("(g a) -> g a", a=2)).then_inc(ssm_in, 16)
            pool.dma_start(r32[:, 0, :], ssm_a_re[0].rearrange("(g a) p -> g (a p)", a=2)).then_inc(ssm_in, 16)
            pool.dma_start(r32[:, 1, :], ssm_a_im[0].rearrange("(g a) p -> g (a p)", a=2)).then_inc(ssm_in, 16)
            for n, b in enumerate((ssm_b_re, ssm_b_im)):
                pool.dma_start(bc[:, n, :, :], b[0].rearrange("(g a) p c -> (a p) g c", a=2)).then_inc(ssm_in, 16)
            for s in (0, 1):
                pool.dma_start(xs[:, s, :], x_rows[s * P:(s + 1) * P, :]).then_inc(x_in[s], 16)

            def fill(ins, n):
                ins.then_inc(const_chain, 1)
                pool.wait_ge(const_chain, n)

            fill(pool.memset(ident[:, :], 0.0), 1)
            pool.affine_select(out=ident[:, :], in_=ident[:, :], compare_op=ALU.not_equal, fill=1.0, base=0,
                               pattern=[[-1, P]], channel_multiplier=1).then_inc(const_ready, 1)
            pool.memset(ones[:, :], 1.0).then_inc(const_ready, 1)
            fill(pool.memset(headsum[:, :], 0.0), 2)
            fill(pool.memset(zero[:, :], 0.0), 3)
            pool.memset(eps_t[:, :], EPS).then_inc(const_ready, 1)
            pool.memset(headsum[0:HD, 0:HD], 1.0).then_inc(const_ready, 1)
            pool.wait_ge(const_ready, 4)
            pool.memset(headsum[HD:P, HD:P], 1.0).then_inc(const_ready, 1)
            pool.wait_ge(const_ready, 5)
            with nc.allow_non_contiguous_dma(reason="gains of a few KB"):
                for n, g in enumerate((norm_mix_g[0], norm_mix_g[1], norm_mlp_g[0], norm_mlp_g[1])):
                    pool.dma_start(gains[:, n, :], g.rearrange("(k p) -> p k", p=P)).then_inc(small_in, 16)
                for n, g in enumerate((attn_q_g, attn_k_g)):
                    for h in range(2):
                        pool.dma_start(qk_g[h * HD:(h + 1) * HD, n:n + 1],
                                       g[0].rearrange("(p a) -> p a", a=1)).then_inc(small_in, 16)
                pool.dma_start(fb[:, :], attn_b_f[0].rearrange("(h a) -> h a", a=1)).then_inc(small_in, 16)
            for n, c in enumerate((ssm_c_re, ssm_c_im)):
                for t in range(4):
                    for a in range(2):
                        pool.dma_start(ct[:, n, t, a * NS:(a + 1) * NS],
                                       c[0].rearrange("(t g a) c p -> t a g c p", t=4, a=2)[t, a])\
                            .then_inc(ct_in, 16)
            pool.dma_start(dm[96:P, :, :], ssm_d[0].rearrange("(o g c) -> o g c", o=1, c=GC)
                           .to_broadcast((32, NG, GC))).then_inc(dm_in, 16)
            pool.dma_start(kp_scr[:, :, 0:(L - 1) * GC],
                           zero[:, :].unsqueeze(1).to_broadcast((NG, GC, (L - 1) * GC))).then_inc(k_out, 16)
            pool.wait_ge(dm_in, 16)
            pool.affine_select(out=dm[96:P, :, :], in_=dm[96:P, :, :], compare_op=ALU.is_equal, fill=0.0,
                               base=-GC, pattern=[[0, NG], [-1, GC]], channel_multiplier=1).then_inc(dm_ready, 1)

            with pool.Fori(0, T // P // 2 - 1) as i:
                for s in (0, 1):
                    pool.wait_ge(x_turned, 4 * i + 2 * s + 2)
                    pool.dma_start(xs[:, s, :], x_rows[bass.ds(i * (2 * P) + (2 + s) * P, P), :])\
                        .then_inc(x_in[s], 16)

            for a in range(2):
                for b in range(GP // 4):
                    n = a * (GP // 4) + b
                    pool.wait_ge(z_copied, n + 1)
                    pool.dma_start(wst_scr[a][:, b * 4 * P:(b + 1) * 4 * P], tst[:, n % 2, :])\
                        .then_inc(tst_out[n % 2], 16)
            pool.wait_ge(k_ready, 1)
            for r in range(L):
                row = 2 * L - 2 - r
                pool.dma_start(kp_scr[:, :, row * GC:(row + 1) * GC].rearrange("g c w -> c g w"),
                               kall[GC * r:GC * r + GC, :, :, :].rearrange("p g a c -> p (g a) c"))\
                    .then_inc(k_out, 16)
            pool.wait_ge(wo_ready, 1)
            pool.dma_start(wo_scr[0], zr[:, :, :, :].rearrange("p g s c -> p (g s c)")).then_inc(wo_out, 16)
            pool.dma_start(wo_scr[1], zi[:, :, :, :].rearrange("p g s c -> p (g s c)")).then_inc(wo_out, 16)
            pool.wait_ge(cs_ready, 1)
            pool.dma_start(cs_scr[0], zr[:, :, :, :].rearrange("p g s c -> p (g s c)")).then_inc(cs_out, 16)
            pool.dma_start(cs_scr[1], zi[:, :, :, :].rearrange("p g s c -> p (g s c)")).then_inc(cs_out, 16)

            def norm_lo(n):
                for k in range(KT):
                    pool.wait_ge(ahi_ready, KT * n + k + 1)
                    pool.tensor_tensor(act_lo[:, k, :], hf[:, k % 2, :], act_hi[:, k, :].bitcast(F32),
                                       ALU.subtract).then_inc(alo_ready, 1)

            norm_lo(0)
            pool.wait_ge(alo_ready, KT)
            pool.dma_start(wf[:, :, :], attn_w_in[0].rearrange("(k p) f -> p k f", p=P)[:, :, 3 * D:3 * D + NH])\
                .then_inc(f_w, 16)
            with pool.Fori(0, N_QK // 2) as i:
                for slot in range(2):
                    for g in range(4):
                        m, half = g // 2, g % 2
                        pool.wait_ge(qk_free, 8 * i + 4 * slot + g + 1 + 4)
                        pool.dma_start(qk_scr[bass.ds(i * (4 * P) + (2 * slot + m) * P, P),
                                              half * HALF:(half + 1) * HALF], stg[:, g % 2, :])\
                            .then_inc(stg_out[g % 2], 16)
            with pool.Fori(0, N_V // 2) as i:
                for slot in range(2):
                    for t in range(KT):
                        pool.wait_ge((v_copied_a, v_copied_d)[t % 2], 8 * i + 4 * slot + t // 2 + 1 + 2)
                        pool.dma_start(v_scr[t * P:(t + 1) * P, bass.ds(i * (2 * PW) + slot * PW, PW)],
                                       vst[:, t % 2, :]).then_inc(vst_out[t % 2], 16)
            pool.wait_ge(f_min, 4)
            pool.dma_start(c_scr, fc[:, :]).then_inc(c_out, 16)

            pool.wait_ge(c_out, 16)
            pool.memset(mask_f[:, :], 0.0).then_inc(mask_chain, 1)
            pool.wait_ge(mask_chain, 1)
            pool.affine_select(out=mask_f[:, :], in_=mask_f[:, :], compare_op=ALU.is_ge, fill=MASKED, base=0,
                               pattern=[[-1, P]], channel_multiplier=1).then_inc(mask_ready, 1)

            def diagonals(u, n):
                pool.wait_ge(inv_ready, n)
                pool.tensor_tensor(diag[:, u, :, :], ident[:, :].unsqueeze(1).to_broadcast((P, 4, P)),
                                   inv_sums[:, 4 * u:4 * u + 4].unsqueeze(2).to_broadcast((P, 4, P)), ALU.mult)\
                    .then_inc(diag_ready, 1)

            with pool.Fori(0, PAIRS) as p:
                for u in range(4):
                    diagonals(u, 4 * p + (u + 1))

            def mlp_hidden(layer):
                pool.sem_inc(hidl_ready[layer], 1)
                with pool.Fori(0, N_MLP // 2) as i:
                    for g in range(5):
                        if g < 4:
                            pool.wait_ge(up_free[layer], 4 * i + g + 1 + 4)
                            pool.tensor_tensor(hsq[:, g, :], relu[:, g, :], relu[:, g, :], ALU.mult)\
                                .then_inc(hsq_ready[layer], 1)
                        if g > 0:
                            m, half = (g - 1) % 2, (g - 1) // 2
                            pool.wait_ge(hidh_ready[layer], 4 * i + g)
                            part = slice(half * HALF, (half + 1) * HALF)
                            pool.tensor_tensor(hid_lo[:, m, part], hsq[:, g - 1, :],
                                               hid_hi[:, m, part].bitcast(F32), ALU.subtract)\
                                .then_inc(hidl_ready[layer], 1)

            norm_lo(1)
            mlp_hidden(0)
            norm_lo(2)

            with pool.Fori(0, N_SIN // 2) as i:
                for slot in range(2):
                    for m in range(2):
                        pool.wait_ge(u_free, 8 * i + (4 * slot + 2 * m + 2 + 4))
                        for g in range(GB):
                            pool.dma_start(
                                u_scr.rearrange("(s c) (g j) -> g c s j", c=GC, j=NC)
                                [bass.ds(i * (4 * GB) + ((2 * slot + m) * GB + g), 1)].squeeze(0),
                                ust[g * GC:(g + 1) * GC, :, :].rearrange("c h (s j) -> c (h s) j", j=NC))\
                                .then_inc(u_out, 16)

            def decay_of(q):
                pool.wait_ge(state_ready, 2 * q + 4)
                pool.tensor_copy(decay[:, :, 1:NC],
                                 ab[:, 6, bass.ds(q * PB, PB)].unsqueeze(2).to_broadcast((P, PB, NC - 1)))\
                    .then_inc(decay_ready, 1)

            def lo_of_z(q):
                pool.wait_ge(z_hi, q + 1)
                pool.tensor_tensor(act_lo[:, bass.ds(q, 1), :].squeeze(1), zt[:, :],
                                   act_hi[:, bass.ds(q, 1), :].squeeze(1).bitcast(F32), ALU.subtract)\
                    .then_inc(z_lo, 1)

            pool.memset(decay[:, :, 0:1], 0.0).then_inc(decay_fill, 1)
            pool.wait_ge(decay_fill, 1)
            pool.sem_inc(z_lo, 1)
            for q in range(4):
                decay_of(q)
            with pool.Fori(0, BLK - 4) as q:
                lo_of_z(q)
                decay_of(q + 4)
            for q in range(BLK - 4, BLK):
                lo_of_z(q)

            norm_lo(3)
            mlp_hidden(1)

        @block.scalar
        def _(act):
            def copy(dst, src):
                return act.activation(dst, src, ACT.Copy)

            def split_hi(slot, m):
                act.wait_ge(raw_in[slot], 16 * m + 16)
                copy(w_hi[:, slot, :], raw[:, slot, :]).then_inc(hi_ready, 1)

            act.sem_inc(x_copied, 4)
            with act.Fori(0, T // P // 2) as i:
                for s in (0, 1):
                    for b in range(2):
                        act.wait_ge(x_turned, 4 * i + 2 * s + b + 1)
                        copy(xT[:, 4 * b:4 * b + 4, bass.ds(i * (2 * P) + s * P, P)],
                             ps[:, 2 * s + b, :].rearrange("p (k t) -> p k t", k=4)).then_inc(x_copied, 1)
            act.wait_ge(par_turned, 1)
            copy(ab[:, 0:7, :], ps[:, 4, 0:7 * GP].rearrange("p (n g) -> p n g", g=GP)).then_inc(par_copied, 1)
            act.wait_ge(c_turned, 1)
            act.wait_ge(b_used, 1)
            copy(bc[:, 0, :, :], ps[:, 5, :].rearrange("p (g c) -> p g c", c=GC)).then_inc(c_copied, 1)
            act.activation(bc[:, 1, :, :], ps[:, 6, :].rearrange("p (g c) -> p g c", c=GC), ACT.Copy,
                           scale=-1.0).then_inc(c_copied, 1)
            for n in range(2 * GP // 4):
                act.wait_ge(z_turned, n + 1)
                if n >= 2:
                    act.wait_ge(tst_out[n % 2], 16 * (n // 2))
                copy(tst[:, n % 2, :], ps[:, (7, 4)[n % 2], :]).then_inc(z_copied, 1)
            act.wait_ge(k_done, 1)
            for a in range(2):
                copy(kall[:, :, a, :], ps[:, 5 + a, :].rearrange("p (g c) -> p g c", c=GC)).then_inc(k_copied, 1)

            def norm(n):
                for k in range(KT):
                    if k >= 2:
                        act.wait_ge(sq_added, KT * n + k - 1)
                    act.activation(sq[:, k % 2, :], xT[:, k, :], ACT.Square).then_inc(sq_ready, 1)
                act.wait_ge(sq_added, KT * n + KT)
                for half in range(2):
                    act.activation(rs[:, half * HALF:(half + 1) * HALF], ps[:, half, :], ACT.Sqrt,
                                   bias=eps_t[:, 0:1], scale=1.0 / D).then_inc(rs_ready, 1)
                for k in range(KT):
                    act.wait_ge(hf_ready, KT * n + k + 1)
                    copy(act_hi[:, k, :], hf[:, k % 2, :]).then_inc(ahi_ready, 1)

            for s in (0, 1):
                act.wait_ge(tst_out[s], 16 * GP // 4)
            act.wait_ge(k_out, 16 * (L + 1))
            act.wait_ge(wo_out, 32)
            act.wait_ge(cs_out, 32)
            act.wait_ge(const_ready, 5)
            act.wait_ge(small_in, 16 * 9)
            act.wait_ge(x_copied, 4 + 2 * KT)
            norm(0)
            split_hi(0, 0)

            act.wait_ge(alo_ready, KT)
            with act.Fori(0, N_QK // 2) as i:
                for slot in range(2):
                    split_hi(1 - slot, i + slot)
                    for g in range(5):
                        if g < 4:
                            act.wait_ge(qk_done, 8 * i + 4 * slot + g + 1)
                            act.activation(sqh[:, g, :], ps[:, g, :], ACT.Square).then_inc(qk_sq, 1)
                        if g > 0:
                            act.wait_ge(qk_sum, 8 * i + 4 * slot + g)
                            act.activation(rsh[:, g - 1, :], ps[:, 4 + g - 1, :], ACT.Sqrt,
                                           bias=eps_t[:, 0:1], scale=1.0 / HD).then_inc(qk_root, 1)
            act.sem_inc(v_copied_a, 2)
            for i in range(N_V // 2):
                for slot in range(2):
                    act.wait_ge(v_done, 16 * i + 8 * slot)
                    if i + slot < N_V // 2:
                        split_hi(1 - slot, N_QK // 2 + i + slot)
                    for t in range(0, KT, 2):
                        act.wait_ge(v_done, 16 * i + 8 * slot + t + 1)
                        if i + slot + t > 0:
                            act.wait_ge(vst_out[0], 16 * (8 * i + 4 * slot + t // 2))
                        copy(vst[:, 0, :], ps[:, t % 4, 0:PW]).then_inc(v_copied_a, 1)
            act.wait_ge(f_w, 16)
            act.wait_ge(f_zero, 2)
            copy(wf_hi[:, :, 0:NH], wf[:, :, :]).then_inc(f_hi, 1)
            act.wait_ge(f_done, 1)
            act.activation(fy[:, :].rearrange("p (h t) -> p h t", h=2), ps[0:NH, 0:2, :], ACT.Identity,
                           bias=fb[:, 0:1]).then_inc(f_act, 1)
            act.wait_ge(f_act, 1)
            act.activation(fe[:, :], fy[:, :], ACT.Abs).then_inc(f_act, 1)
            act.wait_ge(f_act, 2)
            act.activation(fl[:, :], fe[:, :], ACT.Exp, scale=-1.0).then_inc(f_act, 1)
            act.wait_ge(f_act, 3)
            act.activation(fe[:, :], fl[:, :], ACT.Ln, bias=1.0).then_inc(f_act, 1)

            act.wait_ge(mask_ready, 1)
            copy(mask[:, :], mask_f[:, :]).then_inc(mask_hi, 1)
            copy(ident_r[:, :], ident[:, :]).then_inc(mask_hi, 1)
            act.wait_ge(v_pad, 4)

            def attend(order, pair, parity):
                for kind, u, n in order:
                    if kind == "QK":
                        nxt = 0 if pair is START else 1
                        act.wait_ge(qk_in, pair(32, 32 * nxt + 32))
                        act.wait_ge(s_biased, pair(16, 16 * nxt + 2))
                        copy(q_hi, q_raw).then_inc(qk_hi, 1)
                        copy(k_hi, k_raw).then_inc(qk_hi, 1)
                    elif kind in ("V0", "V1"):
                        h = 0 if kind == "V0" else 1
                        nxt = 1 if h == 0 and pair is not START else 0
                        act.wait_ge(v_in, pair(16, 16 * nxt + 16))
                        act.wait_ge(pv_done, pair(24, (16 * nxt if h == 0 else 0) + T_SLOTS))
                        copy(v_hi[:, h, :, h * HD:(h + 1) * HD], v_raw[:, :, h * HD:(h + 1) * HD])\
                            .then_inc(v_hi_ready, 1)
                    elif kind == "E":
                        act.wait_ge(s_biased, pair(16, 4 * u + n + 1 + 2))
                        b = (4 * u + n) % 16
                        probs = prob_of(u, parity)[:, n, 0:keys_of(u, n)]
                        act.activation(probs, probs, ACT.Exp, bias=mx[:, b:b + 1], scale=-1.0,
                                       accum_out=sums[:, b:b + 1]).then_inc(p_ready, 1)
                    elif kind == "T":
                        t = TILES_BEFORE[u] + n
                        act.wait_ge(t_done, pair(24, t + 1))
                        act.wait_ge(pv_done, pair(24, t + 1))
                        copy(pt_hi[:, t % T_SLOTS, first_col(u, n):HALF], ps[:, T_BANKS[t % T_SLOTS],
                                                                            first_col(u, n):HALF])\
                            .then_inc(pth_ready, 1)
                    elif kind == "O":
                        act.wait_ge(pv_done, pair(24, (0, 8, 24)[u + 1] + T_SLOTS))
                        copy(output_of(act_hi, u, pair), ps[:, V_BANK, :]).then_inc(ohi_ready, 1)

            attend(attention_start(), START, 0)
            attend(attention_order(first=True), FIRST, 0)
            with act.Fori(0, PAIRS // 2 - 1) as i:
                for parity in (1, 0):
                    attend(attention_order(), inner(i, parity), parity)
            attend(attention_order(last=True), LAST, 1)

            act.wait_ge(pv_done, 24 * PAIRS + T_SLOTS)
            def proj_splits(panel0, count):
                with act.Fori(0, count // 2) as i:
                    act.wait_ge(oproj_done, 8 * i + 1)
                    split_hi(1, i + panel0 // 2)
                    act.wait_ge(oproj_done, 8 * i + 5)
                    split_hi(0, i + panel0 // 2 + 1)

            split_hi(0, OUT0 // 2)
            proj_splits(OUT0, N_OUT)

            def mlp(layer, panel0, last):
                act.sem_inc(up_free[layer], 4)

                def step(i, more):
                    act.wait_ge(down_done[layer], 16 * i + 1)
                    split_hi(1, i + panel0 // 2)
                    for g in range(5):
                        if g < 4:
                            act.wait_ge(up_done[layer], 4 * i + g + 1)
                            act.wait_ge(hidl_ready[layer], 4 * i + 1)
                            act.activation(relu[:, g, :], ps[:, g, :], ACT.Relu).then_inc(up_free[layer], 1)
                        if g > 0:
                            m, half = (g - 1) % 2, (g - 1) // 2
                            act.wait_ge(hsq_ready[layer], 4 * i + g)
                            act.wait_ge(down_done[layer], 16 * i + 1)
                            copy(hid_hi[:, m, half * HALF:(half + 1) * HALF], hsq[:, g - 1, :])\
                                .then_inc(hidh_ready[layer], 1)
                    if more:
                        split_hi(0, i + panel0 // 2 + 1)
                if last:
                    with act.Fori(0, N_MLP // 2 - 1) as i:
                        step(i, True)
                    step(N_MLP // 2 - 1, False)
                else:
                    with act.Fori(0, N_MLP // 2) as i:
                        step(i, True)

            act.wait_ge(oproj_free, 4 + 4 * N_OUT)
            norm(1)
            act.wait_ge(alo_ready, 2 * KT)
            mlp(0, MLP0, last=False)

            act.wait_ge(down_free[0], 4 + 16 * N_MLP // 2)
            norm(2)
            act.wait_ge(alo_ready, 3 * KT)
            act.sem_inc(u_free, 4)
            for i in range(N_SIN // 2):
                for slot in range(2):
                    split_hi(1 - slot, i + (SIN0 // 2 + slot))
                    for g in range(4):
                        act.wait_ge(u_done, 8 * i + 4 * slot + g + 1)
                        if 4 * i + 2 * slot + g // 2 > 0:
                            act.wait_ge(u_out, 16 * GB * (4 * i + 2 * slot + g // 2))
                        copy(ust[:, g % 2, :], ps[:, g, :]).then_inc(u_free, 1)
            act.sem_inc(gelu_done, 4)

            def block_out(q, s):
                if not (isinstance(q, int) and q == 0):
                    act.wait_ge(y_out, 16 * q)
                for b in range(2):
                    act.wait_ge(y_done, 2 * q + (b + 1 + 2))
                    act.activation(yb[:, :, :].rearrange("p (c a) j -> p a c j", a=2)[:, b, :, :],
                                   ps[:, 4 + 2 * s + b, :].rearrange("p (g j) -> p g j", g=PB),
                                   ACT.Gelu_apprx_tanh).then_inc(gelu_done, 1)
                act.wait_ge(gelu_done, 2 * q + (2 + 4))
                act.dma_start(y_scr[:, bass.ds(q * (GB * NC), GB * NC)], yb[:, :, :].rearrange("p g j -> p (g j)"))\
                    .then_inc(y_out, 16)

            def hi_of_z(q):
                act.wait_ge(z_in, q * (16 * GB) + 16 * GB)
                copy(act_hi[:, bass.ds(q, 1), :].squeeze(1), zt[:, :]).then_inc(z_hi, 1)

            block_out(0, 0)
            block_out(1, 1)
            with act.Fori(0, BLK // 2 - 1) as i:
                for s in (0, 1):
                    block_out(2 * i + (2 + s), s)
                    hi_of_z(2 * i + s)
            hi_of_z(BLK - 2)
            hi_of_z(BLK - 1)
            with act.Fori(0, N_GLU // 2) as i:
                for slot in range(2):
                    if slot == 1:
                        act.wait_ge(glu_done, 8 * i + 4)
                    split_hi(1 - slot, i + (GLU0 // 2 + slot))
                    if slot == 1:
                        for g in range(4):
                            act.wait_ge(glu_done, 8 * i + g + 5)
                            act.wait_ge(glu_free, 4 * i + g + 1)
                            act.activation(sig[:, g, :], ps[:, 4 + g, :], ACT.Sigmoid).then_inc(sig_ready, 1)
            act.wait_ge(glu_added, 2 * N_GLU + 1)
            norm(3)
            act.wait_ge(alo_ready, 4 * KT)
            mlp(1, MLP1, last=True)

            act.sem_inc(out_copied, 4)
            for i in range(T // P // 2):
                for s in (0, 1):
                    if i > 0:
                        act.wait_ge(y_stored[s], 16 * i)
                    for b in range(2):
                        act.wait_ge(out_turned, 4 * i + 2 * s + b + 1)
                        copy(os_[:, s, b * HALF:(b + 1) * HALF], ps[:, 2 * s + b, :]).then_inc(out_copied, 1)

        @block.tensor
        def _(pe):
            def times(dst, w1, w2, a1, a2, start, stop):
                pe.matmul(dst, w1, a1, start=start, stop=False)
                pe.matmul(dst, w1, a2, start=False, stop=False)
                return pe.matmul(dst, w2, a1, start=False, stop=stop)

            def project(bank, slot, col, half):
                tok = slice(half * HALF, (half + 1) * HALF)
                for k in range(KT):
                    last = times(ps[:, bank, :], w_hi8[:, slot, k, col:col + P], w_lo8[:, slot, k, col:col + P],
                                 act_hi[:, k, tok], act_lo[:, k, tok], k == 0, k == KT - 1)
                return last

            pe.wait_ge(const_ready, 1)
            with pe.Fori(0, T // P // 2) as i:
                for s in (0, 1):
                    pe.wait_ge(x_in[s], 16 * i + 16)
                    for b in range(2):
                        pe.wait_ge(x_copied, 4 * i + 2 * s + b + 1)
                        for k in range(4):
                            last = pe.transpose(ps[:, 2 * s + b, k * P:(k + 1) * P],
                                                xs[:, s, (4 * b + k) * P:(4 * b + k + 1) * P], ident[:, :])
                        last.then_inc(x_turned, 1)
            pe.wait_ge(par_ready, 1)
            for n in range(7):
                last = pe.transpose(ps[:, 4, n * GP:(n + 1) * GP], r32[:, 2 + n, :], ident[0:GP, 0:GP])
            last.then_inc(par_turned, 1)
            pe.wait_ge(ct_in, 16 * 16)
            for a in range(2):
                for t in range(4):
                    last = pe.transpose(ps[:, 5 + a, t * P:(t + 1) * P], ct[:, a, t, :], ident[:, :])
            last.then_inc(c_turned, 1)
            pe.wait_ge(z_ready, 1)
            pe.wait_ge(par_copied, 1)
            for n in range(2 * GP // 4):
                z = (zr, zi)[n // (GP // 4)]
                if n >= 2:
                    pe.wait_ge(z_copied, n - 1)
                for b in range(4):
                    last = pe.transpose(ps[:, (7, 4)[n % 2], b * P:(b + 1) * P],
                                        z[:, 4 * (n % (GP // 4)) + b, :, :].rearrange("p s c -> p (s c)"), ident[:, :])
                last.then_inc(z_turned, 1)
            pe.wait_ge(c_copied, 2)
            for a in range(2):
                rows = slice(a * NS, (a + 1) * NS)
                for g in range(GP):
                    dst = ps[:, 5 + a, g * GC:(g + 1) * GC]
                    pe.matmul(dst, zr[rows, g, :, :].rearrange("p s c -> p (s c)"), bc[rows, 0, g, :],
                              start=True, stop=False)
                    last = pe.matmul(dst, zi[rows, g, :, :].rearrange("p s c -> p (s c)"), bc[rows, 1, g, :],
                                     start=False, stop=True)
            last.then_inc(k_done, 1)

            def norm(n):
                for k in range(KT):
                    pe.wait_ge(sq_ready, KT * n + k + 1)
                    for half in range(2):
                        last = pe.matmul(ps[:, half, :], ones[:, :], sq[:, k % 2, half * HALF:(half + 1) * HALF],
                                         start=(k == 0), stop=(k == KT - 1))
                    last.then_inc(sq_added, 1)
                pe.wait_ge(alo_ready, KT * n + KT)

            pe.wait_ge(k_copied, 2)
            norm(0)
            pe.wait_ge(const_ready, 5)
            with pe.Fori(0, N_QK // 2) as i:
                for slot in range(2):
                    pe.wait_ge(lo_ready, 2 * i + slot + 1)
                    for g in range(5):
                        if g < 4:
                            pe.wait_ge(qk_free, 8 * i + 4 * slot + g + 1)
                            project(g, slot, g // 2 * P, g % 2).then_inc(qk_done, 1)
                        if g > 0:
                            pe.wait_ge(qk_sq, 8 * i + 4 * slot + g)
                            pe.matmul(ps[:, 4 + g - 1, :], headsum[:, :], sqh[:, g - 1, :],
                                      start=True, stop=True).then_inc(qk_sum, 1)
            pe.wait_ge(qk_free, 4 * N_QK + 4)
            with pe.Fori(0, N_V // 2) as i:
                for slot in range(2):
                    pe.wait_ge(lo_ready, 2 * i + (N_QK + slot + 1))
                    for t in range(KT):
                        pe.wait_ge((v_copied_a, v_copied_d)[t % 2], 8 * i + 4 * slot + t // 2 + 1)
                        dst = ps[:, t % 4, 0:PW]
                        tok = slice(t * P, (t + 1) * P)
                        for k in range(KT):
                            last = times(dst, act_hi[:, k, tok], act_lo[:, k, tok], w_hi8[:, slot, k, :],
                                         w_lo8[:, slot, k, :], k == 0, k == KT - 1)
                        last.then_inc(v_done, 1)
            pe.wait_ge(v_copied_a, 2 + 4 * N_V)
            pe.wait_ge(v_copied_d, 2 + 4 * N_V)
            pe.wait_ge(f_lo, 1)
            for half in range(2):
                tok = slice(half * HALF, (half + 1) * HALF)
                for k in range(KT):
                    last = times(ps[:, half, :], wf_hi[:, k, :], wf_lo[:, k, :], act_hi[:, k, tok],
                                 act_lo[:, k, tok], k == 0, k == KT - 1)
            last.then_inc(f_done, 1)

            pe.wait_ge(f_act, 1)
            pe.wait_ge(mask_hi, 2)
            pe.sem_inc(pv_done, T_SLOTS)

            def attend(order, pair, parity):
                for kind, u, n in order:
                    if kind == "S":
                        b = 4 * u + n
                        rows = slice(u % 2 * HD, (u % 2 + 1) * HD)
                        i = 4 * (u % 4 // 2) + n
                        mine = slice(i * P, (i + 1) * P)
                        if n == 0 and u in (0, 4):
                            pe.wait_ge(qk_lo, pair(2, 2 if u == 0 else 4))
                        pe.wait_ge(s_biased, pair(16, b + 1))
                        keys = (i + 1) * P
                        for k0 in range(0, keys, HALF):
                            k1 = min(keys, k0 + HALF)
                            times(ps[:, 2 * (b % 2) + k0 // HALF, 0:k1 - k0], q_hi[rows, mine],
                                  q_lo[rows, mine], k_hi[rows, k0:k1], k_lo[rows, k0:k1], True, k1 < keys)
                        pe.matmul(ps[:, 2 * (b % 2) + k0 // HALF, i * P - k0:k1 - k0], ident_r[:, :],
                                  mask[:, :], start=False, stop=True).then_inc(s_done, 1)
                    elif kind == "T":
                        t = TILES_BEFORE[u] + n
                        if n == 0:
                            pe.wait_ge(diag_ready, pair(4, u + 1))
                        pe.wait_ge(ptl_ready, pair(24, t + 1))
                        for m in range(first_col(u, n) // P, 4):
                            last = pe.matmul(ps[:, T_BANKS[t % T_SLOTS], m * P:(m + 1) * P],
                                             prob_of(u, parity)[:, m, n * P:(n + 1) * P], diag[:, u, m, :],
                                             start=True, stop=True)
                        last.then_inc(t_done, 1)
                    elif kind == "V":
                        t = u % 24
                        uu = max(k for k in range(4) if TILES_BEFORE[k] <= t)
                        j = t - TILES_BEFORE[uu]
                        h, lo = uu % 2, first_col(uu, j)
                        if j == 0:
                            pe.wait_ge(v_lo_ready, pair(2, h + 1))
                            if h == 0:
                                pe.wait_ge(olo_ready, pair(2, uu // 2 + 1))
                        pe.wait_ge(ptl_ready, pair(24, u + 1 + T_SLOTS))
                        times(ps[:, V_BANK, lo:HALF], v_hi[:, h, j, :], v_lo[:, h, j, :],
                              pt_hi[:, t % T_SLOTS, lo:HALF], pt_lo[:, t % T_SLOTS, lo:HALF],
                              h == 0 and j == 0, h == 1 and j == key_tiles(uu) - 1).then_inc(pv_done, 1)

            attend(attention_start(), START, 0)
            attend(attention_order(first=True), FIRST, 0)
            with pe.Fori(0, PAIRS // 2 - 1) as i:
                for parity in (1, 0):
                    attend(attention_order(), inner(i, parity), parity)
            attend(attention_order(last=True), LAST, 1)

            pe.wait_ge(olo_ready, 2 * PAIRS + 1)
            pe.wait_ge(s_biased, 16 * PAIRS + 2)

            def project_panels(count, panel0, done, free):
                with pe.Fori(0, count // 2) as i:
                    for slot in range(2):
                        pe.wait_ge(lo_ready, 2 * i + (panel0 + slot + 1))
                        for g in range(4):
                            pe.wait_ge(free, 8 * i + 4 * slot + g + 1)
                            project(g, slot, g // 2 * P, g % 2).then_inc(done, 1)

            pe.sem_inc(oproj_done, 1)
            project_panels(N_OUT, OUT0, oproj_done, oproj_free)

            def mlp(layer, panel0):
                pe.sem_inc(down_done[layer], 1)
                with pe.Fori(0, N_MLP // 2) as i:
                    pe.wait_ge(lo_ready, 2 * i + (panel0 + 1))
                    for g in range(4):
                        pe.wait_ge(up_free[layer], 4 * i + g + 1)
                        project(g, 0, g % 2 * P, g // 2).then_inc(up_done[layer], 1)
                    pe.wait_ge(lo_ready, 2 * i + (panel0 + 2))
                    for half in range(2):
                        pe.wait_ge(hidl_ready[layer], 4 * i + (2 * half + 2 + 1))
                        tok = slice(half * HALF, (half + 1) * HALF)
                        for f in range(KT):
                            q = KT * half + f
                            pe.wait_ge(down_free[layer], 16 * i + q + 1)
                            for k in range(2):
                                last = times(ps[:, 4 + q % 4, :], w_hi2[:, 1, k, f * P:(f + 1) * P],
                                             w_lo2[:, 1, k, f * P:(f + 1) * P], hid_hi[:, k, tok],
                                             hid_lo[:, k, tok], k == 0, k == 1)
                            last.then_inc(down_done[layer], 1)

            pe.wait_ge(oproj_free, 4 + 4 * N_OUT)
            norm(1)
            pe.wait_ge(rs_ready, 4)
            mlp(0, MLP0)
            pe.wait_ge(down_free[0], 4 + 16 * N_MLP // 2)
            norm(2)
            pe.wait_ge(rs_ready, 6)
            project_panels(N_SIN, SIN0, u_done, u_free)

            pe.wait_ge(u_free, 4 + 4 * N_SIN)
            pe.sem_inc(y_done, 2)

            def drive(n, q, s):
                pe.wait_ge(drive_in[s], 32 * n + 32)
                pe.wait_ge(state_ready, 2 * q + 2)
                for c in range(PB):
                    for a in range(2):
                        rows = slice(a * NS, (a + 1) * NS)
                        for n in range(2):
                            last = pe.matmul(ps[rows, 2 * s + n, c * NC:(c + 1) * NC],
                                             wst[:, s, n, c * P + a * NS:c * P + (a + 1) * NS],
                                             ub[:, s, 2 * c + a, :], start=True, stop=True)
                last.then_inc(drive_done, 1)

            def outputs(q, s):
                pe.wait_ge(gelu_done, 2 * q + 2)
                pe.wait_ge(state_ready, 2 * q + (2 + 4))
                for a in range(2):
                    rows = slice(a * NS, (a + 1) * NS)
                    for c in range(PB):
                        c0 = c * NC
                        g0 = (2 * c + a) * P
                        pe.matmul(ps[:, 4 + 2 * s + a, c0:c0 + NC], tap[:, s, g0:g0 + P], ub[:, s, 2 * c + a, :],
                                  start=True, stop=False)
                        for n in range(2):
                            last = pe.matmul(ps[:, 4 + 2 * s + a, c0 + 1:c0 + NC], wo[rows, s, n, c * P:(c + 1) * P],
                                             xb[rows, n, c0:c0 + NC - 1], start=False, stop=(n == 1))
                    last.then_inc(y_done, 1)

            drive(0, 0, 0)
            drive(0, 1, 1)
            outputs(0, 0)
            with pe.Fori(0, BLK // 2 - 1) as i:
                drive(i + 1, 2 * i + 2, 0)
                outputs(2 * i + 1, 1)
                drive(i + 1, 2 * i + 3, 1)
                outputs(2 * i + 2, 0)
            outputs(BLK - 1, 1)

            pe.wait_ge(z_lo, BLK + 1)
            with pe.Fori(0, N_GLU // 2) as i:
                for slot in range(2):
                    pe.wait_ge(lo_ready, 2 * i + (GLU0 + slot + 1))
                    for g in range(4):
                        pe.wait_ge(glu_free, 4 * i + g + 1)
                        project(4 * slot + g, slot, g // 2 * P, g % 2).then_inc(glu_done, 1)
            pe.wait_ge(glu_free, 4 + 2 * N_GLU)
            norm(3)
            pe.wait_ge(rs_ready, 8)
            mlp(1, MLP1)

            pe.wait_ge(down_free[1], 4 + 16 * N_MLP // 2)
            for i in range(T // P // 2):
                for s in (0, 1):
                    for b in range(2):
                        pe.wait_ge(out_copied, 4 * i + 2 * s + b + 1)
                        for k in range(4):
                            last = pe.transpose(ps[:, 2 * s + b, k * P:(k + 1) * P],
                                                xT[:, 4 * b + k, (2 * i + s) * P:(2 * i + s + 1) * P], ident[:, :])
                        last.then_inc(out_turned, 1)

        @block.vector
        def _(dve):
            done = [0]

            def link(ins):
                done[0] += 1
                ins.then_inc(prep_chain, 1)
                dve.wait_ge(prep_chain, done[0])

            def ts(out_, in_, s1, s2, op0, op1=None):
                if op1 is None:
                    link(dve.tensor_scalar(out_, in_, s1, None, op0))
                else:
                    link(dve.tensor_scalar(out_, in_, s1, s2, op0, op1))

            def tt(out_, a, b, op):
                link(dve.tensor_tensor(out_, a, b, op))

            def stt(out_, a, s, b, op0, op1):
                link(dve.scalar_tensor_tensor(out=out_, in0=a, scalar=s, in1=b, op0=op0, op1=op1))

            row = lambda n: r32[:, n, :]
            A_RE, A_IM = row(0), row(1)
            OUT = [row(2 + n) for n in range(7)]
            AB_RE, AB_IM, S_RE, S_IM, PH_C, PH_S, DECAY = OUT
            dt, mag, t0, t1, t2, t3, t4, co, si = (row(9 + n) for n in range(9))

            def exp(dst, src, n, r, y, w):
                dst, src, n, r, y = (v[:, 0:w] for v in (dst, src, n, r, y))
                ts(src, src, 172.0, -172.0, ALU.min, ALU.max)
                ts(n, src, LOG2E, ROUND, ALU.mult, ALU.add)
                ts(n, n, ROUND, None, ALU.subtract)
                stt(r, n, -LN2[0], src, ALU.mult, ALU.add)
                stt(r, n, -LN2[1], r, ALU.mult, ALU.add)
                ts(y, r, EXP_POLY[0], None, ALU.mult)
                for c in EXP_POLY[1:] + (1.0,):
                    stt(y, y, c, r, ALU.add, ALU.mult)
                ts(y, y, 1.0, None, ALU.add)
                ts(r, n, 0.5, ROUND, ALU.mult, ALU.add)
                ts(r, r, ROUND, None, ALU.subtract)
                tt(n, n, r, ALU.subtract)
                ts(i32[:, 0, 0:w], r, 127.0, float(1 << 23), ALU.add, ALU.mult)
                ts(i32[:, 1, 0:w], n, 127.0, float(1 << 23), ALU.add, ALU.mult)
                tt(y, y, i32[:, 0, 0:w].bitcast(F32), ALU.mult)
                tt(dst, y, i32[:, 1, 0:w].bitcast(F32), ALU.mult)

            dve.wait_ge(ssm_in, 80)
            link(dve.tensor_copy(t4[:, 0:2], ldt[:, :]))
            exp(t3, t4, t0, t1, t2, 2)
            link(dve.tensor_copy(dt.rearrange("g (a p) -> g a p", a=2),
                                 t3[:, 0:2].unsqueeze(2).to_broadcast((GP, 2, NS))))
            tt(t4, dt, A_RE, ALU.mult)
            exp(mag, t4, t0, t1, t2, P)
            tt(t0, dt, A_IM, ALU.mult)
            ts(t1, t0, 1.0 / (2.0 * PI), ROUND, ALU.mult, ALU.add)
            ts(t1, t1, ROUND, None, ALU.subtract)
            for c in TWO_PI:
                stt(t0, t1, -c, t0, ALU.mult, ALU.add)
            ts(t0, t0, 0.25, None, ALU.mult)
            tt(t1, t0, t0, ALU.mult)
            ts(t2, t1, SIN_POLY[0], SIN_POLY[1], ALU.mult, ALU.add)
            tt(t2, t2, t1, ALU.mult)
            ts(t2, t2, SIN_POLY[2], None, ALU.add)
            tt(t2, t2, t1, ALU.mult)
            stt(si, t2, 1.0, t0, ALU.add, ALU.mult)
            ts(t2, t1, COS_POLY[0], COS_POLY[1], ALU.mult, ALU.add)
            tt(t2, t2, t1, ALU.mult)
            ts(t2, t2, COS_POLY[2], None, ALU.add)
            tt(t2, t2, t1, ALU.mult)
            stt(co, t2, -0.5, t1, ALU.add, ALU.mult)
            for _ in range(2):
                tt(t2, si, si, ALU.mult)
                stt(si, co, 1.0, si, ALU.add, ALU.mult)
                ts(si, si, 2.0, None, ALU.mult)
                ts(co, t2, -2.0, None, ALU.mult)
            ts(co, co, 1.0, None, ALU.add)
            tt(AB_RE, mag, co, ALU.mult)
            tt(AB_IM, mag, si, ALU.mult)
            ts(t0, AB_RE, 1.0, None, ALU.subtract)
            tt(t1, A_RE, A_RE, ALU.mult)
            tt(t2, A_IM, A_IM, ALU.mult)
            tt(t1, t1, t2, ALU.add)
            link(dve.reciprocal(t1, t1))
            tt(t2, t0, A_RE, ALU.mult)
            tt(t3, AB_IM, A_IM, ALU.mult)
            tt(t2, t2, t3, ALU.add)
            tt(S_RE, t2, t1, ALU.mult)
            tt(t2, AB_IM, A_RE, ALU.mult)
            tt(t3, t0, A_IM, ALU.mult)
            tt(t2, t2, t3, ALU.subtract)
            tt(S_IM, t2, t1, ALU.mult)
            for n in range(3):
                tt(DECAY if n == 2 else t4, mag if n == 0 else t4, mag if n == 0 else t4, ALU.mult)
            for n in range(3):
                c_, s_ = (co, si) if n == 0 else (PH_C, PH_S)
                tt(t0, c_, c_, ALU.mult)
                tt(t1, s_, s_, ALU.mult)
                tt(t2, c_, s_, ALU.mult)
                tt(PH_C, t0, t1, ALU.subtract)
                if n < 2:
                    ts(PH_S, t2, 2.0, None, ALU.mult)
            dve.tensor_scalar(PH_S, t2, 2.0, None, ALU.mult).then_inc(par_ready, 1)

            dve.wait_ge(par_copied, 1)
            over_c = lambda n: ab[:, n, :].unsqueeze(2).to_broadcast((P, GP, GC))
            tmp = pt[:, 0, :].rearrange("p (g c) -> p g c", c=GC)
            tm2 = pt[:, 1, :].rearrange("p (g c) -> p g c", c=GC)

            def cmul(o_re, o_im, a_re, a_im, b_re, b_im, last=None):
                tt(tmp, a_im, b_im, ALU.mult)
                tt(o_re, a_re, b_re, ALU.mult)
                tt(o_re, o_re, tmp, ALU.subtract)
                tt(tmp, a_im, b_re, ALU.mult)
                tt(o_im, a_re, b_im, ALU.mult)
                ins = dve.tensor_tensor(o_im, o_im, tmp, ALU.add)
                if last is None:
                    link(ins)
                else:
                    ins.then_inc(last, 1)

            b_re, b_im = bc[:, 0, :, :], bc[:, 1, :, :]
            cmul(zr[:, :, L - 1, :], zi[:, :, L - 1, :], b_re, b_im, over_c(2), over_c(3), last=b_used)
            dve.wait_ge(b_used, 1)
            for r in range(L - 2, -1, -1):
                cmul(zr[:, :, r, :], zi[:, :, r, :], zr[:, :, r + 1, :], zi[:, :, r + 1, :], over_c(0), over_c(1),
                     last=z_ready if r == 0 else None)

            dve.wait_ge(k_copied, 2)
            dve.wait_ge(dm_ready, 1)
            dve.tensor_tensor(kall[96:P, :, :, :].rearrange("p g a c -> p (g a c)"),
                              kall[96:P, :, :, :].rearrange("p g a c -> p (g a c)"),
                              dm[96:P, :, :].rearrange("p g c -> p (g c)"), ALU.add).then_inc(k_ready, 1)
            dve.wait_ge(k_ready, 1)

            for s in range(L):
                c_re, c_ni = (bc[:, 0, :, :], bc[:, 1, :, :]) if s == 0 else (zr[:, :, s - 1, :], zi[:, :, s - 1, :])
                tt(tmp, c_ni, over_c(1), ALU.mult)
                tt(zr[:, :, s, :], c_re, over_c(0), ALU.mult)
                tt(zr[:, :, s, :], zr[:, :, s, :], tmp, ALU.add)
                tt(tmp, c_re, over_c(1), ALU.mult)
                tt(zi[:, :, s, :], c_ni, over_c(0), ALU.mult)
                ins = dve.tensor_tensor(zi[:, :, s, :], zi[:, :, s, :], tmp, ALU.subtract)
                if s < L - 1:
                    link(ins)
                else:
                    ins.then_inc(wo_ready, 1)

            dve.wait_ge(wo_out, 32)
            e_re = zr[:, :, :, :].rearrange("p g s c -> p g (s c)")
            e_im = zi[:, :, :, :].rearrange("p g s c -> p g (s c)")
            link(dve.memset(e_re[:, :, 0:1], 1.0))
            link(dve.memset(e_im[:, :, 0:1], 0.0))
            for n in range(7):
                m = 1 << n
                if n > 0:
                    tt(sq_t[:, 0, :], ab[:, 4, :], ab[:, 4, :], ALU.mult)
                    tt(sq_t[:, 1, :], ab[:, 5, :], ab[:, 5, :], ALU.mult)
                    tt(sq_t[:, 2, :], ab[:, 4, :], ab[:, 5, :], ALU.mult)
                    tt(ab[:, 4, :], sq_t[:, 0, :], sq_t[:, 1, :], ALU.subtract)
                    ts(ab[:, 5, :], sq_t[:, 2, :], 2.0, None, ALU.mult)
                pairs = min(GP, 2 * GP * GC // m)
                for g0 in range(0, GP, pairs):
                    gs = slice(g0, g0 + pairs)
                    c_ = ab[:, 4, gs].unsqueeze(2).to_broadcast((P, pairs, m))
                    s_ = ab[:, 5, gs].unsqueeze(2).to_broadcast((P, pairs, m))
                    tp = pt[:, :, :].rearrange("p a b -> p (a b)")[:, 0:pairs * m].rearrange("p (g j) -> p g j", j=m)
                    old_re, old_im = e_re[:, gs, 0:m], e_im[:, gs, 0:m]
                    new_re, new_im = e_re[:, gs, m:2 * m], e_im[:, gs, m:2 * m]
                    tt(tp, old_im, s_, ALU.mult)
                    tt(new_re, old_re, c_, ALU.mult)
                    tt(new_re, new_re, tp, ALU.subtract)
                    tt(tp, old_im, c_, ALU.mult)
                    tt(new_im, old_re, s_, ALU.mult)
                    ins = dve.tensor_tensor(new_im, new_im, tp, ALU.add)
                    if n == 6 and g0 + pairs == GP:
                        ins.then_inc(cs_ready, 1)
                    else:
                        link(ins)

            def lo_of(slot, m):
                dve.wait_ge(hi_ready, 2 * m + slot + 1)
                dve.tensor_tensor(w_lo[:, slot, :], raw[:, slot, :], w_hi[:, slot, :].bitcast(F32), ALU.subtract)\
                    .then_inc(lo_ready, 1)

            def norm(n, gain, chunked=False):
                dve.wait_ge(rs_ready, 2 * n + 2)
                dve.reciprocal(rinv[:, :], rs[:, :]).then_inc(rinv_ready, 1)
                dve.wait_ge(rinv_ready, n + 1)
                for k in range(KT):
                    if k >= 2:
                        dve.wait_ge(alo_ready, KT * n + k - 1)
                    dst, src, inv = hf[:, k % 2, :], xT[:, k, :], rinv[:, :]
                    if chunked:
                        dst = dst.rearrange("p (s j) -> p s j", s=L)
                        src = src.rearrange("p (j s) -> p s j", s=L)
                        inv = inv.rearrange("p (j s) -> p s j", s=L)
                    dve.scalar_tensor_tensor(out=dst, in0=src, scalar=gains[:, gain, k:k + 1], in1=inv,
                                             op0=ALU.mult, op1=ALU.mult).then_inc(hf_ready, 1)

            dve.wait_ge(cs_out, 32)
            dve.wait_ge(small_in, 16 * 9)
            norm(0, 0)
            ts(qk_gain[:, 0:4], qk_g[:, 0:1].to_broadcast((P, 4)), -HD ** -0.5, None, ALU.mult)
            link(dve.tensor_copy(qk_gain[:, 4:8], qk_g[:, 1:2].to_broadcast((P, 4))))
            lo_of(0, 0)

            dve.wait_ge(alo_ready, KT)
            dve.sem_inc(qk_free, 4)
            def qk_panels(i):
                for slot in range(2):
                    lo_of(1 - slot, i + slot)
                    for g in range(4):
                        n = 4 * slot + g
                        dve.wait_ge(qk_root, 8 * i + n + 1)
                        dve.reciprocal(rih[:, g % 2, :], rsh[:, g, :]).then_inc(qk_inv, 1)
                        dve.wait_ge(qk_inv, 8 * i + n + 1)
                        if not (isinstance(i, int) and 4 * i + n // 2 == 0):
                            dve.wait_ge(stg_out[g % 2], i * 64 + 16 * (n // 2))
                        dve.scalar_tensor_tensor(out=stg[:, g % 2, :], in0=ps[:, g, :],
                                                 scalar=qk_gain[:, bass.ds(2 * i + slot, 1)], in1=rih[:, g % 2, :],
                                                 op0=ALU.mult, op1=ALU.mult).then_inc(qk_free, 1)
            qk_panels(0)
            with dve.Fori(1, N_QK // 2) as i:
                qk_panels(i)
            dve.sem_inc(v_copied_d, 2)
            for i in range(N_V // 2):
                for slot in range(2):
                    if i + slot < N_V // 2:
                        lo_of(1 - slot, N_QK // 2 + i + slot)
                    for t in range(1, KT, 2):
                        dve.wait_ge(v_done, 16 * i + 8 * slot + t + 1)
                        if i + slot + t > 1:
                            dve.wait_ge(vst_out[1], 16 * (8 * i + 4 * slot + t // 2))
                        dve.tensor_copy(vst[:, 1, :], ps[:, t % 4, 0:PW]).then_inc(v_copied_d, 1)
            dve.memset(wf_hi[:, :, NH:P].bitcast(F32), 0.0).then_inc(f_zero, 1)
            dve.memset(wf_lo[:, :, NH:P].bitcast(F32), 0.0).then_inc(f_zero, 1)
            dve.memset(fone[:, :], 1.0).then_inc(f_zero, 1)
            dve.wait_ge(f_hi, 1)
            dve.tensor_tensor(wf_lo[:, :, 0:NH], wf[:, :, :], wf_hi[:, :, 0:NH].bitcast(F32), ALU.subtract)\
                .then_inc(f_lo, 1)
            dve.wait_ge(f_act, 4)
            dve.tensor_scalar(fy[:, :], fy[:, :], 0.0, None, ALU.min).then_inc(f_min, 1)
            dve.wait_ge(f_min, 1)
            dve.tensor_tensor(fy[:, :], fy[:, :], fe[:, :], ALU.subtract).then_inc(f_min, 1)
            dve.wait_ge(f_min, 2)
            dve.wait_ge(f_zero, 3)
            dve.tensor_tensor_scan(fc[:, :], fone[:, :], fy[:, :], 0.0, ALU.mult, ALU.add).then_inc(f_min, 2)

            dve.wait_ge(v_done, KT * N_V)
            for h in range(2):
                pad = slice((1 - h) * HD, (2 - h) * HD)
                dve.memset(v_hi[:, h, :, pad].bitcast(F32), 0.0).then_inc(v_pad, 1)
                dve.memset(v_lo[:, h, :, pad].bitcast(F32), 0.0).then_inc(v_pad, 1)
            dve.sem_inc(s_biased, 2)
            dve.sem_inc(ptl_ready, T_SLOTS)
            dve.sem_inc(olo_ready, 1)

            def attend(order, pair, parity):
                for kind, u, n in order:
                    if kind == "QK":
                        nxt = 0 if pair is START else 1
                        for k, (d_, r_, h_) in enumerate(((q_lo, q_raw, q_hi), (k_lo, k_raw, k_hi))):
                            dve.wait_ge(qk_hi, pair(2, 2 * nxt + k + 1))
                            dve.tensor_tensor(d_, r_, h_.bitcast(F32), ALU.subtract).then_inc(qk_lo, 1)
                    elif kind in ("V0", "V1"):
                        h = 0 if kind == "V0" else 1
                        nxt = 1 if h == 0 and pair is not START else 0
                        mine = slice(h * HD, (h + 1) * HD)
                        dve.wait_ge(v_hi_ready, pair(2, 2 * nxt + h + 1))
                        dve.tensor_tensor(v_lo[:, h, :, mine], v_raw[:, :, mine],
                                          v_hi[:, h, :, mine].bitcast(F32), ALU.subtract).then_inc(v_lo_ready, 1)
                    elif kind == "S":
                        b = 4 * u + n
                        keys = keys_of(u, n)
                        dve.wait_ge(s_done, pair(16, b + 1))
                        dve.wait_ge(c_in[u % 2], pair(16, 16 + 16 * (u // 4)))
                        turned = {2: 0, 3: 8, 4: 16, 5: 16}.get(u)
                        if pair is not START and not (pair is FIRST and turned == 0):
                            dve.wait_ge(t_done, pair(24, turned))
                        dve.memset(tick[:, b % 8:b % 8 + 1], 0.0)
                        dve.tensor_tensor_reduce(
                            prob_of(u, parity)[:, n, 0:keys], ps[:, 2 * (b % 2):2 * (b % 2) + 2, :]
                            .rearrange("p b k -> p (b k)")[:, 0:keys], cb[:, u % 2, 0:keys], 1.0, 3e38,
                            ALU.add, ALU.min, mx[:, b % 16:b % 16 + 1]).then_inc(s_biased, 1)
                    elif kind == "R":
                        dve.wait_ge(p_ready, pair(16, 4 * u + 4))
                        mine = slice(4 * (u % 4), 4 * (u % 4) + 4)
                        dve.reciprocal(inv_sums[:, mine], sums[:, mine]).then_inc(inv_ready, 1)
                    elif kind == "T":
                        t = TILES_BEFORE[u] + n
                        lo = first_col(u, n)
                        dve.wait_ge(pth_ready, pair(24, t + 1))
                        dve.tensor_tensor(pt_lo[:, t % T_SLOTS, lo:HALF], ps[:, T_BANKS[t % T_SLOTS], lo:HALF],
                                          pt_hi[:, t % T_SLOTS, lo:HALF].bitcast(F32), ALU.subtract)\
                            .then_inc(ptl_ready, 1)
                    elif kind == "O":
                        dve.wait_ge(ohi_ready, pair(2, u + 1))
                        dve.tensor_tensor(output_of(act_lo, u, pair), ps[:, V_BANK, :],
                                          output_of(act_hi, u, pair).bitcast(F32), ALU.subtract)\
                            .then_inc(olo_ready, 1)

            attend(attention_start(), START, 0)
            attend(attention_order(first=True), FIRST, 0)
            with dve.Fori(0, PAIRS // 2 - 1) as i:
                for parity in (1, 0):
                    attend(attention_order(), inner(i, parity), parity)
            attend(attention_order(last=True), LAST, 1)

            lo_of(0, OUT0 // 2)

            def added(done_, free, tile, g, bank, tok, n):
                dve.wait_ge(done_, n + (1 + 1))
                dve.wait_ge(free, n + 1)
                dst = xT[:, bass.ds(tile, 1), tok].squeeze(1) if not isinstance(tile, int) else xT[:, tile, tok]
                dve.tensor_tensor(dst, ps[:, bank, :], dst, ALU.add).then_inc(free, 1)

            dve.sem_inc(oproj_free, 4)
            with dve.Fori(0, N_OUT // 2) as i:
                for slot in range(2):
                    lo_of(1 - slot, i + (OUT0 // 2 + slot))
                    for g in range(4):
                        half = g % 2
                        added(oproj_done, oproj_free, 4 * i + (2 * slot + g // 2), g, g,
                              slice(half * HALF, (half + 1) * HALF), 8 * i + (4 * slot + g))
            dve.wait_ge(oproj_free, 4 + 4 * N_OUT)
            norm(1, 2)

            def mlp(layer, panel0, last):
                dve.sem_inc(down_free[layer], 4)

                def step(i, more):
                    lo_of(1, i + panel0 // 2)
                    for q in range(2 * KT):
                        half = q // KT
                        added(down_done[layer], down_free[layer], q % KT, q, 4 + q % 4,
                              slice(half * HALF, (half + 1) * HALF), 16 * i + q)
                        if q == 3 and more:
                            lo_of(0, i + (panel0 // 2 + 1))
                if last:
                    with dve.Fori(0, N_MLP // 2 - 1) as i:
                        step(i, True)
                    step(N_MLP // 2 - 1, False)
                else:
                    with dve.Fori(0, N_MLP // 2) as i:
                        step(i, True)
                dve.wait_ge(down_free[layer], 4 + 16 * N_MLP // 2)

            mlp(0, MLP0, last=False)
            norm(2, 1, chunked=True)
            with dve.Fori(0, N_SIN // 2) as i:
                for slot in range(2):
                    lo_of(1 - slot, i + (SIN0 // 2 + slot))

            dve.sem_inc(state_ready, 4)
            STEPS = 12

            def states(n, q, s):
                made = [0]

                def step(ins):
                    made[0] += 1
                    ins.then_inc(scan_chain, 1)
                    dve.wait_ge(scan_chain, STEPS * q + made[0])

                c_, s_ = cs[:, s, 0, :], cs[:, s, 1, :]
                v_re, v_im = ps[:, 2 * s, :], ps[:, 2 * s + 1, :]
                w_re, w_im, tmp = (vb[:, n, :] for n in range(3))
                x_re, x_im = xb[:, 0, :], xb[:, 1, :]
                d_ = decay[:, :, :].rearrange("p g j -> p (g j)")
                dve.wait_ge(drive_done, q + 1)
                dve.wait_ge(out_in[s], 48 * n + 48)
                step(dve.tensor_tensor(w_re, v_re, c_, ALU.mult))
                step(dve.tensor_tensor(tmp, v_im, s_, ALU.mult))
                step(dve.tensor_tensor(w_re, w_re, tmp, ALU.add))
                step(dve.tensor_tensor(w_im, v_im, c_, ALU.mult))
                step(dve.tensor_tensor(tmp, v_re, s_, ALU.mult))
                step(dve.tensor_tensor(w_im, w_im, tmp, ALU.subtract))
                dve.wait_ge(decay_ready, q + 1)
                step(dve.tensor_tensor_scan(w_re, d_, w_re, 0.0, ALU.mult, ALU.add))
                step(dve.tensor_tensor_scan(w_im, d_, w_im, 0.0, ALU.mult, ALU.add))
                dve.wait_ge(y_done, 2 * q + 2)
                step(dve.tensor_tensor(x_re, w_re, c_, ALU.mult))
                step(dve.tensor_tensor(tmp, w_im, s_, ALU.mult))
                dve.tensor_tensor(x_re, x_re, tmp, ALU.subtract).then_inc(state_ready, 1)
                dve.wait_ge(state_ready, 2 * q + (1 + 4))
                step(dve.tensor_tensor(x_im, w_re, s_, ALU.mult))
                step(dve.tensor_tensor(tmp, w_im, c_, ALU.mult))
                dve.tensor_tensor(x_im, x_im, tmp, ALU.add).then_inc(state_ready, 1)
                dve.wait_ge(state_ready, 2 * q + (2 + 4))

            with dve.Fori(0, BLK // 2) as i:
                for s in (0, 1):
                    states(i, 2 * i + s, s)

            dve.sem_inc(glu_free, 4)
            dve.sem_inc(glu_added, 1)
            with dve.Fori(0, N_GLU // 2) as i:
                for slot in range(2):
                    lo_of(1 - slot, i + (GLU0 // 2 + slot))
                for g in range(4):
                    m, half = g // 2, g % 2
                    n = 4 * i + g
                    dve.wait_ge(sig_ready, n + 1)
                    dve.wait_ge(glu_added, n + 1)
                    dve.tensor_tensor(gated[:, half, :], ps[:, g, :], sig[:, g, :], ALU.mult).then_inc(glu_free, 1)
                    dve.wait_ge(glu_free, n + 1 + 4)
                    dst = xT[:, bass.ds(2 * i + m, 1), :].squeeze(1).rearrange("p (j s) -> p s j", s=L)\
                        [:, half * L // 2:(half + 1) * L // 2, :]
                    dve.tensor_tensor(dst, gated[:, half, :].rearrange("p (s j) -> p s j", j=NC), dst, ALU.add)\
                        .then_inc(glu_added, 1)
            dve.wait_ge(glu_added, 2 * N_GLU + 1)
            norm(3, 3)
            mlp(1, MLP1, last=True)


INS = ["x", "norm_mix_g", "norm_mlp_g", "attn_w_in", "attn_b_f", "attn_q_g", "attn_k_g", "attn_w_out", "ssm_w_in",
       "ssm_a_re", "ssm_a_im", "ssm_b_re", "ssm_b_im", "ssm_c_re", "ssm_c_im", "ssm_log_dt", "ssm_d", "ssm_w_glu",
       "mlp_w1", "mlp_w2"]


def kernel(**inputs):
    import numpy as np
    import concourse.bacc as bacc
    from concourse.bass_utils import run_bass_kernel_spmd

    nc = bacc.Bacc("TRN2", target_bir_lowering=False, num_devices=1)
    arrays, args = {}, []
    for name in INS:
        a = np.ascontiguousarray(inputs[name])
        arrays[f"in_{name}"] = a
        args.append(nc.dram_tensor(f"in_{name}", a.shape, mybir.dt.from_np(a.dtype), kind="ExternalInput").ap())
    args.append(nc.dram_tensor("out_0", (1, T, D), F32, kind="ExternalOutput").ap())
    build(nc, *args)
    r = run_bass_kernel_spmd(nc, [arrays], core_ids=[0])
    return r.results[0]["out_0"]
```

```python
from contextlib import ExitStack

import concourse.bass as bass
from concourse import mybir

F32 = mybir.dt.float32
F32R = mybir.dt.float32r
I32 = mybir.dt.int32
ALU = mybir.AluOpType
ACT = mybir.ActivationFunctionType

P = 128
T = 1024
D = 1024
KT = D // P
HALF = 512
NH = 16
HD = D // NH
PAIRS = NH // 2
FF = 4096
EPS = 1e-6
PANEL = 2048
PW = PANEL // KT
NG = 64
GC = 16
NS = 64
L = 8
NC = T // L
GP = NG // 2
TST = 4
OUT = 4
BLK = KT
GB = NG // BLK
PB = GP // BLK
MASKED = 1e30

N_QK, N_V = 8, 4
N_ATT = N_QK + N_V
N_OUT = D // PW
N_MLP = 2 * FF // PW
N_SIN = D // PW
N_GLU = 2 * D // PW
OUT0 = N_ATT
MLP0 = OUT0 + N_OUT
SIN0 = MLP0 + N_MLP
GLU0 = SIN0 + N_SIN
MLP1 = GLU0 + N_GLU
N_PANELS = MLP1 + N_MLP

TWO_PI = (6.28125, 0.0019354820251464844, -1.7484555314695172e-07)
LN2 = (0.693359375, -2.12194440e-4)
EXP_POLY = (1.9875691500e-4, 1.3981999507e-3, 8.3334519073e-3, 4.1665795894e-2, 1.6666665459e-1, 5.0000001201e-1)
SIN_POLY = (-1.9515295891e-4, 8.3321608736e-3, -1.6666654611e-1)
COS_POLY = (2.443315711809948e-5, -1.388731625493765e-3, 4.166664568298827e-2)
LOG2E = 1.4426950408889634
PI = 3.141592653589793
ROUND = 12582912.0


def attention_order(first=False, last=False):
    after = {t: [] for t in range(24)}
    for m, t in enumerate((0, 1, 1, 3)):
        after[t].append(("S", 2, m))
        after[t + 1].append(("E", 2, m))
        after[t + 8].append(("S", 3, m))
        after[t + 9].append(("E", 3, m))
    after[4].append(("R", 2, 0))
    after[12].append(("R", 3, 0))
    after[3].append(("V1", 0, 0))
    after[9].insert(0, ("O", 0, 0))
    if not first:
        after[1].insert(0, ("O", -1, 0))
    if not last:
        after[14].append(("QK", 0, 0))
        after[18].append(("V0", 0, 0))
        for m in range(4):
            after[16 + m // 2].append(("S", 4, m))
            after[17 + m // 2].append(("E", 4, m))
            after[18 + m].append(("S", 5, m))
            after[19 + m].append(("E", 5, m))
        after[18].append(("R", 4, 0))
        after[22].append(("R", 5, 0))
    order = []
    for u in range(4):
        for j in range(key_tiles(u)):
            t = TILES_BEFORE[u] + j
            order.append(("T", u, j))
            if t >= V_LAG or not first:
                order.append(("V", t - V_LAG, 0))
            order += after[t]
    if last:
        order += [("V", t, 0) for t in range(24 - V_LAG, 24)] + [("O", 1, 0)]
    return order


def attention_start():
    order = [("QK", 0, 0), ("V0", 0, 0)]
    for u in (0, 1):
        order += [(kind, u, m) for m in range(4) for kind in "SE"] + [("R", u, 0)]
    return order


def key_tiles(u):
    return 4 if u % 4 < 2 else 8


TILES_BEFORE = [0, 4, 8, 16, 24]
V_LAG = 2
T_SLOTS = 3
T_BANKS = (4, 5, 7)
V_BANK = 6


def build(nc, x, norm_mix_g, norm_mlp_g, attn_w_in, attn_b_f, attn_q_g, attn_k_g, attn_w_out, ssm_w_in,
          ssm_a_re, ssm_a_im, ssm_b_re, ssm_b_im, ssm_c_re, ssm_c_im, ssm_log_dt, ssm_d, ssm_w_glu,
          mlp_w1, mlp_w2, out):
    def scratch(name, shape, dt=F32):
        return nc.dram_tensor(name, shape, dt, kind="Internal").ap()

    qk_scr = scratch("qk_scr", (2 * D, T))
    v_scr = scratch("v_scr", (T, D))
    c_scr = scratch("c_scr", (NH, T))
    u_scr = scratch("u_scr", (P, NG * NC))
    y_scr = scratch("y_scr", (P, NG * NC))
    wst_scr = scratch("wst_scr", (2, P, GP * P))
    wo_scr = scratch("wo_scr", (2, P, GP * P))
    cs_scr = scratch("cs_scr", (2, P, GP * NC))
    kp_scr = scratch("kp_scr", (NG, GC, (2 * L - 1) * GC))
    tap_scr = scratch("tap_scr", (P, NG * P))

    ctx = ExitStack()
    with ctx:
        def sem(name):
            return ctx.enter_context(nc.semaphore(name))

        def sb(name, shape, dt=F32, stack=ctx):
            return stack.enter_context(nc.sbuf_tensor(name, shape, dt))

        ps = ctx.enter_context(nc.psum_tensor("ps", [P, 8, HALF], F32))

        xT = sb("xT", [P, KT, T])
        with ExitStack() as st:
            xs = sb("xs", [P, 2, D], stack=st)
            ct = sb("ct", [P, 2, 4, P], stack=st)
            tst = sb("tst", [P, TST, 4 * P], stack=st)
            wr = sb("wr", [P, GP, L, GC], stack=st)
            wi = sb("wi", [P, GP, L, GC], stack=st)
        act_hi = sb("act_hi", [P, KT, T], F32R)
        act_lo = sb("act_lo", [P, KT, T], F32R)
        with ExitStack() as st:
            sb("slot0", [P, PANEL], stack=st)
            kall = sb("kall", [P, GP, 2, GC], stack=st)
            dm = sb("dm", [P, NG, GC], stack=st)
        raw = sb("raw", [P, 2, PANEL])
        with ExitStack() as st:
            er = sb("er", [P, GP, NC], stack=st)
            ei = sb("ei", [P, GP, NC], stack=st)
        w_hi = sb("w_hi", [P, 2, PANEL], F32R)
        w_lo = sb("w_lo", [P, 2, PANEL], F32R)
        ident = sb("ident", [P, P])
        ones = sb("ones", [P, P])
        headsum = sb("headsum", [P, P])
        gains = sb("gains", [P, 4, KT])
        qk_g = sb("qk_g", [P, 2])
        qk_gain = sb("qk_gain", [P, N_QK])
        eps_t = sb("eps_t", [P, 1])
        fb = sb("fb", [NH, 1])
        ab = sb("ab", [P, 7, GP])
        mx = sb("mx", [P, 16])
        sums = sb("sums", [P, 16])
        inv_sums = sb("inv_sums", [P, 16])

        w_hi8 = w_hi[:, :, :].rearrange("p s (k f) -> p s k f", k=KT)
        w_lo8 = w_lo[:, :, :].rearrange("p s (k f) -> p s k f", k=KT)
        w_hi2 = w_hi[:, :, :].rearrange("p s (k f) -> p s k f", k=2)
        w_lo2 = w_lo[:, :, :].rearrange("p s (k f) -> p s k f", k=2)

        def phase():
            return ExitStack()

        with phase() as st:
            r32 = sb("r32", [GP, 22, P], stack=st)
            i32 = sb("i32", [GP, 2, P], I32, stack=st)
            ldt = sb("ldt", [GP, 2], stack=st)
            pt = sb("pt", [P, GP, GC], stack=st)
            ept = sb("ept", [P, 2 * GP * GC], stack=st)
            sq_t = sb("sq_t", [P, 3, GP], stack=st)
            bt = sb("bt", [P, 2, GP, GC], stack=st)
            zero = sb("zero", [NG, (L - 1) * GC], stack=st)
            sb("gap", [P, 302], stack=st)
            cc = sb("cc", [P, 2, GP, GC], stack=st)
            zr = sb("zr", [P, GP, L, GC], stack=st)
            zi = sb("zi", [P, GP, L, GC], stack=st)
        with phase() as st:
            os_ = sb("os", [P, OUT, D], stack=st)
        with phase() as st:
            sq = sb("sq", [P, 4, HALF], stack=st)
            rs = sb("rs", [P, T], stack=st)
            rinv = sb("rinv", [P, T], stack=st)
            hf = sb("hf", [P, 4, HALF], stack=st)
        with phase() as st:
            sqh = sb("sqh", [P, 4, HALF], stack=st)
            rsh = sb("rsh", [P, 4, HALF], stack=st)
            rih = sb("rih", [P, 2, HALF], stack=st)
            stg = sb("stg", [P, 2, HALF], stack=st)
            vst = sb("vst", [P, 2, PW], stack=st)
            wf = sb("wf", [P, KT, NH], stack=st)
            wf_hi = sb("wf_hi", [P, KT, P], F32R, stack=st)
            wf_lo = sb("wf_lo", [P, KT, P], F32R, stack=st)
            fy = sb("fy", [NH, T], stack=st)
            fe = sb("fe", [NH, T], stack=st)
            fl = sb("fl", [NH, T], stack=st)
            fc = sb("fc", [NH, T], stack=st)
            fone = sb("fone", [NH, T], stack=st)
        with phase() as st:
            prob = sb("prob", [P, 2, 4, T], stack=st)
            diag = sb("diag", [P, 4, 4, P], stack=st)
            pt_hi = sb("pt_hi", [P, T_SLOTS, HALF], F32R, stack=st)
            pt_lo = sb("pt_lo", [P, T_SLOTS, HALF], F32R, stack=st)
            cb = sb("cb", [P, 2, T], stack=st)
            mask = sb("mask", [P, P], F32R, stack=st)
            ident_r = sb("ident_r", [P, P], F32R, stack=st)
            mask_f = diag[:, 0, 0, :]
            tick = sb("tick", [P, 8], stack=st)
        with phase() as st:
            hid_hi = sb("hid_hi", [P, 2, T], F32R, stack=st)
            hid_lo = sb("hid_lo", [P, 2, T], F32R, stack=st)
            relu = sb("relu", [P, 4, HALF], stack=st)
            hsq = sb("hsq", [P, 4, HALF], stack=st)
        with phase() as st:
            wst = sb("wst", [P, 2, 2, PB * P], stack=st)
            wo = sb("wo", [P, 2, 2, PB * P], stack=st)
            cs = sb("cs", [P, 2, 2, PB * NC], stack=st)
            tap = sb("tap", [P, 2, GB * P], stack=st)
            ub = sb("ub", [P, 2, GB, NC], stack=st)
            decay = sb("decay", [P, PB, NC], stack=st)
            vb = sb("vb", [P, 3, PB * NC], stack=st)
            xb = sb("xb", [P, 2, PB * NC], stack=st)
            yb = sb("yb", [P, GB, NC], stack=st)
            zt = sb("zt", [P, T], stack=st)
            ust = vb[:, 0:2, :]
        with phase() as st:
            sig = sb("sig", [P, 4, HALF], stack=st)
            gated = sb("gated", [P, 2, HALF], stack=st)

        q_raw, k_raw = raw[:, 0, 0:T], raw[:, 0, T:2 * T]
        v_raw = raw[:, 1, 0:T].rearrange("p (j f) -> p j f", j=KT)
        q_hi, k_hi = w_hi[:, 0, 0:T], w_hi[:, 0, T:2 * T]
        q_lo, k_lo = w_lo[:, 0, 0:T], w_lo[:, 0, T:2 * T]
        v_hi = w_hi[:, 1, :].rearrange("p (h j f) -> p h j f", h=2, j=KT)
        v_lo = w_lo[:, 1, :].rearrange("p (h j f) -> p h j f", h=2, j=KT)

        NORM = 2 * KT

        def tokens(buf, half, chunked):
            if not chunked:
                return buf[:, half * HALF:(half + 1) * HALF]
            return buf.rearrange("p (j s) -> p s j", s=L)[:, half * L // 2:(half + 1) * L // 2, :]

        def as_tokens(buf, chunked):
            return buf.rearrange("p (s j) -> p s j", j=NC) if chunked else buf

        START = lambda a, b: b
        FIRST = lambda a, b: b
        LAST = lambda a, b: (PAIRS - 1) * a + b

        def inner(i, parity):
            return lambda a, b: i * (2 * a) + ((2 - parity) * a + b)

        def keys_of(u, n):
            return (4 * (u % 4 // 2) + n + 1) * P

        def first_col(u, j):
            return max(0, j - 4 * (u // 2)) * P

        def prob_of(u, parity):
            if u in (2, 4, 5):
                parity = 1 - parity
            if u in (2, 3):
                return prob[:, parity, :, :]
            return prob[:, parity, :, :].rearrange("p m (h k) -> p h m k", h=2)[:, u % 2]

        def output_of(buf, g, pair):
            tok = slice(0, HALF) if g == 0 else slice(HALF, T)
            n = pair(1, -1 if g < 0 else 0)
            return buf[:, n, tok] if isinstance(n, int) else buf[:, bass.ds(n, 1), tok].squeeze(1)

        raw_in = [sem("raw_in0"), sem("raw_in1")]
        hi_ready = sem("hi_ready")
        lo_ready = sem("lo_ready")
        const_chain = sem("const_chain")
        const_ready = sem("const_ready")
        small_in = sem("small_in")
        ssm_in = sem("ssm_in")
        b_in = sem("b_in")
        ct_in = sem("ct_in")
        dm_in = sem("dm_in")
        dm_ready = sem("dm_ready")
        prep_chain = sem("prep_chain")
        par_ready = sem("par_ready")
        par_turned = sem("par_turned")
        par_copied = sem("par_copied")
        z_ready = sem("z_ready")
        c_turned = sem("c_turned")
        c_copied = sem("c_copied")
        z_turned = sem("z_turned")
        z_copied = sem("z_copied")
        tst_out = [sem(f"tst_out{n}") for n in range(TST)]
        k_done = sem("k_done")
        k_copied = sem("k_copied")
        k_ready = sem("k_ready")
        zero_out = sem("zero_out")
        k_out = sem("k_out")
        wo_ready = sem("wo_ready")
        wo_out = sem("wo_out")
        phase_chain = sem("phase_chain")
        cs_ready = sem("cs_ready")
        cs_out = sem("cs_out")
        x_in = [sem("x_in0"), sem("x_in1")]
        x_turned = sem("x_turned")
        x_copied = sem("x_copied")
        sq_ready = sem("sq_ready")
        sq_added = sem("sq_added")
        rs_ready = sem("rs_ready")
        rinv_ready = sem("rinv_ready")
        hf_ready = sem("hf_ready")
        ahi_ready = sem("ahi_ready")
        alo_ready = sem("alo_ready")
        qk_done = sem("qk_done")
        qk_sq = sem("qk_sq")
        qk_sum = sem("qk_sum")
        qk_root = sem("qk_root")
        qk_inv = sem("qk_inv")
        qk_free = sem("qk_free")
        stg_out = [sem("stg_out0"), sem("stg_out1")]
        v_done = sem("v_done")
        v_copied_a = sem("v_copied_a")
        v_copied_d = sem("v_copied_d")
        vst_out = [sem("vst_out0"), sem("vst_out1")]
        f_w = sem("f_w")
        f_zero = sem("f_zero")
        f_hi = sem("f_hi")
        f_lo = sem("f_lo")
        f_done = sem("f_done")
        f_act = sem("f_act")
        f_min = sem("f_min")
        c_out = sem("c_out")
        v_pad = sem("v_pad")
        mask_ready = sem("mask_ready")
        mask_chain = sem("mask_chain")
        mask_hi = sem("mask_hi")
        qk_in = sem("qk_in")
        v_in = sem("v_in")
        c_in = [sem("c_in0"), sem("c_in1")]
        qk_hi = sem("qk_hi")
        qk_lo = sem("qk_lo")
        v_hi_ready = sem("v_hi_ready")
        v_lo_ready = sem("v_lo_ready")
        s_done = sem("s_done")
        s_biased = sem("s_biased")
        p_ready = sem("p_ready")
        inv_ready = sem("inv_ready")
        diag_ready = sem("diag_ready")
        t_done = sem("t_done")
        pth_ready = sem("pth_ready")
        ptl_ready = sem("ptl_ready")
        pv_done = sem("pv_done")
        ohi_ready = sem("ohi_ready")
        olo_ready = sem("olo_ready")
        oproj_done = sem("oproj_done")
        oproj_free = sem("oproj_free")
        up_done = [sem("up_done0"), sem("up_done1")]
        up_free = [sem("up_free0"), sem("up_free1")]
        hsq_ready = [sem("hsq_ready0"), sem("hsq_ready1")]
        hidh_ready = [sem("hidh_ready0"), sem("hidh_ready1")]
        hidl_ready = [sem("hidl_ready0"), sem("hidl_ready1")]
        down_done = [sem("down_done0"), sem("down_done1")]
        down_free = [sem("down_free0"), sem("down_free1")]
        u_done = sem("u_done")
        u_free = sem("u_free")
        u_out = sem("u_out")
        decay_fill = sem("decay_fill")
        drive_in = [sem("drive_in0"), sem("drive_in1")]
        phase_in = [sem("phase_in0"), sem("phase_in1")]
        out_in = [sem("out_in0"), sem("out_in1")]
        tap_out = sem("tap_out")
        decay_ready = sem("decay_ready")
        drive_done = sem("drive_done")
        scan_chain = sem("scan_chain")
        state_ready = sem("state_ready")
        y_done = sem("y_done")
        gelu_done = sem("gelu_done")
        y_out = sem("y_out")
        z_in = sem("z_in")
        z_hi = sem("z_hi")
        z_lo = sem("z_lo")
        glu_done = sem("glu_done")
        sig_ready = sem("sig_ready")
        glu_free = sem("glu_free")
        glu_added = sem("glu_added")
        out_turned = sem("out_turned")
        out_copied = sem("out_copied")
        y_stored = [sem(f"y_stored{n}") for n in range(OUT)]

        block = ctx.enter_context(nc.Block())

        x_rows = x.rearrange("b t d -> (b t) d")
        out_rows = out.rearrange("b t d -> (b t) d")

        def cols(w, c0):
            return w.rearrange("(k p) f -> p k f", p=P)[:, :, bass.ds(c0, PW)]

        w_in, w_out_, w_sin, w_glu = attn_w_in[0], attn_w_out[0], ssm_w_in[0], ssm_w_glu[0]

        @block.sync
        def _(sp):
            def load(slot, m, src, first=False):
                if not first:
                    sp.wait_ge(lo_ready, 2 * m + slot - 1)
                dst = raw[:, slot, :]
                if len(src.shape) == 3:
                    dst = dst.rearrange("p (k f) -> p k f", k=src.shape[1])
                elif len(src.shape) == 4:
                    dst = dst.rearrange("p (k a f) -> p k a f", k=src.shape[1], a=src.shape[2])
                sp.dma_start(dst, src).then_inc(raw_in[slot], 16)

            sp.dma_start(ldt[:, :], ssm_log_dt[0].rearrange("(g a) -> g a", a=2)).then_inc(ssm_in, 16)
            sp.dma_start(r32[:, 0, :], ssm_a_re[0].rearrange("(g a) p -> g (a p)", a=2)).then_inc(ssm_in, 16)
            sp.dma_start(r32[:, 1, :], ssm_a_im[0].rearrange("(g a) p -> g (a p)", a=2)).then_inc(ssm_in, 16)
            for s in (0, 1):
                sp.dma_start(xs[:, s, :], x_rows[s * P:(s + 1) * P, :]).then_inc(x_in[s], 16)
            for n, b in enumerate((ssm_b_re, ssm_b_im)):
                sp.dma_start(bt[:, n, :, :], b[0].rearrange("(g a) p c -> (a p) g c", a=2)).then_inc(b_in, 16)
            with sp.Fori(0, T // P // 2 - 1) as i:
                for s in (0, 1):
                    sp.wait_ge(x_turned, 4 * i + (2 * s + 2))
                    sp.dma_start(xs[:, s, :], x_rows[bass.ds(i * (2 * P) + (2 + s) * P, P), :])\
                        .then_inc(x_in[s], 16)
            for n, c in enumerate((ssm_c_re, ssm_c_im)):
                for t in range(4):
                    for a in range(2):
                        sp.dma_start(ct[:, n, t, a * NS:(a + 1) * NS],
                                     c[0].rearrange("(t g a) c p -> t a g c p", t=4, a=2)[t, a])\
                            .then_inc(ct_in, 16)
            load(0, 0, cols(w_in, 0), first=True)
            for n in range(2 * GP // 4):
                a, b = n // (GP // 4), n % (GP // 4)
                sp.wait_ge(z_copied, n + 1)
                sp.dma_start(wst_scr[a][:, b * 4 * P:(b + 1) * 4 * P], tst[:, n % TST, :])\
                    .then_inc(tst_out[n % TST], 16)
            sp.wait_ge(wo_ready, 1)
            for a, w in enumerate((wr, wi)):
                sp.dma_start(wo_scr[a], w[:, :, :, :].rearrange("p g s c -> p (g s c)")).then_inc(wo_out, 16)
            sp.wait_ge(cs_ready, 1)
            for a, e in enumerate((er, ei)):
                sp.dma_start(cs_scr[a], e[:, :, :].rearrange("p g j -> p (g j)")).then_inc(cs_out, 16)
            sp.wait_ge(k_ready, 1)
            for r in range(L):
                row = 2 * L - 2 - r
                sp.dma_start(kp_scr[:, :, row * GC:(row + 1) * GC].rearrange("g c w -> c g w"),
                             kall[GC * r:GC * r + GC, :, :, :].rearrange("p g a c -> p (g a) c"))\
                    .then_inc(k_out, 16)
            sp.wait_ge(k_out, 16 * L)
            load(1, 0, cols(w_in, PW), first=True)
            with sp.Fori(1, N_ATT // 2) as m:
                load(0, m, cols(w_in, m * (2 * PW)))
                load(1, m, cols(w_in, m * (2 * PW) + PW))

            sp.wait_ge(k_out, 16 * L)
            sp.wait_ge(zero_out, 16)
            for s in range(L):
                sp.dma_start(tap_scr.rearrange("p (g w) -> p g w", w=P)[GC * s:GC * s + GC],
                             kp_scr[:, :, (L - 1 - s) * GC:(2 * L - 1 - s) * GC].rearrange("g c w -> c g w"))\
                    .then_inc(tap_out, 16)

            def load_qk(p):
                sp.dma_start(q_raw, qk_scr[bass.ds(p * P, P), :]).then_inc(qk_in, 16)
                sp.dma_start(k_raw, qk_scr[bass.ds(p * P + D, P), :]).then_inc(qk_in, 16)

            def load_v(p):
                sp.dma_start(v_raw, v_scr.rearrange("(j k) f -> k j f", k=P)[:, :, bass.ds(p * P, P)])\
                    .then_inc(v_in, 16)

            def load_c(p, h):
                sp.dma_start(cb[:, h, :], c_scr[bass.ds(p * 2 + h, 1), :].to_broadcast((P, T)))\
                    .then_inc(c_in[h], 16)

            for s in (0, 1):
                sp.wait_ge(stg_out[s], 16 * N_QK * 2)
            sp.wait_ge(lo_ready, N_ATT - 1)
            load_qk(0)
            sp.wait_ge(c_out, 16)
            sp.wait_ge(f_min, 4)
            load_c(0, 0)
            load_c(0, 1)
            for s in (0, 1):
                sp.wait_ge(vst_out[s], 16 * N_V * 4)
            sp.wait_ge(lo_ready, N_ATT)
            load_v(0)
            with sp.Fori(1, PAIRS) as p:
                sp.wait_ge(qk_lo, 2 * p)
                sp.wait_ge(v_lo_ready, 2 * p)
                load_qk(p)
                load_v(p)
                for h in range(2):
                    sp.wait_ge(s_biased, 16 * p + (4 * h - 2))
                    load_c(p, h)
            sp.wait_ge(v_lo_ready, 2 * PAIRS)

            load(0, OUT0 // 2, cols(w_out_, 0))
            load(1, OUT0 // 2, cols(w_out_, PW))
            with sp.Fori(1, N_OUT // 2) as i:
                load(0, i + OUT0 // 2, cols(w_out_, i * (2 * PW)))
                load(1, i + OUT0 // 2, cols(w_out_, i * (2 * PW) + PW))

            def mlp_loads(layer, n0):
                with sp.Fori(0, N_MLP // 2) as i:
                    load(0, i + n0 // 2, cols(mlp_w1[layer], i * PW))
                    load(1, i + n0 // 2,
                         mlp_w2[layer].rearrange("(i k p) f -> i p k f", k=2, p=P)[bass.ds(i, 1)].squeeze(0))

            mlp_loads(0, MLP0)
            with sp.Fori(0, N_SIN // 2) as i:
                load(0, i + SIN0 // 2, cols(w_sin, i * (2 * PW)))
                load(1, i + SIN0 // 2, cols(w_sin, i * (2 * PW) + PW))

            def glu_load(slot, i):
                load(slot, i + GLU0 // 2, cols(w_glu, i * PW + slot * D))

            def store_u(tile):
                sp.wait_ge(u_free, 2 * tile + 2 + 4)
                for g in range(GB):
                    sp.dma_start(u_scr.rearrange("(s c) (g j) -> g c s j", c=GC, j=NC)[tile * GB + g],
                                 ust[g * GC:(g + 1) * GC, :, :].rearrange("c h (s j) -> c (h s) j", j=NC))\
                        .then_inc(u_out, 16)

            for slot in (0, 1):
                store_u(2 * slot)
                store_u(2 * slot + 1)
                glu_load(slot, 0)

            for done in tst_out:
                sp.wait_ge(done, 16 * (2 * GP // 4 // TST))
            sp.wait_ge(tap_out, 16 * L)
            sp.wait_ge(wo_out, 32)
            sp.wait_ge(cs_out, 32)

            def load_table(q, s, buf, scr, done):
                sp.dma_start(buf[:, s, :, :], scr.rearrange("a p f -> p a f")[:, :, bass.ds(q * (PB * P), PB * P)])\
                    .then_inc(done, 16)

            def load_states(q, s):
                load_table(q, s, wst, wst_scr, drive_in[s])
                load_table(q, s, cs, cs_scr, phase_in[s])

            def load_rest(q, s):
                if isinstance(q, int):
                    sp.wait_ge(u_out, 16 * GB * (q + 1))
                sp.dma_start(ub[:, s, :, :].rearrange("p g j -> p (g j)"), u_scr[:, bass.ds(q * (GB * NC), GB * NC)])\
                    .then_inc(drive_in[s], 16)
                load_table(q, s, wo, wo_scr, out_in[s])
                sp.dma_start(tap[:, s, :], tap_scr[:, bass.ds(q * (GB * P), GB * P)]).then_inc(out_in[s], 16)

            sp.wait_ge(alo_ready, 3 * NORM)
            for s in (0, 1):
                load_states(s, s)
                load_rest(s, s)
            for tile in range(2 * N_SIN // 2, KT):
                store_u(tile)
            sp.wait_ge(u_out, 16 * GB * KT)
            def next_block(q, s):
                sp.wait_ge(state_ready, 2 * q + (2 + 4))
                load_states(q + 2, s)
                sp.wait_ge(y_done, 2 * q + (2 + 2))
                load_rest(q + 2, s)

            next_block(0, 0)
            with sp.Fori(0, BLK // 2 - 2) as i:
                for s in (1, 0):
                    next_block(2 * i + (2 - s), s)
            next_block(BLK - 3, 1)

            with sp.Fori(1, N_GLU // 2) as i:
                glu_load(0, i)
                glu_load(1, i)
            mlp_loads(1, MLP1)

            with sp.Fori(0, T // P // OUT) as i:
                for s in range(OUT):
                    sp.wait_ge(out_copied, 2 * OUT * i + (2 * s + 2 + 4))
                    sp.dma_start(out_rows[bass.ds(i * (OUT * P) + s * P, P), :], os_[:, s, :])\
                        .then_inc(y_stored[s], 16)
            for s in range(OUT):
                sp.wait_ge(y_stored[s], 16 * T // P // OUT)

        @block.gpsimd
        def _(pool):
            def fill(ins, n):
                ins.then_inc(const_chain, 1)
                pool.wait_ge(const_chain, n)

            fill(pool.memset(ident[:, :], 0.0), 1)
            pool.affine_select(out=ident[:, :], in_=ident[:, :], compare_op=ALU.not_equal, fill=1.0, base=0,
                               pattern=[[-1, P]], channel_multiplier=1).then_inc(const_ready, 1)
            pool.memset(ones[:, :], 1.0).then_inc(const_ready, 1)
            fill(pool.memset(headsum[:, :], 0.0), 2)
            fill(pool.memset(zero[:, :], 0.0), 3)
            pool.memset(eps_t[:, :], EPS).then_inc(const_ready, 1)
            pool.memset(headsum[0:HD, 0:HD], 1.0).then_inc(const_ready, 1)
            pool.wait_ge(const_ready, 4)
            pool.memset(headsum[HD:P, HD:P], 1.0).then_inc(const_ready, 1)
            pool.wait_ge(const_ready, 5)
            with nc.allow_non_contiguous_dma(reason="gains of a few KB"):
                for n, g in enumerate((norm_mix_g[0], norm_mix_g[1], norm_mlp_g[0], norm_mlp_g[1])):
                    pool.dma_start(gains[:, n, :], g.rearrange("(k p) -> p k", p=P)).then_inc(small_in, 16)
                for n, g in enumerate((attn_q_g, attn_k_g)):
                    for h in range(2):
                        pool.dma_start(qk_g[h * HD:(h + 1) * HD, n:n + 1],
                                       g[0].rearrange("(p a) -> p a", a=1)).then_inc(small_in, 16)
                pool.dma_start(fb[:, :], attn_b_f[0].rearrange("(h a) -> h a", a=1)).then_inc(small_in, 16)
            pool.dma_start(dm[96:P, :, :], ssm_d[0].rearrange("(o g c) -> o g c", o=1, c=GC)
                           .to_broadcast((32, NG, GC))).then_inc(dm_in, 16)
            pool.dma_start(kp_scr[:, :, 0:(L - 1) * GC],
                           zero[:, :].unsqueeze(1).to_broadcast((NG, GC, (L - 1) * GC))).then_inc(zero_out, 16)
            pool.wait_ge(dm_in, 16)
            pool.affine_select(out=dm[96:P, :, :], in_=dm[96:P, :, :], compare_op=ALU.is_equal, fill=0.0,
                               base=-GC, pattern=[[0, NG], [-1, GC]], channel_multiplier=1).then_inc(dm_ready, 1)

            chained = [0]

            def chain(ins):
                chained[0] += 1
                ins.then_inc(phase_chain, 1)
                pool.wait_ge(phase_chain, chained[0])

            def product(dst, a, b, op):
                chain(pool.tensor_tensor(dst, a, b, op))

            pool.wait_ge(par_copied, 1)
            pool.wait_ge(dm_ready, 1)
            e_re = er[:, :, :]
            e_im = ei[:, :, :]
            chain(pool.memset(e_re[:, :, 0:1], 1.0))
            chain(pool.memset(e_im[:, :, 0:1], 0.0))
            for n in range(7):
                m = 1 << n
                if n > 0:
                    product(sq_t[:, 0, :], ab[:, 4, :], ab[:, 4, :], ALU.mult)
                    product(sq_t[:, 1, :], ab[:, 5, :], ab[:, 5, :], ALU.mult)
                    product(sq_t[:, 2, :], ab[:, 4, :], ab[:, 5, :], ALU.mult)
                    product(ab[:, 4, :], sq_t[:, 0, :], sq_t[:, 1, :], ALU.subtract)
                    product(ab[:, 5, :], sq_t[:, 2, :], sq_t[:, 2, :], ALU.add)
                pairs = min(GP, 2 * GP * GC // m)
                for g0 in range(0, GP, pairs):
                    gs = slice(g0, g0 + pairs)
                    c_ = ab[:, 4, gs].unsqueeze(2).to_broadcast((P, pairs, m))
                    s_ = ab[:, 5, gs].unsqueeze(2).to_broadcast((P, pairs, m))
                    tp = ept[:, 0:pairs * m].rearrange("p (g j) -> p g j", j=m)
                    old_re, old_im = e_re[:, gs, 0:m], e_im[:, gs, 0:m]
                    new_re, new_im = e_re[:, gs, m:2 * m], e_im[:, gs, m:2 * m]
                    product(tp, old_im, s_, ALU.mult)
                    product(new_re, old_re, c_, ALU.mult)
                    product(new_re, new_re, tp, ALU.subtract)
                    product(tp, old_im, c_, ALU.mult)
                    product(new_im, old_re, s_, ALU.mult)
                    ins = pool.tensor_tensor(new_im, new_im, tp, ALU.add)
                    if n == 6 and g0 + pairs == GP:
                        ins.then_inc(cs_ready, 1)
                    else:
                        chain(ins)

            def norm_lo(n):
                for half in range(2):
                    for k in range(KT):
                        m = KT * half + k
                        mine = slice(half * HALF, (half + 1) * HALF)
                        pool.wait_ge(ahi_ready, NORM * n + m + 1)
                        pool.tensor_tensor(act_lo[:, k, mine], hf[:, m % 4, :], act_hi[:, k, mine].bitcast(F32),
                                           ALU.subtract).then_inc(alo_ready, 1)

            norm_lo(0)
            pool.wait_ge(alo_ready, NORM)
            pool.wait_ge(k_done, 1)
            pool.dma_start(wf[:, :, :], attn_w_in[0].rearrange("(k p) f -> p k f", p=P)[:, :, 3 * D:3 * D + NH])\
                .then_inc(f_w, 16)
            with pool.Fori(0, N_QK // 2) as i:
                for slot in range(2):
                    for g in range(4):
                        m, half = g // 2, g % 2
                        pool.wait_ge(qk_free, 8 * i + 4 * slot + g + 1 + 4)
                        pool.dma_start(qk_scr[bass.ds(i * (4 * P) + (2 * slot + m) * P, P),
                                              half * HALF:(half + 1) * HALF], stg[:, g % 2, :])\
                            .then_inc(stg_out[g % 2], 16)
            pool.wait_ge(f_min, 4)
            pool.dma_start(c_scr, fc[:, :]).then_inc(c_out, 16)

            with pool.Fori(0, N_V // 2) as i:
                for slot in range(2):
                    for t in range(KT):
                        pool.wait_ge((v_copied_a, v_copied_d)[t % 2], 8 * i + 4 * slot + t // 2 + 1 + 2)
                        pool.dma_start(v_scr[t * P:(t + 1) * P, bass.ds(i * (2 * PW) + slot * PW, PW)],
                                       vst[:, t % 2, :]).then_inc(vst_out[t % 2], 16)
            pool.wait_ge(c_out, 16)
            pool.memset(mask_f[:, :], 0.0).then_inc(mask_chain, 1)
            pool.wait_ge(mask_chain, 1)
            pool.affine_select(out=mask_f[:, :], in_=mask_f[:, :], compare_op=ALU.is_ge, fill=MASKED, base=0,
                               pattern=[[-1, P]], channel_multiplier=1).then_inc(mask_ready, 1)

            def diagonals(u, n):
                pool.wait_ge(inv_ready, n)
                pool.tensor_tensor(diag[:, u, :, :], ident[:, :].unsqueeze(1).to_broadcast((P, 4, P)),
                                   inv_sums[:, 4 * u:4 * u + 4].unsqueeze(2).to_broadcast((P, 4, P)), ALU.mult)\
                    .then_inc(diag_ready, 1)

            with pool.Fori(0, PAIRS) as p:
                for u in range(4):
                    diagonals(u, 4 * p + (u + 1))

            def mlp_hidden(layer):
                pool.sem_inc(hidl_ready[layer], 1)
                with pool.Fori(0, N_MLP // 2) as i:
                    for g in range(5):
                        if g < 4:
                            pool.wait_ge(up_free[layer], 4 * i + g + 1 + 4)
                            pool.tensor_tensor(hsq[:, g, :], relu[:, g, :], relu[:, g, :], ALU.mult)\
                                .then_inc(hsq_ready[layer], 1)
                        if g > 0:
                            m, half = (g - 1) % 2, (g - 1) // 2
                            pool.wait_ge(hidh_ready[layer], 4 * i + g)
                            part = slice(half * HALF, (half + 1) * HALF)
                            pool.tensor_tensor(hid_lo[:, m, part], hsq[:, g - 1, :],
                                               hid_hi[:, m, part].bitcast(F32), ALU.subtract)\
                                .then_inc(hidl_ready[layer], 1)

            norm_lo(1)
            mlp_hidden(0)
            norm_lo(2)

            def decay_of(q):
                pool.wait_ge(state_ready, 2 * q + 4)
                pool.tensor_copy(decay[:, :, 1:NC],
                                 ab[:, 6, bass.ds(q * PB, PB)].unsqueeze(2).to_broadcast((P, PB, NC - 1)))\
                    .then_inc(decay_ready, 1)

            def lo_of_z(q):
                pool.wait_ge(z_hi, q + 1)
                pool.tensor_tensor(act_lo[:, bass.ds(q, 1), :].squeeze(1), zt[:, :],
                                   act_hi[:, bass.ds(q, 1), :].squeeze(1).bitcast(F32), ALU.subtract)\
                    .then_inc(z_lo, 1)

            pool.memset(decay[:, :, 0:1], 0.0).then_inc(decay_fill, 1)
            pool.wait_ge(decay_fill, 1)
            pool.sem_inc(z_lo, 1)
            for q in range(4):
                decay_of(q)
            with pool.Fori(0, BLK - 4) as q:
                lo_of_z(q)
                decay_of(q + 4)
            for q in range(BLK - 4, BLK):
                lo_of_z(q)

            norm_lo(3)
            mlp_hidden(1)

        @block.scalar
        def _(act):
            def copy(dst, src):
                return act.activation(dst, src, ACT.Copy)

            def split_hi(slot, m):
                act.wait_ge(raw_in[slot], 16 * m + 16)
                copy(w_hi[:, slot, :], raw[:, slot, :]).then_inc(hi_ready, 1)

            act.sem_inc(x_copied, 4)
            with act.Fori(0, T // P // 2) as i:
                for s in (0, 1):
                    for b in range(2):
                        act.wait_ge(x_turned, 4 * i + 2 * s + b + 1)
                        copy(xT[:, 4 * b:4 * b + 4, bass.ds(i * (2 * P) + s * P, P)],
                             ps[:, 2 * s + b, :].rearrange("p (k t) -> p k t", k=4)).then_inc(x_copied, 1)
            act.wait_ge(par_turned, 1)
            copy(ab[:, 0:7, :], ps[:, 4, 0:7 * GP].rearrange("p (n g) -> p n g", g=GP)).then_inc(par_copied, 1)
            act.wait_ge(c_turned, 1)
            copy(cc[:, 0, :, :], ps[:, 5, :].rearrange("p (g c) -> p g c", c=GC)).then_inc(c_copied, 1)
            act.activation(cc[:, 1, :, :], ps[:, 6, :].rearrange("p (g c) -> p g c", c=GC), ACT.Copy,
                           scale=-1.0).then_inc(c_copied, 1)
            def norm_steps(n, chunked=False):
                def square(m):
                    if m >= 4:
                        act.wait_ge(sq_added, NORM * n + m - 3)
                    act.activation(as_tokens(sq[:, m % 4, :], chunked), tokens(xT[:, m % KT, :], m // KT, chunked),
                                   ACT.Square).then_inc(sq_ready, 1)

                def root(half):
                    act.wait_ge(sq_added, NORM * n + KT * (half + 1))
                    act.activation(rs[:, half * HALF:(half + 1) * HALF], ps[:, half, :], ACT.Sqrt,
                                   bias=eps_t[:, 0:1], scale=1.0 / D).then_inc(rs_ready, 1)

                def hi(m):
                    act.wait_ge(hf_ready, NORM * n + m + 1)
                    copy(act_hi[:, m % KT, m // KT * HALF:(m // KT + 1) * HALF], hf[:, m % 4, :])\
                        .then_inc(ahi_ready, 1)

                def sum_squares():
                    for m in range(KT + 3):
                        square(m)
                    root(0)
                    for m in range(KT + 3, NORM):
                        square(m)

                return sum_squares, root, hi

            def norm(n, chunked=False):
                sum_squares, root, hi = norm_steps(n, chunked)
                sum_squares()
                for m in range(NORM):
                    if m == 2:
                        root(1)
                    hi(m)

            act.wait_ge(const_ready, 5)
            act.wait_ge(x_copied, 4 + 2 * KT)
            sum_squares, root, hi = norm_steps(0)
            sum_squares()
            root(1)
            for n in range(2 * GP // 4):
                act.wait_ge(z_turned, n + 1)
                if n >= TST:
                    act.wait_ge(tst_out[n % TST], 16 * (n // TST))
                copy(tst[:, n % TST, :], ps[:, (7, 4)[n % 2], :]).then_inc(z_copied, 1)
            for stored in tst_out:
                act.wait_ge(stored, 16 * (2 * GP // 4 // TST))
            act.wait_ge(wo_out, 32)
            for m in range(NORM):
                if m == 4:
                    act.wait_ge(cs_out, 32)
                    split_hi(0, 0)
                hi(m)
            act.wait_ge(k_done, 1)
            for a in range(2):
                copy(kall[:, :, a, :], ps[:, 5 + a, :].rearrange("p (g c) -> p g c", c=GC)).then_inc(k_copied, 1)

            act.wait_ge(alo_ready, NORM)
            act.wait_ge(f_w, 16)
            act.wait_ge(f_zero, 2)
            copy(wf_hi[:, :, 0:NH], wf[:, :, :]).then_inc(f_hi, 1)
            with act.Fori(0, N_QK // 2) as i:
                for slot in range(2):
                    split_hi(1 - slot, i + slot)
                    for g in range(5):
                        if g < 4:
                            act.wait_ge(qk_done, 8 * i + 4 * slot + g + 1)
                            act.activation(sqh[:, g, :], ps[:, g, :], ACT.Square).then_inc(qk_sq, 1)
                        if g > 0:
                            act.wait_ge(qk_sum, 8 * i + 4 * slot + g)
                            act.activation(rsh[:, g - 1, :], ps[:, 4 + g - 1, :], ACT.Sqrt,
                                           bias=eps_t[:, 0:1], scale=1.0 / HD).then_inc(qk_root, 1)
            act.wait_ge(f_done, 1)
            act.activation(fy[:, :].rearrange("p (h t) -> p h t", h=2), ps[0:NH, 4:6, :], ACT.Identity,
                           bias=fb[:, 0:1]).then_inc(f_act, 1)
            act.wait_ge(f_act, 1)
            act.activation(fe[:, :], fy[:, :], ACT.Abs).then_inc(f_act, 1)
            act.wait_ge(f_act, 2)
            act.activation(fl[:, :], fe[:, :], ACT.Exp, scale=-1.0).then_inc(f_act, 1)
            act.wait_ge(f_act, 3)
            act.activation(fe[:, :], fl[:, :], ACT.Ln, bias=1.0).then_inc(f_act, 1)

            act.sem_inc(v_copied_a, 2)
            for i in range(N_V // 2):
                for slot in range(2):
                    act.wait_ge(v_done, 16 * i + 8 * slot)
                    if i + slot < N_V // 2:
                        split_hi(1 - slot, N_QK // 2 + i + slot)
                    for t in range(0, KT, 2):
                        act.wait_ge(v_done, 16 * i + 8 * slot + t + 1)
                        if i + slot + t > 0:
                            act.wait_ge(vst_out[0], 16 * (8 * i + 4 * slot + t // 2))
                        copy(vst[:, 0, :], ps[:, t % 4, 0:PW]).then_inc(v_copied_a, 1)
            act.wait_ge(mask_ready, 1)
            copy(mask[:, :], mask_f[:, :]).then_inc(mask_hi, 1)
            copy(ident_r[:, :], ident[:, :]).then_inc(mask_hi, 1)
            act.wait_ge(v_pad, 4)

            def attend(order, pair, parity):
                for kind, u, n in order:
                    if kind == "QK":
                        nxt = 0 if pair is START else 1
                        act.wait_ge(qk_in, pair(32, 32 * nxt + 32))
                        act.wait_ge(s_biased, pair(16, 16 * nxt + 2))
                        copy(q_hi, q_raw).then_inc(qk_hi, 1)
                        copy(k_hi, k_raw).then_inc(qk_hi, 1)
                    elif kind in ("V0", "V1"):
                        h = 0 if kind == "V0" else 1
                        nxt = 1 if h == 0 and pair is not START else 0
                        act.wait_ge(v_in, pair(16, 16 * nxt + 16))
                        act.wait_ge(pv_done, pair(24, (16 * nxt if h == 0 else 0) + T_SLOTS))
                        copy(v_hi[:, h, :, h * HD:(h + 1) * HD], v_raw[:, :, h * HD:(h + 1) * HD])\
                            .then_inc(v_hi_ready, 1)
                    elif kind == "E":
                        act.wait_ge(s_biased, pair(16, 4 * u + n + 1 + 2))
                        b = (4 * u + n) % 16
                        probs = prob_of(u, parity)[:, n, 0:keys_of(u, n)]
                        act.activation(probs, probs, ACT.Exp, bias=mx[:, b:b + 1], scale=-1.0,
                                       accum_out=sums[:, b:b + 1]).then_inc(p_ready, 1)
                    elif kind == "T":
                        t = TILES_BEFORE[u] + n
                        act.wait_ge(t_done, pair(24, t + 1))
                        act.wait_ge(pv_done, pair(24, t + 1))
                        copy(pt_hi[:, t % T_SLOTS, first_col(u, n):HALF], ps[:, T_BANKS[t % T_SLOTS],
                                                                            first_col(u, n):HALF])\
                            .then_inc(pth_ready, 1)
                    elif kind == "O":
                        act.wait_ge(pv_done, pair(24, (0, 8, 24)[u + 1] + T_SLOTS))
                        copy(output_of(act_hi, u, pair), ps[:, V_BANK, :]).then_inc(ohi_ready, 1)

            attend(attention_start(), START, 0)
            attend(attention_order(first=True), FIRST, 0)
            with act.Fori(0, PAIRS // 2 - 1) as i:
                for parity in (1, 0):
                    attend(attention_order(), inner(i, parity), parity)
            attend(attention_order(last=True), LAST, 1)

            act.wait_ge(pv_done, 24 * PAIRS + T_SLOTS)
            def proj_splits(panel0, count):
                with act.Fori(0, count // 2) as i:
                    act.wait_ge(oproj_done, 8 * i + 1)
                    split_hi(1, i + panel0 // 2)
                    act.wait_ge(oproj_done, 8 * i + 5)
                    split_hi(0, i + panel0 // 2 + 1)

            split_hi(0, OUT0 // 2)
            proj_splits(OUT0, N_OUT)

            def mlp(layer, panel0, last):
                def step(i, more):
                    act.wait_ge(down_done[layer], 16 * i + 1)
                    split_hi(1, i + panel0 // 2)
                    for g in range(5):
                        if g < 4:
                            act.wait_ge(up_done[layer], 4 * i + g + 1)
                            act.wait_ge(hidl_ready[layer], 4 * i + 1)
                            act.activation(relu[:, g, :], ps[:, g, :], ACT.Relu).then_inc(up_free[layer], 1)
                        if g > 0:
                            m, half = (g - 1) % 2, (g - 1) // 2
                            act.wait_ge(hsq_ready[layer], 4 * i + g)
                            act.wait_ge(down_done[layer], 16 * i + 1)
                            copy(hid_hi[:, m, half * HALF:(half + 1) * HALF], hsq[:, g - 1, :])\
                                .then_inc(hidh_ready[layer], 1)
                    if more:
                        split_hi(0, i + panel0 // 2 + 1)
                if last:
                    with act.Fori(0, N_MLP // 2 - 1) as i:
                        step(i, True)
                    step(N_MLP // 2 - 1, False)
                else:
                    with act.Fori(0, N_MLP // 2) as i:
                        step(i, True)

            act.wait_ge(oproj_free, 4 + 4 * N_OUT)
            act.sem_inc(up_free[0], 4)
            norm(1)
            act.wait_ge(alo_ready, 2 * NORM)
            mlp(0, MLP0, last=False)

            act.wait_ge(down_free[0], 4 + 16 * N_MLP // 2)
            act.sem_inc(u_free, 4)
            norm(2, chunked=True)
            act.wait_ge(alo_ready, 3 * NORM)
            for i in range(N_SIN // 2):
                for slot in range(2):
                    split_hi(1 - slot, i + (SIN0 // 2 + slot))
                    for g in range(4):
                        act.wait_ge(u_done, 8 * i + 4 * slot + g + 1)
                        if 4 * i + 2 * slot + g // 2 > 0:
                            act.wait_ge(u_out, 16 * GB * (4 * i + 2 * slot + g // 2))
                        copy(ust[:, g % 2, :], ps[:, g, :]).then_inc(u_free, 1)
            act.sem_inc(gelu_done, 4)

            def block_out(q, s):
                if not (isinstance(q, int) and q == 0):
                    act.wait_ge(y_out, 16 * q)
                for b in range(2):
                    act.wait_ge(y_done, 2 * q + (b + 1 + 2))
                    act.activation(yb[:, :, :].rearrange("p (c a) j -> p a c j", a=2)[:, b, :, :],
                                   ps[:, 4 + 2 * s + b, :].rearrange("p (g j) -> p g j", g=PB),
                                   ACT.Gelu_apprx_tanh).then_inc(gelu_done, 1)
                act.wait_ge(gelu_done, 2 * q + (2 + 4))
                act.dma_start(y_scr[:, bass.ds(q * (GB * NC), GB * NC)], yb[:, :, :].rearrange("p g j -> p (g j)"))\
                    .then_inc(y_out, 16)

            def hi_of_z(q):
                act.wait_ge(z_in, q * (16 * GB) + 16 * GB)
                copy(act_hi[:, bass.ds(q, 1), :].squeeze(1), zt[:, :]).then_inc(z_hi, 1)

            def load_z(q):
                act.wait_ge(y_out, 16 * q + 16)
                act.wait_ge(z_lo, q + 1)
                for g in range(GB):
                    act.dma_start(zt[g * GC:(g + 1) * GC, :].rearrange("c (s j) -> c s j", s=L),
                                 y_scr.rearrange("(s c) (g j) -> g c s j", c=GC, j=NC)[bass.ds(q * GB + g, 1)].squeeze(0))\
                        .then_inc(z_in, 16)

            block_out(0, 0)
            block_out(1, 1)
            load_z(0)
            with act.Fori(0, BLK // 2 - 1) as i:
                for s in (0, 1):
                    block_out(2 * i + (2 + s), s)
                    hi_of_z(2 * i + s)
                    load_z(2 * i + (1 + s))
            hi_of_z(BLK - 2)
            load_z(BLK - 1)
            hi_of_z(BLK - 1)
            with act.Fori(0, N_GLU // 2) as i:
                for slot in range(2):
                    if slot == 1:
                        act.wait_ge(glu_done, 8 * i + 4)
                    split_hi(1 - slot, i + (GLU0 // 2 + slot))
                    if slot == 1:
                        for g in range(4):
                            act.wait_ge(glu_done, 8 * i + g + 5)
                            act.wait_ge(glu_free, 4 * i + g + 1)
                            act.activation(sig[:, g, :], ps[:, 4 + g, :], ACT.Sigmoid).then_inc(sig_ready, 1)
            act.wait_ge(glu_added, 2 * N_GLU + 1)
            act.sem_inc(up_free[1], 4)
            norm(3)
            act.wait_ge(alo_ready, 4 * NORM)
            mlp(1, MLP1, last=True)

            act.sem_inc(out_copied, 4)
            for t in range(T // P):
                if t >= OUT:
                    act.wait_ge(y_stored[t % OUT], 16 * (t // OUT))
                for b in range(2):
                    act.wait_ge(out_turned, 2 * t + b + 1)
                    copy(os_[:, t % OUT, b * HALF:(b + 1) * HALF], ps[:, 2 * (t % 2) + b, :]).then_inc(out_copied, 1)

        @block.tensor
        def _(pe):
            def times(dst, w1, w2, a1, a2, start, stop):
                pe.matmul(dst, w1, a1, start=start, stop=False)
                pe.matmul(dst, w1, a2, start=False, stop=False)
                return pe.matmul(dst, w2, a1, start=False, stop=stop)

            def project(bank, slot, col, half, ready=None, n=0):
                tok = slice(half * HALF, (half + 1) * HALF)
                for k in range(KT):
                    if ready is not None:
                        pe.wait_ge(ready, n + k + 1)
                    last = times(ps[:, bank, :], w_hi8[:, slot, k, col:col + P], w_lo8[:, slot, k, col:col + P],
                                 act_hi[:, k, tok], act_lo[:, k, tok], k == 0, k == KT - 1)
                return last

            pe.wait_ge(const_ready, 1)
            with pe.Fori(0, T // P // 2) as i:
                for s in (0, 1):
                    pe.wait_ge(x_in[s], 16 * i + 16)
                    for b in range(2):
                        pe.wait_ge(x_copied, 4 * i + 2 * s + b + 1)
                        for k in range(4):
                            last = pe.transpose(ps[:, 2 * s + b, k * P:(k + 1) * P],
                                                xs[:, s, (4 * b + k) * P:(4 * b + k + 1) * P], ident[:, :])
                        last.then_inc(x_turned, 1)
            pe.wait_ge(par_ready, 1)
            for n in range(7):
                last = pe.transpose(ps[:, 4, n * GP:(n + 1) * GP], r32[:, 2 + n, :], ident[0:GP, 0:GP])
            last.then_inc(par_turned, 1)
            pe.wait_ge(ct_in, 16 * 16)
            for a in range(2):
                for t in range(4):
                    last = pe.transpose(ps[:, 5 + a, t * P:(t + 1) * P], ct[:, a, t, :], ident[:, :])
            last.then_inc(c_turned, 1)
            def norm(n):
                for m in range(NORM):
                    pe.wait_ge(sq_ready, NORM * n + m + 1)
                    pe.matmul(ps[:, m // KT, :], ones[:, :], sq[:, m % 4, :], start=(m % KT == 0),
                              stop=(m % KT == KT - 1)).then_inc(sq_added, 1)

            def second_half(n):
                pe.wait_ge(alo_ready, NORM * n + NORM)

            norm(0)
            pe.wait_ge(z_ready, 1)
            pe.wait_ge(par_copied, 1)
            for n in range(2 * GP // 4):
                z = (zr, zi)[n // (GP // 4)]
                if n >= 2:
                    pe.wait_ge(z_copied, n - 1)
                for b in range(4):
                    last = pe.transpose(ps[:, (7, 4)[n % 2], b * P:(b + 1) * P],
                                        z[:, 4 * (n % (GP // 4)) + b, :, :].rearrange("p s c -> p (s c)"), ident[:, :])
                last.then_inc(z_turned, 1)
            pe.wait_ge(c_copied, 2)
            for a in range(2):
                rows = slice(a * NS, (a + 1) * NS)
                for g in range(GP):
                    dst = ps[:, 5 + a, g * GC:(g + 1) * GC]
                    pe.matmul(dst, zr[rows, g, :, :].rearrange("p s c -> p (s c)"), cc[rows, 0, g, :],
                              start=True, stop=False)
                    last = pe.matmul(dst, zi[rows, g, :, :].rearrange("p s c -> p (s c)"), cc[rows, 1, g, :],
                                     start=False, stop=True)
            last.then_inc(k_done, 1)

            pe.wait_ge(z_copied, 2 * GP // 4)
            pe.wait_ge(k_copied, 2)
            pe.wait_ge(const_ready, 5)
            with pe.Fori(0, N_QK // 2) as i:
                for slot in range(2):
                    pe.wait_ge(lo_ready, 2 * i + slot + 1)
                    for g in range(5):
                        if g < 4:
                            pe.wait_ge(qk_free, 8 * i + 4 * slot + g + 1)
                            if g == 1:
                                pe.wait_ge(rs_ready, 2)
                                second_half(0)
                            project(g, slot, g // 2 * P, g % 2, alo_ready if g == 0 else None).then_inc(qk_done, 1)
                        if g > 0:
                            pe.wait_ge(qk_sq, 8 * i + 4 * slot + g)
                            pe.matmul(ps[:, 4 + g - 1, :], headsum[:, :], sqh[:, g - 1, :],
                                      start=True, stop=True).then_inc(qk_sum, 1)
            pe.wait_ge(qk_root, 4 * N_QK)
            pe.wait_ge(f_lo, 1)
            for half in range(2):
                tok = slice(half * HALF, (half + 1) * HALF)
                for k in range(KT):
                    last = times(ps[:, 4 + half, :], wf_hi[:, k, :], wf_lo[:, k, :], act_hi[:, k, tok],
                                 act_lo[:, k, tok], k == 0, k == KT - 1)
            last.then_inc(f_done, 1)

            pe.wait_ge(qk_free, 4 * N_QK + 4)
            with pe.Fori(0, N_V // 2) as i:
                for slot in range(2):
                    pe.wait_ge(lo_ready, 2 * i + (N_QK + slot + 1))
                    for t in range(KT):
                        pe.wait_ge((v_copied_a, v_copied_d)[t % 2], 8 * i + 4 * slot + t // 2 + 1)
                        dst = ps[:, t % 4, 0:PW]
                        tok = slice(t * P, (t + 1) * P)
                        for k in range(KT):
                            last = times(dst, act_hi[:, k, tok], act_lo[:, k, tok], w_hi8[:, slot, k, :],
                                         w_lo8[:, slot, k, :], k == 0, k == KT - 1)
                        last.then_inc(v_done, 1)
            pe.wait_ge(f_act, 1)
            pe.wait_ge(v_copied_a, 2 + 4 * N_V)
            pe.wait_ge(v_copied_d, 2 + 4 * N_V)
            pe.wait_ge(mask_hi, 2)
            pe.sem_inc(pv_done, T_SLOTS)

            def attend(order, pair, parity):
                for kind, u, n in order:
                    if kind == "S":
                        b = 4 * u + n
                        rows = slice(u % 2 * HD, (u % 2 + 1) * HD)
                        i = 4 * (u % 4 // 2) + n
                        mine = slice(i * P, (i + 1) * P)
                        if n == 0 and u in (0, 4):
                            pe.wait_ge(qk_lo, pair(2, 2 if u == 0 else 4))
                        pe.wait_ge(s_biased, pair(16, b + 1))
                        keys = (i + 1) * P
                        for k0 in range(0, keys, HALF):
                            k1 = min(keys, k0 + HALF)
                            times(ps[:, 2 * (b % 2) + k0 // HALF, 0:k1 - k0], q_hi[rows, mine],
                                  q_lo[rows, mine], k_hi[rows, k0:k1], k_lo[rows, k0:k1], True, k1 < keys)
                        pe.matmul(ps[:, 2 * (b % 2) + k0 // HALF, i * P - k0:k1 - k0], ident_r[:, :],
                                  mask[:, :], start=False, stop=True).then_inc(s_done, 1)
                    elif kind == "T":
                        t = TILES_BEFORE[u] + n
                        if n == 0:
                            pe.wait_ge(diag_ready, pair(4, u + 1))
                        pe.wait_ge(ptl_ready, pair(24, t + 1))
                        for m in range(first_col(u, n) // P, 4):
                            last = pe.matmul(ps[:, T_BANKS[t % T_SLOTS], m * P:(m + 1) * P],
                                             prob_of(u, parity)[:, m, n * P:(n + 1) * P], diag[:, u, m, :],
                                             start=True, stop=True)
                        last.then_inc(t_done, 1)
                    elif kind == "V":
                        t = u % 24
                        uu = max(k for k in range(4) if TILES_BEFORE[k] <= t)
                        j = t - TILES_BEFORE[uu]
                        h, lo = uu % 2, first_col(uu, j)
                        if j == 0:
                            pe.wait_ge(v_lo_ready, pair(2, h + 1))
                            if h == 0:
                                pe.wait_ge(olo_ready, pair(2, uu // 2 + 1))
                        pe.wait_ge(ptl_ready, pair(24, u + 1 + T_SLOTS))
                        times(ps[:, V_BANK, lo:HALF], v_hi[:, h, j, :], v_lo[:, h, j, :],
                              pt_hi[:, t % T_SLOTS, lo:HALF], pt_lo[:, t % T_SLOTS, lo:HALF],
                              h == 0 and j == 0, h == 1 and j == key_tiles(uu) - 1).then_inc(pv_done, 1)

            attend(attention_start(), START, 0)
            attend(attention_order(first=True), FIRST, 0)
            with pe.Fori(0, PAIRS // 2 - 1) as i:
                for parity in (1, 0):
                    attend(attention_order(), inner(i, parity), parity)
            attend(attention_order(last=True), LAST, 1)

            pe.wait_ge(olo_ready, 2 * PAIRS + 1)
            pe.wait_ge(s_biased, 16 * PAIRS + 2)

            def project_panels(count, panel0, done, free, n=None):
                with pe.Fori(0, count // 2) as i:
                    for slot in range(2):
                        pe.wait_ge(lo_ready, 2 * i + (panel0 + slot + 1))
                        for g in range(4):
                            pe.wait_ge(free, 8 * i + 4 * slot + g + 1)
                            if g == 1 and n is not None:
                                second_half(n)
                            project(g, slot, g // 2 * P, g % 2, alo_ready if g == 0 and n is not None else None,
                                    NORM * (n or 0)).then_inc(done, 1)

            pe.sem_inc(oproj_done, 1)
            project_panels(N_OUT, OUT0, oproj_done, oproj_free)

            def mlp(layer, panel0):
                pe.sem_inc(down_done[layer], 1)
                with pe.Fori(0, N_MLP // 2) as i:
                    pe.wait_ge(lo_ready, 2 * i + (panel0 + 1))
                    for g in range(4):
                        pe.wait_ge(up_free[layer], 4 * i + g + 1)
                        if g == 2:
                            second_half(1 + 2 * layer)
                        project(g, 0, g % 2 * P, g // 2, alo_ready if g == 0 else None, NORM * (1 + 2 * layer))\
                            .then_inc(up_done[layer], 1)
                    pe.wait_ge(lo_ready, 2 * i + (panel0 + 2))
                    for half in range(2):
                        pe.wait_ge(hidl_ready[layer], 4 * i + (2 * half + 2 + 1))
                        tok = slice(half * HALF, (half + 1) * HALF)
                        for f in range(KT):
                            q = KT * half + f
                            pe.wait_ge(down_free[layer], 16 * i + q + 1)
                            for k in range(2):
                                last = times(ps[:, 4 + q % 4, :], w_hi2[:, 1, k, f * P:(f + 1) * P],
                                             w_lo2[:, 1, k, f * P:(f + 1) * P], hid_hi[:, k, tok],
                                             hid_lo[:, k, tok], k == 0, k == 1)
                            last.then_inc(down_done[layer], 1)

            pe.wait_ge(oproj_free, 4 + 4 * N_OUT)
            norm(1)
            pe.wait_ge(rs_ready, 4)
            mlp(0, MLP0)
            pe.wait_ge(down_free[0], 4 + 16 * N_MLP // 2)
            norm(2)
            pe.wait_ge(rs_ready, 6)
            project_panels(N_SIN, SIN0, u_done, u_free, n=2)

            pe.wait_ge(u_free, 4 + 4 * N_SIN)
            pe.sem_inc(y_done, 2)

            def drive(n, q, s):
                pe.wait_ge(drive_in[s], 32 * n + 32)
                pe.wait_ge(state_ready, 2 * q + 2)
                for c in range(PB):
                    for a in range(2):
                        rows = slice(a * NS, (a + 1) * NS)
                        for n in range(2):
                            last = pe.matmul(ps[rows, 2 * s + n, c * NC:(c + 1) * NC],
                                             wst[:, s, n, c * P + a * NS:c * P + (a + 1) * NS],
                                             ub[:, s, 2 * c + a, :], start=True, stop=True)
                last.then_inc(drive_done, 1)

            def from_inputs(n, q, s):
                pe.wait_ge(gelu_done, 2 * q + 2)
                pe.wait_ge(out_in[s], 32 * n + 32)
                for a in range(2):
                    for c in range(PB):
                        g = 2 * c + a
                        pe.matmul(ps[:, 4 + 2 * s + a, c * NC:(c + 1) * NC], tap[:, s, g * P:(g + 1) * P],
                                  ub[:, s, g, :], start=(c == 0), stop=False)

            def from_states(q, s):
                pe.wait_ge(state_ready, 2 * q + (2 + 4))
                for a in range(2):
                    rows = slice(a * NS, (a + 1) * NS)
                    for c in range(PB):
                        c0 = c * NC
                        for n in range(2):
                            last = pe.matmul(ps[:, 4 + 2 * s + a, c0 + 1:c0 + NC], wo[rows, s, n, c * P:(c + 1) * P],
                                             xb[rows, n, c0:c0 + NC - 1], start=False, stop=(n == 1 and c == PB - 1))
                    last.then_inc(y_done, 1)

            drive(0, 0, 0)
            drive(0, 1, 1)
            from_inputs(0, 0, 0)
            from_states(0, 0)
            with pe.Fori(0, BLK // 2 - 1) as i:
                for s in (1, 0):
                    from_inputs(i + (1 - s), 2 * i + (2 - s), s)
                    drive(i + 1, 2 * i + (3 - s), 1 - s)
                    from_states(2 * i + (2 - s), s)
            from_inputs(BLK // 2 - 1, BLK - 1, 1)
            from_states(BLK - 1, 1)

            with pe.Fori(0, N_GLU // 2) as i:
                for slot in range(2):
                    pe.wait_ge(lo_ready, 2 * i + (GLU0 + slot + 1))
                    for g in range(4):
                        pe.wait_ge(glu_free, 4 * i + g + 1)
                        project(4 * slot + g, slot, g // 2 * P, g % 2, z_lo if slot == 0 and g == 0 else None, 1)\
                            .then_inc(glu_done, 1)
            pe.wait_ge(glu_free, 4 + 2 * N_GLU)
            norm(3)
            pe.wait_ge(rs_ready, 8)
            mlp(1, MLP1)

            for t in range(T // P):
                if t % (KT // 2) == 0:
                    pe.wait_ge(down_free[1], 4 + 16 * N_MLP // 2 - (KT if t == 0 else 0))
                for b in range(2):
                    pe.wait_ge(out_copied, 2 * t + b + 1)
                    for k in range(4):
                        last = pe.transpose(ps[:, 2 * (t % 2) + b, k * P:(k + 1) * P],
                                            xT[:, 4 * b + k, t * P:(t + 1) * P], ident[:, :])
                    last.then_inc(out_turned, 1)

        @block.vector
        def _(dve):
            done = [0]

            def link(ins):
                done[0] += 1
                ins.then_inc(prep_chain, 1)
                dve.wait_ge(prep_chain, done[0])

            def ts(out_, in_, s1, s2, op0, op1=None):
                if op1 is None:
                    link(dve.tensor_scalar(out_, in_, s1, None, op0))
                else:
                    link(dve.tensor_scalar(out_, in_, s1, s2, op0, op1))

            def tt(out_, a, b, op):
                link(dve.tensor_tensor(out_, a, b, op))

            def stt(out_, a, s, b, op0, op1):
                link(dve.scalar_tensor_tensor(out=out_, in0=a, scalar=s, in1=b, op0=op0, op1=op1))

            row = lambda n: r32[:, n, :]
            A_RE, A_IM = row(0), row(1)
            OUT = [row(2 + n) for n in range(7)]
            AB_RE, AB_IM, S_RE, S_IM, PH_C, PH_S, DECAY = OUT
            dt, mag, t0, t1, t2, t3, t4, co, si = (row(9 + n) for n in range(9))

            def exp(dst, src, n, r, y, w):
                dst, src, n, r, y = (v[:, 0:w] for v in (dst, src, n, r, y))
                ts(src, src, 172.0, -172.0, ALU.min, ALU.max)
                ts(n, src, LOG2E, ROUND, ALU.mult, ALU.add)
                ts(n, n, ROUND, None, ALU.subtract)
                stt(r, n, -LN2[0], src, ALU.mult, ALU.add)
                stt(r, n, -LN2[1], r, ALU.mult, ALU.add)
                ts(y, r, EXP_POLY[0], None, ALU.mult)
                for c in EXP_POLY[1:] + (1.0,):
                    stt(y, y, c, r, ALU.add, ALU.mult)
                ts(y, y, 1.0, None, ALU.add)
                ts(r, n, 0.5, ROUND, ALU.mult, ALU.add)
                ts(r, r, ROUND, None, ALU.subtract)
                tt(n, n, r, ALU.subtract)
                ts(i32[:, 0, 0:w], r, 127.0, float(1 << 23), ALU.add, ALU.mult)
                ts(i32[:, 1, 0:w], n, 127.0, float(1 << 23), ALU.add, ALU.mult)
                tt(y, y, i32[:, 0, 0:w].bitcast(F32), ALU.mult)
                tt(dst, y, i32[:, 1, 0:w].bitcast(F32), ALU.mult)

            dve.wait_ge(ssm_in, 48)
            link(dve.tensor_copy(t4[:, 0:2], ldt[:, :]))
            exp(t3, t4, t0, t1, t2, 2)
            link(dve.tensor_copy(dt.rearrange("g (a p) -> g a p", a=2),
                                 t3[:, 0:2].unsqueeze(2).to_broadcast((GP, 2, NS))))
            tt(t4, dt, A_RE, ALU.mult)
            exp(mag, t4, t0, t1, t2, P)
            tt(t0, dt, A_IM, ALU.mult)
            ts(t1, t0, 1.0 / (2.0 * PI), ROUND, ALU.mult, ALU.add)
            ts(t1, t1, ROUND, None, ALU.subtract)
            for c in TWO_PI:
                stt(t0, t1, -c, t0, ALU.mult, ALU.add)
            ts(t0, t0, 0.25, None, ALU.mult)
            tt(t1, t0, t0, ALU.mult)
            ts(t2, t1, SIN_POLY[0], SIN_POLY[1], ALU.mult, ALU.add)
            tt(t2, t2, t1, ALU.mult)
            ts(t2, t2, SIN_POLY[2], None, ALU.add)
            tt(t2, t2, t1, ALU.mult)
            stt(si, t2, 1.0, t0, ALU.add, ALU.mult)
            ts(t2, t1, COS_POLY[0], COS_POLY[1], ALU.mult, ALU.add)
            tt(t2, t2, t1, ALU.mult)
            ts(t2, t2, COS_POLY[2], None, ALU.add)
            tt(t2, t2, t1, ALU.mult)
            stt(co, t2, -0.5, t1, ALU.add, ALU.mult)
            for _ in range(2):
                tt(t2, si, si, ALU.mult)
                stt(si, co, 1.0, si, ALU.add, ALU.mult)
                ts(si, si, 2.0, None, ALU.mult)
                ts(co, t2, -2.0, None, ALU.mult)
            ts(co, co, 1.0, None, ALU.add)
            tt(AB_RE, mag, co, ALU.mult)
            tt(AB_IM, mag, si, ALU.mult)
            ts(t0, AB_RE, 1.0, None, ALU.subtract)
            tt(t1, A_RE, A_RE, ALU.mult)
            tt(t2, A_IM, A_IM, ALU.mult)
            tt(t1, t1, t2, ALU.add)
            link(dve.reciprocal(t1, t1))
            tt(t2, t0, A_RE, ALU.mult)
            tt(t3, AB_IM, A_IM, ALU.mult)
            tt(t2, t2, t3, ALU.add)
            tt(S_RE, t2, t1, ALU.mult)
            tt(t2, AB_IM, A_RE, ALU.mult)
            tt(t3, t0, A_IM, ALU.mult)
            tt(t2, t2, t3, ALU.subtract)
            tt(S_IM, t2, t1, ALU.mult)
            for n in range(3):
                tt(DECAY if n == 2 else t4, mag if n == 0 else t4, mag if n == 0 else t4, ALU.mult)
            for n in range(3):
                c_, s_ = (co, si) if n == 0 else (PH_C, PH_S)
                tt(t0, c_, c_, ALU.mult)
                tt(t1, s_, s_, ALU.mult)
                tt(t2, c_, s_, ALU.mult)
                tt(PH_C, t0, t1, ALU.subtract)
                if n < 2:
                    ts(PH_S, t2, 2.0, None, ALU.mult)
            dve.tensor_scalar(PH_S, t2, 2.0, None, ALU.mult).then_inc(par_ready, 1)

            dve.wait_ge(par_copied, 1)
            over_c = lambda n: ab[:, n, :].unsqueeze(2).to_broadcast((P, GP, GC))
            tmp = pt[:, :, :]

            def cmul(o_re, o_im, a_re, a_im, b_re, b_im, last=None):
                tt(tmp, a_im, b_im, ALU.mult)
                tt(o_re, a_re, b_re, ALU.mult)
                tt(o_re, o_re, tmp, ALU.subtract)
                tt(tmp, a_im, b_re, ALU.mult)
                tt(o_im, a_re, b_im, ALU.mult)
                ins = dve.tensor_tensor(o_im, o_im, tmp, ALU.add)
                if last is None:
                    link(ins)
                else:
                    ins.then_inc(last, 1)

            dve.wait_ge(b_in, 32)
            b_re, b_im = bt[:, 0, :, :], bt[:, 1, :, :]
            cmul(zr[:, :, L - 1, :], zi[:, :, L - 1, :], b_re, b_im, over_c(2), over_c(3))
            for r in range(L - 2, -1, -1):
                cmul(zr[:, :, r, :], zi[:, :, r, :], zr[:, :, r + 1, :], zi[:, :, r + 1, :], over_c(0), over_c(1),
                     last=z_ready if r == 0 else None)

            dve.wait_ge(z_ready, 1)
            dve.wait_ge(c_copied, 2)
            for s in range(L):
                c_re, c_ni = (cc[:, 0, :, :], cc[:, 1, :, :]) if s == 0 else (wr[:, :, s - 1, :], wi[:, :, s - 1, :])
                tt(tmp, c_ni, over_c(1), ALU.mult)
                tt(wr[:, :, s, :], c_re, over_c(0), ALU.mult)
                tt(wr[:, :, s, :], wr[:, :, s, :], tmp, ALU.add)
                tt(tmp, c_re, over_c(1), ALU.mult)
                tt(wi[:, :, s, :], c_ni, over_c(0), ALU.mult)
                ins = dve.tensor_tensor(wi[:, :, s, :], wi[:, :, s, :], tmp, ALU.subtract)
                if s < L - 1:
                    link(ins)
                else:
                    ins.then_inc(wo_ready, 1)

            def lo_of(slot, m):
                dve.wait_ge(hi_ready, 2 * m + slot + 1)
                dve.tensor_tensor(w_lo[:, slot, :], raw[:, slot, :], w_hi[:, slot, :].bitcast(F32), ALU.subtract)\
                    .then_inc(lo_ready, 1)

            def norm(n, gain, chunked=False):
                for half in range(2):
                    mine = slice(half * HALF, (half + 1) * HALF)
                    if n == 0 and half == 1:
                        lo_of(0, 0)
                    dve.wait_ge(rs_ready, 2 * n + half + 1)
                    dve.reciprocal(rinv[:, mine], rs[:, mine]).then_inc(rinv_ready, 1)
                    dve.wait_ge(rinv_ready, 2 * n + half + 1)
                    for k in range(KT):
                        m = KT * half + k
                        if m >= 4:
                            dve.wait_ge(alo_ready, NORM * n + m - 3)
                        dve.scalar_tensor_tensor(
                            out=as_tokens(hf[:, m % 4, :], chunked), in0=tokens(xT[:, k, :], half, chunked),
                            scalar=gains[:, gain, k:k + 1], in1=as_tokens(rinv[:, mine], chunked),
                            op0=ALU.mult, op1=ALU.mult).then_inc(hf_ready, 1)

            dve.wait_ge(wo_ready, 1)
            dve.wait_ge(cs_ready, 1)
            dve.wait_ge(zero_out, 16)
            dve.wait_ge(small_in, 16 * 9)
            norm(0, 0)
            ts(qk_gain[:, 0:4], qk_g[:, 0:1].to_broadcast((P, 4)), -HD ** -0.5, None, ALU.mult)
            link(dve.tensor_copy(qk_gain[:, 4:8], qk_g[:, 1:2].to_broadcast((P, 4))))

            dve.wait_ge(k_copied, 2)
            dve.wait_ge(dm_ready, 1)
            dve.tensor_tensor(kall[96:P, :, :, :].rearrange("p g a c -> p (g a c)"),
                              kall[96:P, :, :, :].rearrange("p g a c -> p (g a c)"),
                              dm[96:P, :, :].rearrange("p g c -> p (g c)"), ALU.add).then_inc(k_ready, 1)

            dve.wait_ge(alo_ready, NORM)
            dve.sem_inc(qk_free, 4)
            dve.wait_ge(k_done, 1)
            dve.memset(wf_hi[:, :, NH:P].bitcast(F32), 0.0).then_inc(f_zero, 1)
            dve.memset(wf_lo[:, :, NH:P].bitcast(F32), 0.0).then_inc(f_zero, 1)
            dve.memset(fone[:, :], 1.0).then_inc(f_zero, 1)
            dve.wait_ge(f_hi, 1)
            dve.tensor_tensor(wf_lo[:, :, 0:NH], wf[:, :, :], wf_hi[:, :, 0:NH].bitcast(F32), ALU.subtract)\
                .then_inc(f_lo, 1)
            def qk_panels(i):
                for slot in range(2):
                    lo_of(1 - slot, i + slot)
                    for g in range(4):
                        n = 4 * slot + g
                        dve.wait_ge(qk_root, 8 * i + n + 1)
                        dve.reciprocal(rih[:, g % 2, :], rsh[:, g, :]).then_inc(qk_inv, 1)
                        dve.wait_ge(qk_inv, 8 * i + n + 1)
                        if not (isinstance(i, int) and 4 * i + n // 2 == 0):
                            dve.wait_ge(stg_out[g % 2], i * 64 + 16 * (n // 2))
                        dve.scalar_tensor_tensor(out=stg[:, g % 2, :], in0=ps[:, g, :],
                                                 scalar=qk_gain[:, bass.ds(2 * i + slot, 1)], in1=rih[:, g % 2, :],
                                                 op0=ALU.mult, op1=ALU.mult).then_inc(qk_free, 1)
            qk_panels(0)
            with dve.Fori(1, N_QK // 2) as i:
                qk_panels(i)
            dve.wait_ge(f_act, 4)
            dve.tensor_scalar(fy[:, :], fy[:, :], 0.0, None, ALU.min).then_inc(f_min, 1)
            dve.wait_ge(f_min, 1)
            dve.tensor_tensor(fy[:, :], fy[:, :], fe[:, :], ALU.subtract).then_inc(f_min, 1)
            dve.wait_ge(f_min, 2)
            dve.wait_ge(f_zero, 3)
            dve.tensor_tensor_scan(fc[:, :], fone[:, :], fy[:, :], 0.0, ALU.mult, ALU.add).then_inc(f_min, 2)

            dve.sem_inc(v_copied_d, 2)
            for i in range(N_V // 2):
                for slot in range(2):
                    if i + slot < N_V // 2:
                        lo_of(1 - slot, N_QK // 2 + i + slot)
                    for t in range(1, KT, 2):
                        dve.wait_ge(v_done, 16 * i + 8 * slot + t + 1)
                        if i + slot + t > 1:
                            dve.wait_ge(vst_out[1], 16 * (8 * i + 4 * slot + t // 2))
                        dve.tensor_copy(vst[:, 1, :], ps[:, t % 4, 0:PW]).then_inc(v_copied_d, 1)
            dve.sem_inc(s_biased, 2)
            dve.wait_ge(v_done, KT * N_V)
            for h in range(2):
                pad = slice((1 - h) * HD, (2 - h) * HD)
                dve.memset(v_hi[:, h, :, pad].bitcast(F32), 0.0).then_inc(v_pad, 1)
                dve.memset(v_lo[:, h, :, pad].bitcast(F32), 0.0).then_inc(v_pad, 1)
            dve.sem_inc(ptl_ready, T_SLOTS)
            dve.sem_inc(olo_ready, 1)

            def attend(order, pair, parity):
                for kind, u, n in order:
                    if kind == "QK":
                        nxt = 0 if pair is START else 1
                        for k, (d_, r_, h_) in enumerate(((q_lo, q_raw, q_hi), (k_lo, k_raw, k_hi))):
                            dve.wait_ge(qk_hi, pair(2, 2 * nxt + k + 1))
                            dve.tensor_tensor(d_, r_, h_.bitcast(F32), ALU.subtract).then_inc(qk_lo, 1)
                    elif kind in ("V0", "V1"):
                        h = 0 if kind == "V0" else 1
                        nxt = 1 if h == 0 and pair is not START else 0
                        mine = slice(h * HD, (h + 1) * HD)
                        dve.wait_ge(v_hi_ready, pair(2, 2 * nxt + h + 1))
                        dve.tensor_tensor(v_lo[:, h, :, mine], v_raw[:, :, mine],
                                          v_hi[:, h, :, mine].bitcast(F32), ALU.subtract).then_inc(v_lo_ready, 1)
                    elif kind == "S":
                        b = 4 * u + n
                        keys = keys_of(u, n)
                        dve.wait_ge(s_done, pair(16, b + 1))
                        dve.wait_ge(c_in[u % 2], pair(16, 16 + 16 * (u // 4)))
                        turned = {2: 0, 3: 8, 4: 16, 5: 16}.get(u)
                        if pair is not START and not (pair is FIRST and turned == 0):
                            dve.wait_ge(t_done, pair(24, turned))
                        dve.memset(tick[:, b % 8:b % 8 + 1], 0.0)
                        dve.tensor_tensor_reduce(
                            prob_of(u, parity)[:, n, 0:keys], ps[:, 2 * (b % 2):2 * (b % 2) + 2, :]
                            .rearrange("p b k -> p (b k)")[:, 0:keys], cb[:, u % 2, 0:keys], 1.0, 3e38,
                            ALU.add, ALU.min, mx[:, b % 16:b % 16 + 1]).then_inc(s_biased, 1)
                    elif kind == "R":
                        dve.wait_ge(p_ready, pair(16, 4 * u + 4))
                        mine = slice(4 * (u % 4), 4 * (u % 4) + 4)
                        dve.reciprocal(inv_sums[:, mine], sums[:, mine]).then_inc(inv_ready, 1)
                    elif kind == "T":
                        t = TILES_BEFORE[u] + n
                        lo = first_col(u, n)
                        dve.wait_ge(pth_ready, pair(24, t + 1))
                        dve.tensor_tensor(pt_lo[:, t % T_SLOTS, lo:HALF], ps[:, T_BANKS[t % T_SLOTS], lo:HALF],
                                          pt_hi[:, t % T_SLOTS, lo:HALF].bitcast(F32), ALU.subtract)\
                            .then_inc(ptl_ready, 1)
                    elif kind == "O":
                        dve.wait_ge(ohi_ready, pair(2, u + 1))
                        dve.tensor_tensor(output_of(act_lo, u, pair), ps[:, V_BANK, :],
                                          output_of(act_hi, u, pair).bitcast(F32), ALU.subtract)\
                            .then_inc(olo_ready, 1)

            attend(attention_start(), START, 0)
            attend(attention_order(first=True), FIRST, 0)
            with dve.Fori(0, PAIRS // 2 - 1) as i:
                for parity in (1, 0):
                    attend(attention_order(), inner(i, parity), parity)
            attend(attention_order(last=True), LAST, 1)

            lo_of(0, OUT0 // 2)

            def added(done_, free, tile, g, bank, tok, n):
                dve.wait_ge(done_, n + (1 + 1))
                dve.wait_ge(free, n + 1)
                dst = xT[:, bass.ds(tile, 1), tok].squeeze(1) if not isinstance(tile, int) else xT[:, tile, tok]
                dve.tensor_tensor(dst, ps[:, bank, :], dst, ALU.add).then_inc(free, 1)

            dve.sem_inc(oproj_free, 4)
            with dve.Fori(0, N_OUT // 2) as i:
                for slot in range(2):
                    lo_of(1 - slot, i + (OUT0 // 2 + slot))
                    for g in range(4):
                        half = g % 2
                        added(oproj_done, oproj_free, 4 * i + (2 * slot + g // 2), g, g,
                              slice(half * HALF, (half + 1) * HALF), 8 * i + (4 * slot + g))
            dve.wait_ge(oproj_free, 4 + 4 * N_OUT)
            norm(1, 2)

            def mlp(layer, panel0, last):
                dve.sem_inc(down_free[layer], 4)

                def step(i, more):
                    lo_of(1, i + panel0 // 2)
                    for q in range(2 * KT):
                        half = q // KT
                        added(down_done[layer], down_free[layer], q % KT, q, 4 + q % 4,
                              slice(half * HALF, (half + 1) * HALF), 16 * i + q)
                        if q == 3 and more:
                            lo_of(0, i + (panel0 // 2 + 1))
                if last:
                    with dve.Fori(0, N_MLP // 2 - 1) as i:
                        step(i, True)
                    step(N_MLP // 2 - 1, False)
                else:
                    with dve.Fori(0, N_MLP // 2) as i:
                        step(i, True)
                dve.wait_ge(down_free[layer], 4 + 16 * N_MLP // 2)

            mlp(0, MLP0, last=False)
            norm(2, 1, chunked=True)
            with dve.Fori(0, N_SIN // 2) as i:
                for slot in range(2):
                    lo_of(1 - slot, i + (SIN0 // 2 + slot))

            dve.wait_ge(u_out, 16 * GB * KT)
            dve.sem_inc(state_ready, 4)
            STEPS = 12

            def states(n, q, s):
                made = [0]

                def step(ins):
                    made[0] += 1
                    ins.then_inc(scan_chain, 1)
                    dve.wait_ge(scan_chain, STEPS * q + made[0])

                c_, s_ = cs[:, s, 0, :], cs[:, s, 1, :]
                v_re, v_im = ps[:, 2 * s, :], ps[:, 2 * s + 1, :]
                w_re, w_im, tmp = (vb[:, n, :] for n in range(3))
                x_re, x_im = xb[:, 0, :], xb[:, 1, :]
                d_ = decay[:, :, :].rearrange("p g j -> p (g j)")
                dve.wait_ge(drive_done, q + 1)
                dve.wait_ge(phase_in[s], 16 * n + 16)
                step(dve.tensor_tensor(w_re, v_re, c_, ALU.mult))
                step(dve.tensor_tensor(tmp, v_im, s_, ALU.mult))
                step(dve.tensor_tensor(w_re, w_re, tmp, ALU.add))
                step(dve.tensor_tensor(w_im, v_im, c_, ALU.mult))
                step(dve.tensor_tensor(tmp, v_re, s_, ALU.mult))
                step(dve.tensor_tensor(w_im, w_im, tmp, ALU.subtract))
                dve.wait_ge(decay_ready, q + 1)
                step(dve.tensor_tensor_scan(w_re, d_, w_re, 0.0, ALU.mult, ALU.add))
                step(dve.tensor_tensor_scan(w_im, d_, w_im, 0.0, ALU.mult, ALU.add))
                dve.wait_ge(y_done, 2 * q + 2)
                step(dve.tensor_tensor(x_re, w_re, c_, ALU.mult))
                step(dve.tensor_tensor(tmp, w_im, s_, ALU.mult))
                dve.tensor_tensor(x_re, x_re, tmp, ALU.subtract).then_inc(state_ready, 1)
                dve.wait_ge(state_ready, 2 * q + (1 + 4))
                step(dve.tensor_tensor(x_im, w_re, s_, ALU.mult))
                step(dve.tensor_tensor(tmp, w_im, c_, ALU.mult))
                dve.tensor_tensor(x_im, x_im, tmp, ALU.add).then_inc(state_ready, 1)
                dve.wait_ge(state_ready, 2 * q + (2 + 4))

            with dve.Fori(0, BLK // 2) as i:
                for s in (0, 1):
                    states(i, 2 * i + s, s)

            dve.sem_inc(glu_free, 4)
            dve.sem_inc(glu_added, 1)
            with dve.Fori(0, N_GLU // 2) as i:
                for slot in range(2):
                    lo_of(1 - slot, i + (GLU0 // 2 + slot))
                for g in range(4):
                    m, half = g // 2, g % 2
                    n = 4 * i + g
                    dve.wait_ge(sig_ready, n + 1)
                    dve.wait_ge(glu_added, n + 1)
                    dve.tensor_tensor(gated[:, half, :], ps[:, g, :], sig[:, g, :], ALU.mult).then_inc(glu_free, 1)
                    dve.wait_ge(glu_free, n + 1 + 4)
                    dst = xT[:, bass.ds(2 * i + m, 1), :].squeeze(1).rearrange("p (j s) -> p s j", s=L)\
                        [:, half * L // 2:(half + 1) * L // 2, :]
                    dve.tensor_tensor(dst, gated[:, half, :].rearrange("p (s j) -> p s j", j=NC), dst, ALU.add)\
                        .then_inc(glu_added, 1)
            dve.wait_ge(glu_added, 2 * N_GLU + 1)
            norm(3, 3)
            mlp(1, MLP1, last=True)


INS = ["x", "norm_mix_g", "norm_mlp_g", "attn_w_in", "attn_b_f", "attn_q_g", "attn_k_g", "attn_w_out", "ssm_w_in",
       "ssm_a_re", "ssm_a_im", "ssm_b_re", "ssm_b_im", "ssm_c_re", "ssm_c_im", "ssm_log_dt", "ssm_d", "ssm_w_glu",
       "mlp_w1", "mlp_w2"]


def kernel(**inputs):
    import numpy as np
    import concourse.bacc as bacc
    from concourse.bass_utils import run_bass_kernel_spmd

    nc = bacc.Bacc("TRN2", target_bir_lowering=False, num_devices=1)
    arrays, args = {}, []
    for name in INS:
        a = np.ascontiguousarray(inputs[name])
        arrays[f"in_{name}"] = a
        args.append(nc.dram_tensor(f"in_{name}", a.shape, mybir.dt.from_np(a.dtype), kind="ExternalInput").ap())
    args.append(nc.dram_tensor("out_0", (1, T, D), F32, kind="ExternalOutput").ap())
    build(nc, *args)
    r = run_bass_kernel_spmd(nc, [arrays], core_ids=[0])
    return r.results[0]["out_0"]
```
